# Optimizing a Trainium2 kernel written in Bass

```python
import math
import jax, jax.numpy as jnp
from jax import lax
import numpy as np
import jax
import jax.numpy as jnp

D_MODEL = 1024
BATCH = 1
SEQ = 512
DEPTH = 2

CTX_LEN = 256
GRID_W = 64
N_MIXERS = 2
N_HEADS = 8
HEAD_DIM = 64
V_DIM = 2 * HEAD_DIM
QK_WIDTH = N_HEADS * 2 * HEAD_DIM
V_WIDTH = N_HEADS * V_DIM
ROPE_THETA = 10000.0
ROPE_PAIRS = HEAD_DIM // 4
N_FOURIER_GROUPS = 4
FOURIER_GROUP = D_MODEL // N_FOURIER_GROUPS
D_FF = 2816
N_MOD = 9
Q_BLOCK = 128
EPS = 1e-6
N_ATTN_LAYERS = (DEPTH + N_MIXERS - 1) // N_MIXERS
N_FOURIER_LAYERS = DEPTH // N_MIXERS


def rms_norm(x, g):
    x32 = x.astype(jnp.float32)
    y = x32 * lax.rsqrt(jnp.mean(x32 * x32, axis=-1, keepdims=True) + EPS)
    return (y * g.astype(jnp.float32)).astype(x.dtype)

def modulate(h, shift, scale):
    return h * (1 + scale) + shift

def swiglu(h, w_gu, w_d):
    g, u = jnp.split(h @ w_gu, 2, axis=-1)
    return (jax.nn.silu(g) * u) @ w_d

def ada_params(cond, w_mod, b_mod):
    m = jax.nn.silu(cond) @ w_mod + b_mod
    m = m.reshape(m.shape[:-1] + (N_MOD, 1, D_MODEL))
    return [m[..., k, :, :] for k in range(N_MOD)]

def axial_rope_tables(n_tokens):
    rows = n_tokens // GRID_W
    row = jnp.repeat(jnp.arange(rows, dtype=jnp.float32), GRID_W)
    col = jnp.tile(jnp.arange(GRID_W, dtype=jnp.float32), rows)
    inv_freq = ROPE_THETA ** (-(jnp.arange(ROPE_PAIRS, dtype=jnp.float32) / ROPE_PAIRS))
    ang = jnp.concatenate([row[:, None] * inv_freq, col[:, None] * inv_freq], axis=-1)
    ang = ang.reshape(n_tokens, 2, ROPE_PAIRS)
    return jnp.cos(ang), jnp.sin(ang)

def apply_axial_rope(t, cos, sin):
    shp = t.shape
    t = t.reshape(shp[:-1] + (2, 2, ROPE_PAIRS))
    t1, t2 = t[..., 0, :], t[..., 1, :]
    cs = cos.astype(t.dtype)[:, None, None]
    sn = sin.astype(t.dtype)[:, None, None]
    out = jnp.stack([t1 * cs - t2 * sn, t2 * cs + t1 * sn], axis=-2)
    return out.reshape(shp)

def diff_attn_core(q, k, v, lam):
    s = jnp.einsum('bqhcd,bkhcd->bhcqk', q.astype(jnp.float32), k.astype(jnp.float32))
    p = jax.nn.softmax(s * (1.0 / math.sqrt(HEAD_DIM)), axis=-1)
    a = p[:, :, 0] - lam * p[:, :, 1]
    return jnp.einsum('bhqk,bkhe->bqhe', a.astype(v.dtype), v)

def split_qkv(h, w_qkv):
    b, n, _ = h.shape
    qkv = h @ w_qkv
    q = qkv[..., :QK_WIDTH].reshape(b, n, N_HEADS, 2, HEAD_DIM)
    k = qkv[..., QK_WIDTH:2 * QK_WIDTH].reshape(b, n, N_HEADS, 2, HEAD_DIM)
    v = qkv[..., 2 * QK_WIDTH:].reshape(b, n, N_HEADS, V_DIM)
    return q, k, v

def diff_head_out(o, sub_g, w_o, lambda_init):
    b, n = o.shape[:2]
    o = rms_norm(o, sub_g) * (1.0 - lambda_init)
    return o.reshape(b, n, V_WIDTH) @ w_o

def diff_attention(hx, hy, w_qkv, w_o, q_g, k_g, lq1, lk1, lq2, lk2, sub_g,
                   lambda_init, cos, sin, with_ctx_queries):
    b, n, _ = hx.shape
    lam = (jnp.exp(jnp.sum(lq1.astype(jnp.float32) * lk1.astype(jnp.float32)))
           - jnp.exp(jnp.sum(lq2.astype(jnp.float32) * lk2.astype(jnp.float32)))
           + lambda_init)
    q, k, v = split_qkv(hx, w_qkv)
    q = apply_axial_rope(rms_norm(q, q_g), cos, sin)
    k = apply_axial_rope(rms_norm(k, k_g), cos, sin)
    qy, ky, vy = split_qkv(hy, w_qkv)
    ky = rms_norm(ky, k_g)
    keys = jnp.concatenate([ky, k], axis=1)
    vals = jnp.concatenate([vy, v], axis=1)
    nb = n // Q_BLOCK
    qb = q.reshape(b, nb, Q_BLOCK, N_HEADS, 2, HEAD_DIM).swapaxes(0, 1)
    ob = lax.map(lambda qq: diff_attn_core(qq, keys, vals, lam), qb)
    o = ob.swapaxes(0, 1).reshape(b, n, N_HEADS, V_DIM)
    out_x = diff_head_out(o, sub_g, w_o, lambda_init)
    out_y = None
    if with_ctx_queries:
        qy = rms_norm(qy, q_g)
        oy = diff_attn_core(qy, ky, vy, lam)
        out_y = diff_head_out(oy, sub_g, w_o, lambda_init)
    return out_x, out_y

def fourier_mix(h, w_f):
    b, n, d = h.shape
    hg = h.astype(jnp.float32).reshape(b, n, N_FOURIER_GROUPS, FOURIER_GROUP)
    f = jnp.fft.fft2(hg, axes=(1, 3), norm="ortho").real
    return f.reshape(b, n, d).astype(h.dtype) @ w_f

def first_inputs(seed: int = 0) -> dict:
    key = jax.random.key(seed)
    ks = jax.random.split(key, 24)
    nrm = jax.random.normal
    f32 = jnp.float32
    NA, NF = N_ATTN_LAYERS, N_FOURIER_LAYERS
    return {
        "x": nrm(ks[0], (BATCH, SEQ, D_MODEL), f32),
        "c": nrm(ks[1], (BATCH, D_MODEL), f32),
        "ctx": nrm(ks[2], (BATCH, CTX_LEN, D_MODEL), f32),
        "c_ctx": nrm(ks[3], (D_MODEL,), f32),
        "norm_g": 1.0 + 0.05 * nrm(ks[4], (DEPTH, 3, D_MODEL), f32),
        "w_mod": 0.5 * nrm(ks[5], (DEPTH, D_MODEL, N_MOD * D_MODEL), f32) * D_MODEL ** -0.5,
        "b_mod": 0.01 * nrm(ks[6], (DEPTH, N_MOD * D_MODEL), f32),
        "ffn1_w_gu": nrm(ks[7], (DEPTH, D_MODEL, 2 * D_FF), f32) * D_MODEL ** -0.5,
        "ffn1_w_d": nrm(ks[8], (DEPTH, D_FF, D_MODEL), f32) * D_FF ** -0.5,
        "ffn2_w_gu": nrm(ks[9], (DEPTH, D_MODEL, 2 * D_FF), f32) * D_MODEL ** -0.5,
        "ffn2_w_d": nrm(ks[10], (DEPTH, D_FF, D_MODEL), f32) * D_FF ** -0.5,
        "attn_w_qkv": nrm(ks[11], (NA, D_MODEL, 2 * QK_WIDTH + V_WIDTH), f32) * D_MODEL ** -0.5,
        "attn_w_o": nrm(ks[12], (NA, V_WIDTH, D_MODEL), f32) * V_WIDTH ** -0.5,
        "attn_q_g": 1.0 + 0.05 * nrm(ks[13], (NA, HEAD_DIM), f32),
        "attn_k_g": 1.0 + 0.05 * nrm(ks[14], (NA, HEAD_DIM), f32),
        "attn_lam_q1": 0.1 * nrm(ks[15], (NA, HEAD_DIM), f32),
        "attn_lam_k1": 0.1 * nrm(ks[16], (NA, HEAD_DIM), f32),
        "attn_lam_q2": 0.1 * nrm(ks[17], (NA, HEAD_DIM), f32),
        "attn_lam_k2": 0.1 * nrm(ks[18], (NA, HEAD_DIM), f32),
        "attn_sub_g": 1.0 + 0.05 * nrm(ks[19], (NA, V_DIM), f32),
        "fourier_w": nrm(ks[20], (NF, D_MODEL, D_MODEL), f32) * D_MODEL ** -0.5,
    }

def first_block(x, c, ctx, c_ctx, norm_g, w_mod, b_mod, ffn1_w_gu, ffn1_w_d, ffn2_w_gu,
              ffn2_w_d, attn_w_qkv, attn_w_o, attn_q_g, attn_k_g, attn_lam_q1, attn_lam_k1,
              attn_lam_q2, attn_lam_k2, attn_sub_g, fourier_w):
    n_lat = x.shape[1]
    cos, sin = axial_rope_tables(n_lat)
    y = ctx
    for i in range(DEPTH):
        kind = i % N_MIXERS
        ctx_needed_after = any(j % N_MIXERS == 0 for j in range(i + 1, DEPTH))
        ctx_in_layer = ctx_needed_after or kind == 0
        mx = ada_params(c, w_mod[i], b_mod[i])
        x = x + 0.5 * mx[2] * swiglu(modulate(rms_norm(x, norm_g[i, 0]), mx[0], mx[1]),
                                     ffn1_w_gu[i], ffn1_w_d[i])
        if ctx_in_layer:
            my = ada_params(c_ctx, w_mod[i], b_mod[i])
            y = y + 0.5 * my[2] * swiglu(modulate(rms_norm(y, norm_g[i, 0]), my[0], my[1]),
                                         ffn1_w_gu[i], ffn1_w_d[i])
        hx = modulate(rms_norm(x, norm_g[i, 1]), mx[3], mx[4])
        if kind == 0:
            a = i // N_MIXERS
            hy = modulate(rms_norm(y, norm_g[i, 1]), my[3], my[4])
            lambda_init = 0.8 - 0.6 * math.exp(-0.3 * i)
            ox, oy = diff_attention(hx, hy, attn_w_qkv[a], attn_w_o[a], attn_q_g[a],
                                    attn_k_g[a], attn_lam_q1[a], attn_lam_k1[a],
                                    attn_lam_q2[a], attn_lam_k2[a], attn_sub_g[a],
                                    lambda_init, cos, sin, ctx_needed_after)
            x = x + mx[5] * ox
            if ctx_needed_after:
                y = y + my[5] * oy
        else:
            f = i // N_MIXERS
            x = x + mx[5] * fourier_mix(hx, fourier_w[f])
            if ctx_needed_after:
                hy = modulate(rms_norm(y, norm_g[i, 1]), my[3], my[4])
                y = y + my[5] * fourier_mix(hy, fourier_w[f])
        x = x + 0.5 * mx[8] * swiglu(modulate(rms_norm(x, norm_g[i, 2]), mx[6], mx[7]),
                                     ffn2_w_gu[i], ffn2_w_d[i])
        if ctx_needed_after:
            y = y + 0.5 * my[8] * swiglu(modulate(rms_norm(y, norm_g[i, 2]), my[6], my[7]),
                                         ffn2_w_gu[i], ffn2_w_d[i])
    return x


DEPTH_2 = 1

NSA_HEADS = 8
NSA_KV_HEADS = 2
NSA_GROUP = NSA_HEADS // NSA_KV_HEADS
SWA_HEADS = 8
SWA_KV_HEADS = 2
SWA_GROUP = SWA_HEADS // SWA_KV_HEADS
NSA_WIDTH = NSA_HEADS * HEAD_DIM
SWA_WIDTH = SWA_HEADS * HEAD_DIM
NSA_KV_WIDTH = NSA_KV_HEADS * HEAD_DIM
SWA_KV_WIDTH = SWA_KV_HEADS * HEAD_DIM
CMP_LEN = 32
CMP_STRIDE = 16
CMP_HIDDEN = 256
SLC_LEN = 64
SLC_TOPK = 8
NSA_WINDOW = 256
SLC_QUERY_CHUNK = 64
SWA_WINDOW = 128
BAND_BLOCK = 128
N_GROUPS = 4
EXPERTS_PER_GROUP = 8
N_EXPERTS = N_GROUPS * EXPERTS_PER_GROUP
EXPERT_TOPK = 2
EXPERT_FF = 256
MOE_BLOCK = 128
IN_SIZES = (NSA_WIDTH, NSA_KV_WIDTH, NSA_KV_WIDTH, NSA_KV_WIDTH, NSA_KV_WIDTH, NSA_KV_WIDTH, NSA_KV_WIDTH,
            3 * NSA_HEADS, SWA_WIDTH, SWA_KV_WIDTH, SWA_KV_WIDTH, 2 * D_MODEL)
IN_WIDTH = sum(IN_SIZES)
RMS_EPS = 1e-6
NEG_INF = -1e30
FORCE_SCORE = 1e9


def rms_norm_2(x, g):
    x32 = x.astype(jnp.float32)
    y = x32 * lax.rsqrt(jnp.mean(x32 * x32, axis=-1, keepdims=True) + RMS_EPS)
    return (y * g.astype(jnp.float32)).astype(x.dtype)

def masked_softmax(s, mask):
    s = jnp.where(mask, s, NEG_INF)
    m = jnp.max(s, axis=-1, keepdims=True)
    e = jnp.where(mask, jnp.exp(s - m), 0.0)
    z = jnp.sum(e, axis=-1, keepdims=True)
    return e / jnp.where(z > 0, z, 1.0)

def alibi_slopes():
    n = NSA_HEADS + SWA_HEADS
    s = 2.0 ** (-8.0 * np.arange(1, n + 1) / n)
    return jnp.asarray(s[:SWA_HEADS], jnp.float32), jnp.asarray(s[SWA_HEADS:], jnp.float32)

def compress_blocks(kv, pos, w1, w2):
    B, S, H, d = kv.shape
    r = CMP_LEN // CMP_STRIDE
    nc = S // CMP_STRIDE - r + 1
    kc = kv.reshape(B, S // CMP_STRIDE, CMP_STRIDE, H, d)
    blocks = jnp.concatenate([kc[:, i:i + nc] for i in range(r)], axis=2)
    blocks = blocks + pos[None, None, :, None, :]
    flat = jnp.transpose(blocks, (0, 1, 3, 2, 4)).reshape(B, nc, H, CMP_LEN * d)
    return jax.nn.silu(flat @ w1) @ w2

def compressed_branch(q, kc, vc, slopes):
    B, S, Hkv, G, d = q.shape
    nc = kc.shape[1]
    s = jnp.einsum('bshgd,bchd->bhgsc', q, kc, preferred_element_type=jnp.float32) * (d ** -0.5)
    end = jnp.arange(nc) * CMP_STRIDE + CMP_LEN - 1
    dist = jnp.arange(S)[:, None] - end[None, :]
    s = s - slopes.reshape(Hkv, G, 1, 1) * dist.astype(jnp.float32)
    p = masked_softmax(s, dist >= 0)
    o = jnp.einsum('bhgsc,bchd->bshgd', p.astype(vc.dtype), vc)
    return o, p

def select_blocks(p_cmp, S):
    nc = p_cmp.shape[-1]
    ns = S // SLC_LEN
    c0 = np.arange(nc) * CMP_STRIDE
    s0 = np.arange(ns) * SLC_LEN
    ov = np.clip(np.minimum(c0[:, None] + CMP_LEN, s0[None, :] + SLC_LEN)
                 - np.maximum(c0[:, None], s0[None, :]), 0, None) / CMP_LEN
    imp = jnp.einsum('bhsc,cj->bhsj', jnp.sum(p_cmp, axis=2), jnp.asarray(ov, jnp.float32))
    t = jnp.arange(S)[:, None]
    j = jnp.arange(ns)[None, :]
    cur = t // SLC_LEN
    valid = j * SLC_LEN <= t
    forced = (j == 0) | (j == cur) | (j == cur - 1)
    score = jnp.where(forced, FORCE_SCORE, jnp.where(valid, imp, NEG_INF))
    vals, idx = lax.top_k(score, min(SLC_TOPK, ns))
    return idx, vals > 0.5 * NEG_INF

def selected_branch(q, k, v, idx, valid, slopes):
    B, S, Hkv, G, d = q.shape
    ns = S // SLC_LEN
    n = idx.shape[-1]
    QC = SLC_QUERY_CHUNK
    nq = S // QC
    kb = jnp.transpose(k.reshape(B, ns, SLC_LEN, Hkv, d), (0, 3, 1, 2, 4))
    vb = jnp.transpose(v.reshape(B, ns, SLC_LEN, Hkv, d), (0, 3, 1, 2, 4))
    qc = jnp.swapaxes(q.reshape(B, nq, QC, Hkv, G, d), 0, 1)
    ic = jnp.transpose(idx.reshape(B, Hkv, nq, QC, n), (2, 0, 1, 3, 4))
    vc = jnp.transpose(valid.reshape(B, Hkv, nq, QC, n), (2, 0, 1, 3, 4))
    tc = jnp.arange(S).reshape(nq, QC)
    bi = jnp.arange(B)[:, None, None, None]
    hi = jnp.arange(Hkv)[None, :, None, None]
    sl = slopes.reshape(1, Hkv, G, 1, 1, 1)
    scale = d ** -0.5

    def chunk(args):
        qq, ii, vv, tt = args
        kg = kb[bi, hi, ii]
        vg = vb[bi, hi, ii]
        s = jnp.einsum('bqhgd,bhqnld->bhgqnl', qq, kg, preferred_element_type=jnp.float32) * scale
        kpos = ii[..., None] * SLC_LEN + jnp.arange(SLC_LEN)
        dist = tt[None, None, :, None, None] - kpos
        mask = (vv[..., None] & (dist >= 0))[:, :, None]
        s = s - sl * dist[:, :, None].astype(jnp.float32)
        p = masked_softmax(s.reshape(B, Hkv, G, QC, n * SLC_LEN), mask.reshape(B, Hkv, 1, QC, n * SLC_LEN))
        return jnp.einsum('bhgqk,bhqkd->bqhgd', p.astype(vg.dtype), vg.reshape(B, Hkv, QC, n * SLC_LEN, d))

    out = lax.map(chunk, (qc, ic, vc, tc))
    return jnp.swapaxes(out, 0, 1).reshape(B, S, Hkv, G, d)

def banded_attention(q, k, v, slopes, window, sinks):
    B, S, Hkv, G, d = q.shape
    nb = S // BAND_BLOCK
    nprev = -(-(window - 1) // BAND_BLOCK)
    pad = nprev * BAND_BLOCK
    kw = (nprev + 1) * BAND_BLOCK

    def band(a):
        ap = jnp.pad(a, ((0, 0), (pad, 0), (0, 0), (0, 0))).reshape(B, nb + nprev, BAND_BLOCK, Hkv, d)
        return jnp.concatenate([ap[:, j:j + nb] for j in range(nprev + 1)], axis=2)

    kb, vb = band(k), band(v)
    qb = q.reshape(B, nb, BAND_BLOCK, Hkv, G, d)
    s = jnp.einsum('bnqhgd,bnkhd->bnhgqk', qb, kb, preferred_element_type=jnp.float32) * (d ** -0.5)
    blk = jnp.arange(nb)[:, None] * BAND_BLOCK
    tpos = blk + jnp.arange(BAND_BLOCK)
    kpos = blk - pad + jnp.arange(kw)
    dist = tpos[:, :, None] - kpos[:, None, :]
    mask = ((dist >= 0) & (dist < window) & (kpos[:, None, :] >= 0))[None, :, None, None]
    s = s - slopes.reshape(1, 1, Hkv, G, 1, 1) * dist.astype(jnp.float32)[None, :, None, None]
    s = jnp.where(mask, s, NEG_INF)
    m = jnp.max(s, axis=-1, keepdims=True)
    if sinks is not None:
        sk = sinks.astype(jnp.float32).reshape(1, 1, Hkv, G, 1, 1)
        m = jnp.maximum(m, sk)
    e = jnp.where(mask, jnp.exp(s - m), 0.0)
    z = jnp.sum(e, axis=-1, keepdims=True)
    if sinks is not None:
        z = z + jnp.exp(sk - m)
    p = e / z
    o = jnp.einsum('bnhgqk,bnkhd->bnqhgd', p.astype(v.dtype), vb)
    return o.reshape(B, S, Hkv, G, d)

def hier_moe(h, w_group, b_group, w_expert, b_expert, w_gate_e, w_up_e, w_down_e):
    B, S, D = h.shape
    N = B * S
    hf = h.reshape(N, D)
    g_logits = (hf @ w_group).astype(jnp.float32) + b_group.astype(jnp.float32)
    g_prob = jax.nn.softmax(g_logits, axis=-1)
    grp = jnp.argmax(g_logits, axis=-1)
    p_grp = jnp.take_along_axis(g_prob, grp[:, None], axis=-1)[:, 0]
    e_logits = ((hf @ w_expert).astype(jnp.float32) + b_expert.astype(jnp.float32)).reshape(N, N_GROUPS, EXPERTS_PER_GROUP)
    e_in = jnp.take_along_axis(e_logits, grp[:, None, None], axis=1)[:, 0]
    top_v, top_i = lax.top_k(e_in, EXPERT_TOPK)
    weight = p_grp[:, None] * jax.nn.softmax(top_v, axis=-1)
    eid = (grp[:, None] * EXPERTS_PER_GROUP + top_i).reshape(-1)
    w_f = weight.reshape(-1)
    NK = N * EXPERT_TOPK
    tok = jnp.arange(NK) // EXPERT_TOPK
    order = jnp.argsort(eid)
    e_sorted = eid[order]
    counts = jnp.bincount(eid, length=N_EXPERTS)
    padded = (counts + MOE_BLOCK - 1) // MOE_BLOCK * MOE_BLOCK
    pad_end = jnp.cumsum(padded)
    pad_start = pad_end - padded
    cnt_start = jnp.cumsum(counts) - counts
    dest = pad_start[e_sorted] + jnp.arange(NK) - cnt_start[e_sorted]
    n_blocks = -(-(NK + N_EXPERTS * (MOE_BLOCK - 1)) // MOE_BLOCK)
    buf = jnp.zeros((n_blocks * MOE_BLOCK, D), h.dtype).at[dest].set(hf[tok[order]])
    block_e = jnp.minimum(jnp.searchsorted(pad_end, jnp.arange(n_blocks) * MOE_BLOCK, side='right'), N_EXPERTS - 1)

    def expert_block(args):
        xb, e = args
        return (jax.nn.silu(xb @ w_gate_e[e]) * (xb @ w_up_e[e])) @ w_down_e[e]

    yb = lax.map(expert_block, (buf.reshape(n_blocks, MOE_BLOCK, D), block_e)).reshape(-1, D)
    y_slot = yb[dest] * w_f[order][:, None].astype(yb.dtype)
    y = jnp.zeros((N, D), h.dtype).at[tok[order]].add(y_slot)
    return y.reshape(B, S, D)

def second_inputs(seed: int = 0) -> dict:
    key = jax.random.key(seed)
    ks = jax.random.split(key, 24)
    f32 = jnp.float32
    L = DEPTH_2
    d = HEAD_DIM

    def nrm(k, shape, scale):
        return jax.random.normal(k, shape, f32) * scale

    return {
        "x": nrm(ks[0], (BATCH, SEQ, D_MODEL), 1.0),
        "norm_mix_g": 1.0 + nrm(ks[1], (L, D_MODEL), 0.02),
        "w_in": nrm(ks[2], (L, D_MODEL, IN_WIDTH), D_MODEL ** -0.5),
        "cmp_pos_k": nrm(ks[3], (L, CMP_LEN, d), 0.1),
        "cmp_w1_k": nrm(ks[4], (L, CMP_LEN * d, CMP_HIDDEN), (CMP_LEN * d) ** -0.5),
        "cmp_w2_k": nrm(ks[5], (L, CMP_HIDDEN, d), CMP_HIDDEN ** -0.5),
        "cmp_pos_v": nrm(ks[6], (L, CMP_LEN, d), 0.1),
        "cmp_w1_v": nrm(ks[7], (L, CMP_LEN * d, CMP_HIDDEN), (CMP_LEN * d) ** -0.5),
        "cmp_w2_v": nrm(ks[8], (L, CMP_HIDDEN, d), CMP_HIDDEN ** -0.5),
        "sinks": nrm(ks[9], (L, SWA_HEADS), 0.5),
        "w_a": nrm(ks[10], (L, NSA_WIDTH, D_MODEL), NSA_WIDTH ** -0.5),
        "w_b": nrm(ks[11], (L, SWA_WIDTH, D_MODEL), SWA_WIDTH ** -0.5),
        "w_o": nrm(ks[12], (L, D_MODEL, D_MODEL), D_MODEL ** -0.5),
        "norm_ffn_g": 1.0 + nrm(ks[13], (L, D_MODEL), 0.02),
        "w_group": nrm(ks[14], (L, D_MODEL, N_GROUPS), D_MODEL ** -0.5),
        "b_group": nrm(ks[15], (L, N_GROUPS), 0.01),
        "w_expert": nrm(ks[16], (L, D_MODEL, N_EXPERTS), D_MODEL ** -0.5),
        "b_expert": nrm(ks[17], (L, N_EXPERTS), 0.01),
        "w_gate_e": nrm(ks[18], (L, N_EXPERTS, D_MODEL, EXPERT_FF), D_MODEL ** -0.5),
        "w_up_e": nrm(ks[19], (L, N_EXPERTS, D_MODEL, EXPERT_FF), D_MODEL ** -0.5),
        "w_down_e": nrm(ks[20], (L, N_EXPERTS, EXPERT_FF, D_MODEL), EXPERT_FF ** -0.5),
        "norm_final_g": 1.0 + nrm(ks[21], (D_MODEL,), 0.02),
    }

def second_block(x, norm_mix_g, w_in, cmp_pos_k, cmp_w1_k, cmp_w2_k, cmp_pos_v, cmp_w1_v, cmp_w2_v,
              sinks, w_a, w_b, w_o, norm_ffn_g, w_group, b_group, w_expert, b_expert,
              w_gate_e, w_up_e, w_down_e, norm_final_g):
    B, S, _ = x.shape
    slopes_swa, slopes_nsa = alibi_slopes()
    split_points = [int(c) for c in np.cumsum(IN_SIZES)[:-1]]
    for l in range(DEPTH_2):
        h = rms_norm_2(x, norm_mix_g[l])
        proj = h @ w_in[l]
        (q_a, k_cmp, v_cmp, k_slc, v_slc, k_win, v_win, g_nsa,
         q_b, k_b, v_b, g_merge) = jnp.split(proj, split_points, axis=-1)
        q_a = q_a.reshape(B, S, NSA_KV_HEADS, NSA_GROUP, HEAD_DIM)
        kv_a = [t.reshape(B, S, NSA_KV_HEADS, HEAD_DIM) for t in (k_cmp, v_cmp, k_slc, v_slc, k_win, v_win)]
        kc = compress_blocks(kv_a[0], cmp_pos_k[l], cmp_w1_k[l], cmp_w2_k[l])
        vc = compress_blocks(kv_a[1], cmp_pos_v[l], cmp_w1_v[l], cmp_w2_v[l])
        o_cmp, p_cmp = compressed_branch(q_a, kc, vc, slopes_nsa)
        idx, valid = select_blocks(p_cmp, S)
        o_slc = selected_branch(q_a, kv_a[2], kv_a[3], idx, valid, slopes_nsa)
        o_win = banded_attention(q_a, kv_a[4], kv_a[5], slopes_nsa, NSA_WINDOW, None)
        g = jax.nn.sigmoid(g_nsa).reshape(B, S, NSA_KV_HEADS, NSA_GROUP, 3)
        o_a = (g[..., 0:1] * o_cmp + g[..., 1:2] * o_slc + g[..., 2:3] * o_win).reshape(B, S, NSA_WIDTH)
        q_b = q_b.reshape(B, S, SWA_KV_HEADS, SWA_GROUP, HEAD_DIM)
        k_b = k_b.reshape(B, S, SWA_KV_HEADS, HEAD_DIM)
        v_b = v_b.reshape(B, S, SWA_KV_HEADS, HEAD_DIM)
        o_b = banded_attention(q_b, k_b, v_b, slopes_swa, SWA_WINDOW, sinks[l]).reshape(B, S, SWA_WIDTH)
        gate_a, gate_b = jnp.split(jax.nn.sigmoid(g_merge), 2, axis=-1)
        mix = (gate_a * (o_a @ w_a[l]) + gate_b * (o_b @ w_b[l])) @ w_o[l]
        x = x + mix
        x = x + hier_moe(rms_norm_2(x, norm_ffn_g[l]), w_group[l], b_group[l], w_expert[l], b_expert[l],
                         w_gate_e[l], w_up_e[l], w_down_e[l])
    return rms_norm_2(x, norm_final_g)


def setup_inputs(seed=0):
    out = dict(first_inputs(seed))
    for name, value in second_inputs(seed + 1).items():
        if name != "x":
            out[name + "_2"] = value
    return out


def reference(
    x, c, ctx, c_ctx, norm_g, w_mod, b_mod, ffn1_w_gu, ffn1_w_d, ffn2_w_gu, ffn2_w_d,
    attn_w_qkv, attn_w_o, attn_q_g, attn_k_g, attn_lam_q1, attn_lam_k1, attn_lam_q2,
    attn_lam_k2, attn_sub_g, fourier_w, norm_mix_g_2, w_in_2, cmp_pos_k_2, cmp_w1_k_2,
    cmp_w2_k_2, cmp_pos_v_2, cmp_w1_v_2, cmp_w2_v_2, sinks_2, w_a_2, w_b_2, w_o_2, norm_ffn_g_2,
    w_group_2, b_group_2, w_expert_2, b_expert_2, w_gate_e_2, w_up_e_2, w_down_e_2,
    norm_final_g_2,
):
    x = first_block(
        x, c, ctx, c_ctx, norm_g, w_mod, b_mod, ffn1_w_gu, ffn1_w_d, ffn2_w_gu, ffn2_w_d,
        attn_w_qkv, attn_w_o, attn_q_g, attn_k_g, attn_lam_q1, attn_lam_k1, attn_lam_q2,
        attn_lam_k2, attn_sub_g, fourier_w,
    )
    return second_block(
        x, norm_mix_g_2, w_in_2, cmp_pos_k_2, cmp_w1_k_2, cmp_w2_k_2, cmp_pos_v_2, cmp_w1_v_2,
        cmp_w2_v_2, sinks_2, w_a_2, w_b_2, w_o_2, norm_ffn_g_2, w_group_2, b_group_2,
        w_expert_2, b_expert_2, w_gate_e_2, w_up_e_2, w_down_e_2, norm_final_g_2,
    )


_drawn_inputs = setup_inputs


def setup_inputs(seed=0):
    import zlib

    import numpy as np

    out = dict(_drawn_inputs(seed))
    spreads = {}
    factors = {'attn_q_g': 4.855,
     'attn_k_g': 4.042,
     'attn_lam_q1': 3.201,
     'attn_lam_k1': 3.914,
     'attn_lam_q2': 3.43,
     'attn_lam_k2': 5.482,
     'norm_mix_g_2': 4.053,
     'cmp_pos_k_2': 6.729,
     'b_group_2': 27.456,
     'b_expert_2': 20.81,
     'norm_final_g_2': 8.048,
     'cmp_pos_v_2': 5.382,
     'sinks_2': 8.0,
     'norm_ffn_g_2': 5.878}
    for name, (base, spread) in spreads.items():
        noise = np.random.default_rng([zlib.crc32(name.encode()), seed]).standard_normal(out[name].shape)
        drawn = base * np.exp(spread * noise) if base else spread * noise
        out[name] = jnp.asarray(drawn.astype(out[name].dtype))
    for name, factor in factors.items():
        out[name] = (out[name] * factor).astype(out[name].dtype)
    return out
```

```python
from contextlib import ExitStack

import numpy as np

import concourse.bass as bass
from concourse import mybir

F32 = mybir.dt.float32
ALU = mybir.AluOpType
ACT = mybir.ActivationFunctionType
AX_X = mybir.AxisListType.X
ds = bass.ds

P = 128
D = 1024
KD = D // P
NX = 512
NY = 256
NT = NX + NY
FF = 2816
KF = FF // P
NMOD = 9
EPS = 1e-6
CMP_LEN, CMP_STRIDE, CMP_HIDDEN = 32, 16, 256
CMP_BLOCKS = NX // CMP_STRIDE - CMP_LEN // CMP_STRIDE + 1
NSA_WINDOW, SWA_WINDOW = 256, 128
EXPERTS, GROUPS = 32, 4
HEADS = 8
HD = 64
KT = NT // P
LAMBDA_INIT = 0.2
SLOTS = 3
SLOT = KF * P


class Count:

    def __init__(self, ctx, nc, name):
        self.sem = ctx.enter_context(nc.semaphore(name))
        self.at = 0


class Ring:

    def __init__(self, ctx, nc):
        self.buf = ctx.enter_context(nc.sbuf_tensor("weights", [P, SLOTS, SLOT], F32))
        self.landed = [ctx.enter_context(nc.semaphore(f"slab_landed{s}")) for s in range(SLOTS)]
        self.used = [ctx.enter_context(nc.semaphore(f"slab_used{s}")) for s in range(SLOTS)]
        self.n = [0] * SLOTS

    def view(self, s, *dims):
        size = int(np.prod(dims))
        names = "abcd"[:len(dims)]
        flat = self.buf[:, s, 0:size]
        if len(dims) == 1:
            return flat
        return flat.rearrange(f"p ({' '.join(names)}) -> p {' '.join(names)}",
                              **{a: n for a, n in zip(names, dims)})


def program(nc, io):
    with ExitStack() as ctx:
        build(nc, io, ctx)


def build(nc, io, ctx):
    def sb(name, shape):
        return ctx.enter_context(nc.sbuf_tensor(name, shape, F32))

    def count(name):
        return Count(ctx, nc, name)

    ring = Ring(ctx, nc)
    ps = ctx.enter_context(nc.psum_tensor("ps", [P, 8, 512], F32))

    xy = sb("xy", [P, KD, NT])
    hbuf = sb("hbuf", [P, KD * NT])
    h = hbuf[:].rearrange("p (k n) -> p k n", k=KD)
    big = sb("big", [P, KF * NT])
    ones = sb("ones", [P, P])
    eps = sb("eps", [P, 1])
    cond = sb("cond", [P, KD, 2])
    scond = sb("scond", [P, KD, 2])
    mods = sb("mods", [P, NMOD * KD, 2])
    bmod = sb("bmod", [P, NMOD * KD, 2])
    normg = sb("normg", [P, 3 * KD, 2])
    modA = sb("modA", [P, 3, KD, 2])
    rstd = sb("rstd", [P, NT])
    tmp = sb("tmp", [P, 2, NT])

    work = sb("work", [P, 12 * NT])
    bones = sb("bones", [P, P])
    ident = sb("ident", [P, P])
    rope = sb("rope", [P, 4, NX])
    rot = sb("rot", [P, 3, P])
    qkg = sb("qkg", [P, 2])
    lamv = work[:, 0:4 * HD].rearrange("p (a n) -> p a n", a=4)
    lamt = sb("lamt", [P, 8])
    subg = sb("subg", [P, 2])
    stat = sb("stat", [P, 2, 8])
    gains2 = sb("gains2", [P, 3, KD, 1])
    dist = tmp[:].rearrange("p a n -> p (a n)")[:, 0:1152]
    dist_c = sb("dist_c", [P, 4, CMP_BLOCKS])
    slopes = sb("slopes", [P, 16])
    sinks = sb("sinks", [P, 8])
    gates = sb("gates", [P, HEADS, 3, 4])
    stat2 = sb("stat2", [P, 2, 4, 16])
    kc_sb = sb("kc", [P, CMP_BLOCKS])
    vc_sb = sb("vc", [CMP_BLOCKS, 2, HD])

    loaded = count("inputs_loaded")
    tables = count("tables_landed")
    proj_done = [count(f"head_product{s}") for s in range(2)]
    raw_done = [count(f"head_copied{s}") for s in range(2)]
    hss_done = [count(f"head_square_sums{s}") for s in range(2)]
    hroot = [count(f"head_roots{s}") for s in range(2)]
    t1_done = [count(f"rope_cos_part{s}") for s in range(2)]
    head_done = [count(f"head_normalised{s}") for s in range(2)]
    staged = [count(f"head_staged{s}") for s in range(2)]
    score_done = [count(f"scores{s}") for s in range(2)]
    max_done = [count(f"score_max{s}") for s in range(2)]
    exp_done = [count(f"exponentials{s}") for s in range(2)]
    prob_done = [count(f"probabilities{s}") for s in range(2)]
    turn_done = [count(f"turned{s}") for s in range(2)]
    turn_ev = [count(f"turned_copied{s}") for s in range(2)]
    pv_done = [count(f"values_product{s}") for s in range(2)]
    o_done = [count(f"output_copied{s}") for s in range(2)]
    const_set = count("constants_set")
    silu_done = count("condition_silu")
    mod_mm = [count(f"mod_product{s}") for s in range(SLOTS)]
    mod_ev = [count(f"mod_stored{s}") for s in range(SLOTS)]
    small_landed = count("mod_tables_landed")
    dve_chain = count("vector_step")
    sq_done = count("squares")
    ss_done = count("square_sums")
    root_done = count("roots")
    rstd_done = count("inverse_roots")
    scaled = count("scaled")
    shifted = count("shifted")
    gu_done = [count(f"gate_up_product{s}") for s in range(2)]
    silu_g = [count(f"gate_silu{s}") for s in range(2)]
    act_done = [count(f"hidden{s}") for s in range(2)]
    down_done = [count(f"down_product{s}") for s in range(2)]
    added = [count(f"residual_added{s}") for s in range(2)]
    out_done = count("out_stored")

    def step(ins):
        ins.then_inc(dve_chain.sem, 1)
        dve_chain.at += 1

    def steps_done(eng):
        eng.wait_ge(dve_chain.sem, dve_chain.at)

    def prefetch(sync, first, used):
        for s, src in first:
            sync.wait_ge(ring.used[s], used[s])
            sync.dma_start(ring.buf[:, s, 0:src.shape[1]], src).then_inc(ring.landed[s], 16)

    def first_mod(i):
        return [(s, io["w_mod"][i, s]) for s in range(3)]

    def first_gu(name, i):
        return [(s, io[name + "_gu"][i, s]) for s in range(2)]

    def open_counts(eng, counts):
        for c in counts:
            eng.sem_inc(c.sem, 1)
            c.at = 1

    def start(nxt):
        with nc.Block() as block:
            @block.sync
            def _(sync):
                prefetch(sync, nxt, ring.n)
                sync.dma_start(cond[:], io["cond"]).then_inc(loaded.sem, 16)
                sync.dma_start(xy[:], io["xy"]).then_inc(loaded.sem, 16)

            @block.tensor
            def _(pe):
                open_counts(pe, pv_done + turn_done + proj_done + score_done)

            @block.vector
            def _(vector):
                open_counts(vector, mod_ev + act_done + added + head_done + prob_done + o_done)
                vector.memset(ones[:], 1.0).then_inc(const_set.sem, 1)
                vector.memset(eps[:], EPS).then_inc(const_set.sem, 1)

            @block.scalar
            def _(scalar):
                open_counts(scalar, raw_done + exp_done + turn_ev)
                scalar.wait_ge(loaded.sem, 32)
                scalar.activation(scond[:], cond[:], ACT.Silu).then_inc(silu_done.sem, 1)
        loaded.at = 32

    def modulation(i, nxt):
        turns = NMOD * KD // 2 // SLOTS
        n0 = list(ring.n)
        m0 = [c.at for c in mod_mm]
        e0 = [c.at for c in mod_ev]
        t0 = small_landed.at
        with nc.Block() as block:
            @block.sync
            def _(sync):
                sync.dma_start(bmod[:], io["b_mod"][i]).then_inc(small_landed.sem, 16)
                sync.dma_start(normg[:], io["norm_g"][i]).then_inc(small_landed.sem, 16)
                with sync.Fori(0, turns - 1) as t:
                    for s in range(SLOTS):
                        sync.wait_ge(ring.used[s], t + (n0[s] + 1))
                        sync.dma_start(ring.buf[:, s, 0:2 * KD * P],
                                       io["w_mod"][i, ds(t * SLOTS + (SLOTS + s), 1)].rearrange("a p n -> (a p) n"))\
                            .then_inc(ring.landed[s], 16)
                prefetch(sync, nxt, [n + turns for n in n0])

            @block.tensor
            def _(pe):
                pe.wait_ge(silu_done.sem, 1)
                with pe.Fori(0, turns) as t:
                    for s in range(SLOTS):
                        w = ring.view(s, 2, KD, P)
                        pe.wait_ge(ring.landed[s], t * 16 + 16 * (n0[s] + 1))
                        pe.wait_ge(mod_ev[s].sem, t + e0[s])
                        for j in range(2):
                            for k in range(KD):
                                mm = pe.matmul(ps[:, s, 2 * j:2 * j + 2], w[:, j, k, :], scond[:, k, :],
                                               start=(k == 0), stop=(k == KD - 1))
                        mm.then_inc(mod_mm[s].sem, 1)
                        pe.wait_ge(mod_mm[s].sem, t + (m0[s] + 1))
                        pe.sem_inc(ring.used[s], 1)

            @block.vector
            def _(vector):
                vector.wait_ge(small_landed.sem, t0 + 32)
                with vector.Fori(0, turns) as t:
                    for s in range(SLOTS):
                        at = ds(t * (2 * SLOTS) + 2 * s, 2)
                        vector.wait_ge(mod_mm[s].sem, t + (m0[s] + 1))
                        vector.tensor_tensor(mods[:, at, :], ps[:, s, 0:4].rearrange("p (a b) -> p a b", a=2),
                                             bmod[:, at, :], ALU.add).then_inc(mod_ev[s].sem, 1)
                for s in range(SLOTS):
                    vector.wait_ge(mod_ev[s].sem, e0[s] + turns)
                for j in range(3):
                    a = (3 * j + 1) * KD
                    step(vector.scalar_tensor_tensor(modA[:, j], mods[:, a:a + KD, :], 1.0,
                                                     normg[:, j * KD:(j + 1) * KD, :], ALU.add, ALU.mult))
                for j in (2, 8):
                    step(vector.tensor_scalar(mods[:, j * KD:(j + 1) * KD, :], mods[:, j * KD:(j + 1) * KD, :],
                                              0.5, None, ALU.mult))
                steps_done(vector)
        for s in range(SLOTS):
            ring.n[s] += turns
            mod_mm[s].at += turns
            mod_ev[s].at += turns
        small_landed.at += 32

    def norm(cols, gain, shift):
        s0, q0, r0, i0, c0, f0 = (c.at for c in (sq_done, ss_done, root_done, rstd_done, scaled, shifted))
        sq = big[:, 0:KD * NT].rearrange("p (k n) -> p k n", k=KD)
        parts = [(0, NX, 0), (NX, NY, 1)][:1 if cols == NX else 2]
        with nc.Block() as block:
            @block.scalar
            def _(scalar):
                for k in range(KD):
                    scalar.activation(sq[:, k, 0:cols], xy[:, k, 0:cols], ACT.Square).then_inc(sq_done.sem, 1)
                scalar.wait_ge(ss_done.sem, q0 + 1)
                for a, n, c in parts:
                    scalar.activation(tmp[:, 0, a:a + n], ps[:, c, 0:n], ACT.Sqrt, bias=eps[:, 0:1],
                                      scale=1.0 / D).then_inc(root_done.sem, 1)
                if shift is not None:
                    for k in range(KD):
                        for a, n, c in parts:
                            scalar.wait_ge(scaled.sem, c0 + k * len(parts) + c + 1)
                            scalar.activation(h[:, k, a:a + n], h[:, k, a:a + n], ACT.Identity,
                                              bias=shift[:, k, c:c + 1]).then_inc(shifted.sem, 1)
                    scalar.wait_ge(shifted.sem, f0 + KD * len(parts))

            @block.tensor
            def _(pe):
                pe.wait_ge(const_set.sem, 2)
                for k in range(KD):
                    pe.wait_ge(sq_done.sem, s0 + k + 1)
                    for a, n, c in parts:
                        mm = pe.matmul(ps[:, c, 0:n], ones[:], sq[:, k, a:a + n],
                                       start=(k == 0), stop=(k == KD - 1))
                mm.then_inc(ss_done.sem, 1)

            @block.vector
            def _(vector):
                vector.wait_ge(root_done.sem, r0 + len(parts))
                vector.reciprocal(rstd[:, 0:cols], tmp[:, 0, 0:cols]).then_inc(rstd_done.sem, 1)
                vector.wait_ge(rstd_done.sem, i0 + 1)
                for k in range(KD):
                    for a, n, c in parts:
                        vector.scalar_tensor_tensor(h[:, k, a:a + n], xy[:, k, a:a + n], gain[:, k, c:c + 1],
                                                    rstd[:, a:a + n], ALU.mult, ALU.mult)\
                            .then_inc(scaled.sem, 1)
                vector.wait_ge(scaled.sem, c0 + KD * len(parts))
        sq_done.at += KD
        ss_done.at += 1
        root_done.at += len(parts)
        rstd_done.at += 1
        scaled.at += KD * len(parts)
        if shift is not None:
            shifted.at += KD * len(parts)

    def feed_forward(name, i, cols, gate, nxt):
        act = big[:].rearrange("p (f n) -> p f n", f=KF)
        parts = [(0, NX), (NX, NY)][:1 if cols == NX else 2]
        wgu, wd = io[name + "_gu"], io[name + "_d"]
        turns, dturns = KF // 2, KD // 2
        n0 = list(ring.n)
        g0, s0, a0, d0, r0 = ([c.at for c in cs] for cs in (gu_done, silu_g, act_done, down_done, added))

        def gate_up(s, j, a, n):
            return ps[:, 3 * s + j, 0:n] if a == 0 else ps[:, 3 * s + 2, j * NY:(j + 1) * NY]

        with nc.Block() as block:
            @block.sync
            def _(sync):
                with sync.Fori(0, turns - 1) as t:
                    for s in range(2):
                        sync.wait_ge(ring.used[s], t + (n0[s] + 1))
                        sync.dma_start(ring.buf[:, s, 0:2 * KD * P],
                                       wgu[i, ds(t * 2 + (2 + s), 1)].rearrange("a p n -> (a p) n"))\
                            .then_inc(ring.landed[s], 16)
                prefetch(sync, [(s, wd[i, s]) for s in range(2)], [n + turns for n in n0])
                with sync.Fori(0, dturns - 1) as t:
                    for s in range(2):
                        sync.wait_ge(ring.used[s], t + (n0[s] + turns + 1))
                        sync.dma_start(ring.buf[:, s, :], wd[i, ds(t * 2 + (2 + s), 1)].rearrange("a p n -> (a p) n"))\
                            .then_inc(ring.landed[s], 16)
                prefetch(sync, nxt, [n + (turns + dturns if s < 2 else 0) for s, n in enumerate(n0)])

            @block.tensor
            def _(pe):
                with pe.Fori(0, turns) as t:
                    for s in range(2):
                        w = ring.view(s, 2, KD, P)
                        pe.wait_ge(ring.landed[s], t * 16 + 16 * (n0[s] + 1))
                        pe.wait_ge(act_done[s].sem, t * len(parts) + a0[s])
                        for j in range(2):
                            for a, n in parts:
                                for k in range(KD):
                                    mm = pe.matmul(gate_up(s, j, a, n), w[:, j, k, :], h[:, k, a:a + n],
                                                   start=(k == 0), stop=(k == KD - 1))
                        mm.then_inc(gu_done[s].sem, 1)
                        pe.wait_ge(gu_done[s].sem, t + (g0[s] + 1))
                        pe.sem_inc(ring.used[s], 1)
                for s in range(2):
                    pe.wait_ge(act_done[s].sem, a0[s] + turns * len(parts))
                with pe.Fori(0, dturns) as t:
                    for s in range(2):
                        w = ring.view(s, KF, P)
                        pe.wait_ge(ring.landed[s], t * 16 + 16 * (n0[s] + turns + 1))
                        pe.wait_ge(added[s].sem, t * len(parts) + r0[s])
                        for c, (a, n) in enumerate(parts):
                            for f in range(KF):
                                mm = pe.matmul(ps[:, 3 * s + c, 0:n], w[:, f, :], act[:, f, a:a + n],
                                               start=(f == 0), stop=(f == KF - 1))
                        mm.then_inc(down_done[s].sem, 1)
                        pe.wait_ge(down_done[s].sem, t + (d0[s] + 1))
                        pe.sem_inc(ring.used[s], 1)

            @block.scalar
            def _(scalar):
                with scalar.Fori(0, turns) as t:
                    for s in range(2):
                        scalar.wait_ge(gu_done[s].sem, t + (g0[s] + 1))
                        scalar.wait_ge(act_done[s].sem, t * len(parts) + a0[s])
                        for a, n in parts:
                            scalar.activation(tmp[:, s, a:a + n], gate_up(s, 0, a, n), ACT.Silu)\
                                .then_inc(silu_g[s].sem, 1)

            @block.vector
            def _(vector):
                with vector.Fori(0, turns) as t:
                    for s in range(2):
                        for c, (a, n) in enumerate(parts):
                            vector.wait_ge(silu_g[s].sem, t * len(parts) + (s0[s] + c + 1))
                            vector.tensor_tensor(act[:, ds(t * 2 + s, 1), a:a + n].rearrange("p a n -> p (a n)"),
                                                 gate_up(s, 1, a, n), tmp[:, s, a:a + n], ALU.mult)\
                                .then_inc(act_done[s].sem, 1)
                with vector.Fori(0, dturns) as t:
                    for s in range(2):
                        vector.wait_ge(down_done[s].sem, t + (d0[s] + 1))
                        for c, (a, n) in enumerate(parts):
                            x = xy[:, ds(t * 2 + s, 1), a:a + n].rearrange("p a n -> p (a n)")
                            g = gate[:, ds(t * 2 + s, 1), c:c + 1].rearrange("p a n -> p (a n)")
                            vector.scalar_tensor_tensor(x, ps[:, 3 * s + c, 0:n], g, x, ALU.mult, ALU.add)\
                                .then_inc(added[s].sem, 1)
                for s in range(2):
                    vector.wait_ge(added[s].sem, r0[s] + dturns * len(parts))
        for s in range(2):
            ring.n[s] += turns + dturns
            gu_done[s].at += turns
            silu_g[s].at += turns * len(parts)
            act_done[s].at += turns * len(parts)
            down_done[s].at += dturns
            added[s].at += dturns * len(parts)

    def finish(src, dst):
        o0 = out_done.at
        with nc.Block() as block:
            @block.sync
            def _(sync):
                sync.dma_start(dst, src).then_inc(out_done.sem, 16)
                sync.wait_ge(out_done.sem, o0 + 16)
        out_done.at += 16

    def advance(counts, n):
        for c in counts:
            c.at += n

    def attention_tables():
        t0, e0 = tables.at, exp_done[0].at
        with nc.Block() as block:
            @block.sync
            def _(sync):
                for dst, name in ((bones[:], "bones"), (ident[:], "ident"), (lamv, "lam"), (qkg[:], "qk_gain"),
                                  (subg[:, 0:1], "sub_gain"), (rope[:, 0:2], "rope"), (rot[:, 0], "rot")):
                    sync.dma_start(dst, io[name]).then_inc(tables.sem, 16)

            @block.vector
            def _(vector):
                vector.wait_ge(tables.sem, t0 + 16 * 7)
                for j in range(2):
                    step(vector.tensor_scalar(rope[:, 2 + j, :], rope[:, 0, :], qkg[:, j:j + 1], None, ALU.mult))
                    step(vector.tensor_scalar(rot[:, 1 + j, :], rot[:, 0, :], qkg[:, j:j + 1], None, ALU.mult))
                    step(vector.tensor_tensor(lamv[:, 2 * j, :], lamv[:, 2 * j, :], lamv[:, 2 * j + 1, :], ALU.mult))
                step(vector.tensor_scalar(subg[:, 1:2], subg[:, 0:1], 1.0 - LAMBDA_INIT, None, ALU.mult))
                steps_done(vector)
                for j in range(2):
                    step(vector.reduce_sum(lamt[:, j:j + 1], lamv[:, 2 * j, :], AX_X))
                lam_sum = dve_chain.at
                vector.wait_ge(exp_done[0].sem, e0 + 1)
                step(vector.tensor_tensor(lamt[:, 4:5], lamt[:, 3:4], lamt[:, 2:3], ALU.subtract))
                steps_done(vector)
                step(vector.tensor_scalar(lamt[:, 5:6], lamt[:, 4:5], -LAMBDA_INIT, None, ALU.add))
                steps_done(vector)
                lam_at.append(lam_sum)

            @block.scalar
            def _(scalar):
                scalar.wait_ge(dve_chain.sem, lam_at[0])
                scalar.activation(lamt[:, 2:4], lamt[:, 0:2], ACT.Exp).then_inc(exp_done[0].sem, 1)
        exp_done[0].at += 1
        tables.at += 16 * 7

    lam_at = []

    def head_inputs(which, dst, nxt):
        turns, slab0 = 2, 4 * which
        has_ctx = which == 1
        HSTEPS = 4 if has_ctx else 3
        n0 = list(ring.n)
        x0 = [c.at for c in hstep]
        p0, w0, q0, r0, t0, d0 = ([c.at for c in cs] for cs in (proj_done, raw_done, hss_done, hroot, t1_done, head_done))
        width = NT if has_ctx else NX
        raw = work[:, 4 * NT:8 * NT].rearrange("p (s j n) -> p s j n", s=2, j=2)
        sq = work[:, 0:4 * NT].rearrange("p (s j n) -> p s j n", s=2, j=2)
        root = work[:, 8 * NT:12 * NT].rearrange("p (s j n) -> p s j n", s=2, j=2)
        with nc.Block() as block:
            @block.sync
            def _(sync):
                with sync.Fori(0, turns - 1) as t:
                    for s in range(2):
                        sync.wait_ge(ring.used[s], t + (n0[s] + 1))
                        sync.dma_start(ring.buf[:, s, 0:2 * KD * P],
                                       io["w_qk"][ds(t * 2 + (slab0 + 2 + s), 1)].rearrange("a p n -> (a p) n"))\
                            .then_inc(ring.landed[s], 16)
                prefetch(sync, nxt, [n + (turns if s < 2 else 0) for s, n in enumerate(n0)])

            @block.tensor
            def _(pe):
                with pe.Fori(0, turns) as t:
                    for s in range(2):
                        w = ring.view(s, 2, KD, P)
                        pe.wait_ge(ring.landed[s], t * 16 + 16 * (n0[s] + 1))
                        if s == 1:
                            pe.wait_ge(raw_done[0].sem, t * 2 + (w0[0] + 2))
                        else:
                            pe.wait_ge(raw_done[1].sem, t * 2 + w0[1])
                        for j in range(2):
                            for k in range(KD):
                                mm = pe.matmul(ps[:, j, :], w[:, j, k, :], h[:, k, 0:NX], start=(k == 0), stop=(k == KD - 1))
                            if has_ctx:
                                for k in range(KD):
                                    mm = pe.matmul(ps[:, 2, j * NY:(j + 1) * NY], w[:, j, k, :], h[:, k, NX:NT],
                                                   start=(k == 0), stop=(k == KD - 1))
                        mm.then_inc(proj_done[s].sem, 1)
                        pe.wait_ge(proj_done[s].sem, t + (p0[s] + 1))
                        pe.sem_inc(ring.used[s], 1)
                        if s == 1:
                            pe.wait_ge(head_done[0].sem, t * 2 + (d0[0] + 2))
                        else:
                            pe.wait_ge(head_done[1].sem, t * 2 + d0[1])
                        for j in range(2):
                            pe.wait_ge(raw_done[s].sem, t * 2 + (w0[s] + j + 1))
                            pe.matmul(ps[:, 3 + j, :], rot[:, 1 + which, :], raw[:, s, j, 0:NX], start=True, stop=True)
                            mm = pe.matmul(ps[:, 5 + j, :], bones[:], sq[:, s, j, 0:NX], start=True, stop=True)
                            if has_ctx:
                                mm = pe.matmul(ps[:, 7, j * NY:(j + 1) * NY], bones[:], sq[:, s, j, NX:NT],
                                               start=True, stop=True)
                        mm.then_inc(hss_done[s].sem, 1)

            @block.scalar
            def _(scalar):
                with scalar.Fori(0, turns) as t:
                    for s in range(2):
                        scalar.wait_ge(proj_done[s].sem, t + (p0[s] + 1))
                        scalar.wait_ge(head_done[s].sem, t * 2 + d0[s])
                        for j in range(2):
                            ctx_ps = ps[:, 2, j * NY:(j + 1) * NY]
                            scalar.activation(raw[:, s, j, 0:NX], ps[:, j, :], ACT.Copy)
                            if has_ctx:
                                scalar.activation(raw[:, s, j, NX:NT], ctx_ps, ACT.Copy)
                                scalar.activation(sq[:, s, j, NX:NT], ctx_ps, ACT.Square)
                            scalar.activation(sq[:, s, j, 0:NX], ps[:, j, :], ACT.Square).then_inc(raw_done[s].sem, 1)
                        scalar.wait_ge(hss_done[s].sem, t + (q0[s] + 1))
                        for j in range(2):
                            if has_ctx:
                                scalar.activation(root[:, s, j, NX:NT], ps[:, 7, j * NY:(j + 1) * NY], ACT.Sqrt,
                                                  bias=eps[:, 0:1], scale=1.0 / HD)
                            scalar.activation(root[:, s, j, 0:NX], ps[:, 5 + j, :], ACT.Sqrt,
                                              bias=eps[:, 0:1], scale=1.0 / HD).then_inc(hroot[s].sem, 1)

            @block.gpsimd
            def _(gpsimd):
                with gpsimd.Fori(0, turns) as t:
                    for s in range(2):
                        for j in range(2):
                            gpsimd.wait_ge(raw_done[s].sem, t * 2 + (w0[s] + j + 1))
                            gpsimd.wait_ge(hss_done[s].sem, t + (q0[s] + 1))
                            gpsimd.tensor_tensor(sq[:, s, j, 0:NX], raw[:, s, j, 0:NX], rope[:, 2 + which, :], ALU.mult)\
                                .then_inc(t1_done[s].sem, 1)

            @block.vector
            def _(vector):
                with vector.Fori(0, turns) as t:
                    for s in range(2):
                        for j in range(2):
                            out = ds(t * 4 + (2 * s + j), 1)
                            r = root[:, s, j, 0:width]
                            vector.wait_ge(hroot[s].sem, t * 2 + (r0[s] + j + 1))
                            vector.reciprocal(r, r).then_inc(hstep[s].sem, 1)
                            vector.wait_ge(t1_done[s].sem, t * 2 + (t0[s] + j + 1))
                            vector.tensor_tensor(raw[:, s, j, 0:NX], ps[:, 3 + j, :], rope[:, 1, :], ALU.mult)\
                                .then_inc(hstep[s].sem, 1)
                            vector.wait_ge(hstep[s].sem, t * (2 * HSTEPS) + (x0[s] + HSTEPS * j + 2))
                            vector.tensor_tensor(raw[:, s, j, 0:NX], raw[:, s, j, 0:NX], sq[:, s, j, 0:NX], ALU.add)\
                                .then_inc(hstep[s].sem, 1)
                            if has_ctx:
                                vector.scalar_tensor_tensor(dst[:, out, NX:NT].rearrange("p a n -> p (a n)"),
                                                            raw[:, s, j, NX:NT], qkg[:, 1:2], r[:, NX:NT],
                                                            ALU.mult, ALU.mult).then_inc(hstep[s].sem, 1)
                            vector.wait_ge(hstep[s].sem, t * (2 * HSTEPS) + (x0[s] + HSTEPS * j + HSTEPS))
                            vector.tensor_tensor(dst[:, out, 0:NX].rearrange("p a n -> p (a n)"),
                                                 raw[:, s, j, 0:NX], r[:, 0:NX], ALU.mult).then_inc(head_done[s].sem, 1)
                for s in range(2):
                    vector.wait_ge(head_done[s].sem, d0[s] + 2 * turns)
        for s in range(2):
            ring.n[s] += turns
        for cs, n in ((proj_done, turns), (raw_done, 2 * turns), (hss_done, turns), (hroot, 2 * turns),
                      (t1_done, 2 * turns), (head_done, 2 * turns), (hstep, 2 * HSTEPS * turns)):
            advance(cs, n)

    hstep = [count(f"head_step{s}") for s in range(2)]

    def values(V, nxt):
        turns, C = 2, 2 * P
        n0 = list(ring.n)
        p0, w0 = ([c.at for c in cs] for cs in (proj_done, raw_done))
        with nc.Block() as block:
            @block.sync
            def _(sync):
                with sync.Fori(0, turns - 1) as t:
                    for s in range(2):
                        sync.wait_ge(ring.used[s], t + (n0[s] + 1))
                        sync.dma_start(ring.buf[:, s, 0:KD * C],
                                       io["w_v"][ds(t * 2 + (2 + s), 1)].rearrange("a p n -> (a p) n"))\
                            .then_inc(ring.landed[s], 16)
                prefetch(sync, nxt, [n + (turns if s < 2 else 0) for s, n in enumerate(n0)])

            @block.tensor
            def _(pe):
                with pe.Fori(0, turns) as t:
                    for s in range(2):
                        w = ring.view(s, KD, C)
                        pe.wait_ge(ring.landed[s], t * 16 + 16 * (n0[s] + 1))
                        for m in range(KT):
                            if s == 1:
                                pe.wait_ge(raw_done[0].sem, t * KT + (w0[0] + m + 1))
                            else:
                                pe.wait_ge(raw_done[1].sem, t * KT + w0[1])
                            for k in range(KD):
                                mm = pe.matmul(ps[:, m, 0:C], h[:, k, m * P:(m + 1) * P], w[:, k, :],
                                               start=(k == 0), stop=(k == KD - 1))
                            mm.then_inc(proj_done[s].sem, 1)
                        pe.wait_ge(proj_done[s].sem, t * KT + (p0[s] + KT))
                        pe.sem_inc(ring.used[s], 1)

            @block.scalar
            def _(scalar):
                with scalar.Fori(0, turns) as t:
                    for s in range(2):
                        for m in range(KT):
                            scalar.wait_ge(proj_done[s].sem, t * KT + (p0[s] + m + 1))
                            scalar.activation(V[:, m, ds(t * 2 * C + s * C, C)], ps[:, m, 0:C], ACT.Copy)\
                                .then_inc(raw_done[s].sem, 1)
                for s in range(2):
                    scalar.wait_ge(raw_done[s].sem, w0[s] + turns * KT)
        for s in range(2):
            ring.n[s] += turns
        advance(proj_done, KT * turns)
        advance(raw_done, KT * turns)

    def attention(Q, K, V, O):
        QT = NX // P
        turns = HEADS // 2
        names = (staged, score_done, max_done, exp_done, prob_done, turn_done, turn_ev, pv_done, o_done, hstep)
        g0, s0, m0, e0, b0, u0, v0, p0, o0, h0 = ([c.at for c in cs] for cs in names)
        at = [0]

        def part(n):
            at[0] += n
            return work[:, at[0] - n:at[0]]

        qs = [hbuf[:, (HEADS + b) * NX:(HEADS + b + 1) * NX] for b in range(2)]
        ks = [part(NT) for _ in range(2)]
        vs = [part(NT).rearrange("p (m n) -> p m n", m=KT) for _ in range(2)]
        pr = [part(2 * NT).rearrange("p (c n) -> p c n", c=2) for _ in range(2)]
        aT = part(KT * NX).rearrange("p (m n) -> p m n", m=KT)
        sc = ps[:, 0:4, :].rearrange("p (c b) n -> p c (b n)", c=2)
        tp = ps[:, 4:6, :].rearrange("p b n -> p (b n)")

        with nc.Block() as block:
            @block.gpsimd
            def _(gpsimd):
                with gpsimd.Fori(0, turns) as t:
                    for b in range(2):
                        hd = ds(t * 2 + b, 1)
                        gpsimd.wait_ge(pv_done[b].sem, t + p0[b])
                        gpsimd.tensor_copy(qs[b], Q[:, hd, :].rearrange("p a n -> p (a n)")).then_inc(staged[b].sem, 1)
                        gpsimd.tensor_copy(ks[b], K[:, hd, :].rearrange("p a n -> p (a n)")).then_inc(staged[b].sem, 1)
                        gpsimd.tensor_copy(vs[b], V[:, :, ds(t * 2 * P + b * P, P)]).then_inc(staged[b].sem, 1)

            @block.tensor
            def _(pe):
                def scores(t, b, q):
                    if q > 0:
                        pe.wait_ge(exp_done[b].sem, t * (2 * QT) + (e0[b] + 2 * q))
                    elif b == 1:
                        pe.wait_ge(exp_done[0].sem, t * (2 * QT) + (e0[0] + 2 * QT))
                    else:
                        pe.wait_ge(exp_done[1].sem, t * (2 * QT) + e0[1])
                    for c in range(2):
                        half = slice(c * HD, (c + 1) * HD)
                        for a, n in ((0, NX), (NX, NY)):
                            mm = pe.matmul(sc[:, c, a:a + n], qs[b][half, q * P:(q + 1) * P], ks[b][half, a:a + n],
                                           start=True, stop=True)
                    mm.then_inc(score_done[b].sem, 1)

                def turn(t, b, q):
                    pe.wait_ge(prob_done[b].sem, t * QT + (b0[b] + q + 1))
                    if q > 0:
                        pe.wait_ge(turn_ev[b].sem, t * QT + (v0[b] + q))
                    elif b == 1:
                        pe.wait_ge(turn_ev[0].sem, t * QT + (v0[0] + QT))
                    else:
                        pe.wait_ge(turn_ev[1].sem, t * QT + v0[1])
                    for m in range(KT):
                        mm = pe.transpose(tp[:, m * P:(m + 1) * P], pr[q % 2][:, 0, m * P:(m + 1) * P], ident[:])
                    mm.then_inc(turn_done[b].sem, 1)

                with pe.Fori(0, turns) as t:
                    for b in range(2):
                        pe.wait_ge(staged[b].sem, t * 3 + (g0[b] + 3))
                        scores(t, b, 0)
                        for q in range(QT):
                            if q + 1 < QT:
                                scores(t, b, q + 1)
                            turn(t, b, q)
                        pe.wait_ge(turn_ev[b].sem, t * QT + (v0[b] + QT))
                        pe.wait_ge(o_done[b].sem, t + o0[b])
                        for m in range(KT):
                            mm = pe.matmul(ps[:, 6 + b, :], vs[b][:, m, :], aT[:, m, :], start=(m == 0), stop=(m == KT - 1))
                        mm.then_inc(pv_done[b].sem, 1)

            @block.scalar
            def _(scalar):
                with scalar.Fori(0, turns) as t:
                    for b in range(2):
                        for q in range(QT):
                            scalar.wait_ge(max_done[b].sem, t * QT + (m0[b] + q + 1))
                            if q >= 2:
                                scalar.wait_ge(turn_done[b].sem, t * QT + (u0[b] + q - 1))
                            elif b == 1:
                                scalar.wait_ge(turn_done[0].sem, t * QT + (u0[0] + QT - 1 + q))
                            for c in range(2):
                                if q < 2 and b == 0 and c == 0:
                                    scalar.wait_ge(turn_done[1].sem, t * QT + u0[1])
                                scalar.activation(pr[q % 2][:, c, :], sc[:, c, 0:NT], ACT.Exp,
                                                  bias=stat[:, q % 2, 2 + c:3 + c], scale=HD ** -0.5,
                                                  accum_out=stat[:, q % 2, 4 + c:5 + c]).then_inc(exp_done[b].sem, 1)
                            if q > 0:
                                scalar.wait_ge(turn_done[b].sem, t * QT + (u0[b] + q))
                                if q == 1:
                                    if b == 1:
                                        scalar.wait_ge(pv_done[0].sem, t + (p0[0] + 1))
                                    else:
                                        scalar.wait_ge(pv_done[1].sem, t + p0[1])
                                scalar.activation(aT[:, :, (q - 1) * P:q * P], tp[:, 0:NT].rearrange("p (m n) -> p m n", m=KT),
                                                  ACT.Copy).then_inc(turn_ev[b].sem, 1)
                        scalar.wait_ge(turn_done[b].sem, t * QT + (u0[b] + QT))
                        scalar.activation(aT[:, :, (QT - 1) * P:QT * P], tp[:, 0:NT].rearrange("p (m n) -> p m n", m=KT),
                                          ACT.Copy).then_inc(turn_ev[b].sem, 1)

            @block.vector
            def _(vector):
                VS = 5

                def softmax(t, b, q):
                    def sstep(ins, n):
                        ins.then_inc(hstep[b].sem, 1)
                        vector.wait_ge(hstep[b].sem, t * (VS * QT) + (h0[b] + VS * q + n))
                    st = stat[:, q % 2]
                    vector.wait_ge(score_done[b].sem, t * QT + (s0[b] + q + 1))
                    sstep(vector.reduce_max(st[:, 0:2], sc[:, :, 0:NT], AX_X), 1)
                    vector.tensor_scalar(st[:, 2:4], st[:, 0:2], -HD ** -0.5, None, ALU.mult).then_inc(max_done[b].sem, 1)
                    vector.wait_ge(exp_done[b].sem, t * (2 * QT) + (e0[b] + 2 * q + 2))
                    sstep(vector.reciprocal(st[:, 6:8], st[:, 4:6]), 2)
                    sstep(vector.tensor_scalar(st[:, 7:8], st[:, 7:8], lamt[:, 5:6], None, ALU.mult), 3)
                    sstep(vector.tensor_scalar(pr[q % 2][:, 0, :], pr[q % 2][:, 0, :], st[:, 6:7], None, ALU.mult), 4)
                    sstep(vector.scalar_tensor_tensor(pr[q % 2][:, 0, :], pr[q % 2][:, 1, :], st[:, 7:8],
                                                      pr[q % 2][:, 0, :], ALU.mult, ALU.add), 5)
                    vector.sem_inc(prob_done[b].sem, 1)

                with vector.Fori(0, turns) as t:
                    for b in range(2):
                        for q in range(QT):
                            softmax(t, b, q)
                        vector.wait_ge(pv_done[b].sem, t + (p0[b] + 1))
                        vector.tensor_copy(O[:, ds(t * 2 + b, 1), :].rearrange("p a n -> p (a n)"), ps[:, 6 + b, :])\
                            .then_inc(o_done[b].sem, 1)
                for b in range(2):
                    vector.wait_ge(o_done[b].sem, o0[b] + turns)
        for cs, n in zip(names, (3, QT, QT, 2 * QT, QT, QT, QT, 1, 1, 5 * QT)):
            advance(cs, n * turns)

    def output_norm(O, gain):
        q0, r0, s0, h0, d0 = (c.at for c in (sq_done, root_done, ss_done, rstd_done, scaled))
        sq = work[:, 0:2 * NX].rearrange("p (b n) -> p b n", b=2)
        with nc.Block() as block:
            @block.scalar
            def _(scalar):
                for j in range(HEADS):
                    if j >= 2:
                        scalar.wait_ge(ss_done.sem, s0 + j - 1)
                    scalar.activation(sq[:, j % 2, :], O[:, j, :], ACT.Square).then_inc(sq_done.sem, 1)
                for j in range(HEADS):
                    scalar.wait_ge(ss_done.sem, s0 + j + 1)
                    if j >= 2:
                        scalar.wait_ge(scaled.sem, d0 + j - 1)
                    scalar.activation(tmp[:, j % 2, 0:NX], ps[:, j, :], ACT.Sqrt, bias=eps[:, 0:1], scale=1.0 / P)\
                        .then_inc(root_done.sem, 1)

            @block.tensor
            def _(pe):
                for j in range(HEADS):
                    pe.wait_ge(sq_done.sem, q0 + j + 1)
                    pe.matmul(ps[:, j, :], ones[:], sq[:, j % 2, :], start=True, stop=True).then_inc(ss_done.sem, 1)

            @block.vector
            def _(vector):
                for j in range(HEADS):
                    vector.wait_ge(root_done.sem, r0 + j + 1)
                    vector.reciprocal(tmp[:, j % 2, 0:NX], tmp[:, j % 2, 0:NX]).then_inc(rstd_done.sem, 1)
                    vector.wait_ge(rstd_done.sem, h0 + j + 1)
                    vector.scalar_tensor_tensor(O[:, j, :], O[:, j, :], gain, tmp[:, j % 2, 0:NX], ALU.mult, ALU.mult)\
                        .then_inc(scaled.sem, 1)
                vector.wait_ge(scaled.sem, d0 + HEADS)
        for c in (sq_done, root_done, ss_done, rstd_done, scaled):
            c.at += HEADS

    def project_residual(w, src, gate, nxt):
        turns = 2
        n0 = list(ring.n)
        d0, r0 = ([c.at for c in cs] for cs in (down_done, added))
        with nc.Block() as block:
            @block.sync
            def _(sync):
                with sync.Fori(0, turns - 1) as t:
                    for s in range(2):
                        sync.wait_ge(ring.used[s], t + (n0[s] + 1))
                        sync.dma_start(ring.buf[:, s, 0:2 * KD * P], w[ds(t * 2 + (2 + s), 1)].rearrange("a p n -> (a p) n"))\
                            .then_inc(ring.landed[s], 16)
                prefetch(sync, nxt, [n + (turns if s < 2 else 0) for s, n in enumerate(n0)])

            @block.tensor
            def _(pe):
                with pe.Fori(0, turns) as t:
                    for s in range(2):
                        wv = ring.view(s, 2, KD, P)
                        pe.wait_ge(ring.landed[s], t * 16 + 16 * (n0[s] + 1))
                        pe.wait_ge(added[s].sem, t * 2 + r0[s])
                        for j in range(2):
                            for k in range(KD):
                                mm = pe.matmul(ps[:, 2 * s + j, :], wv[:, j, k, :], src[:, k, 0:NX],
                                               start=(k == 0), stop=(k == KD - 1))
                        mm.then_inc(down_done[s].sem, 1)
                        pe.wait_ge(down_done[s].sem, t + (d0[s] + 1))
                        pe.sem_inc(ring.used[s], 1)

            @block.vector
            def _(vector):
                with vector.Fori(0, turns) as t:
                    for s in range(2):
                        vector.wait_ge(down_done[s].sem, t + (d0[s] + 1))
                        for j in range(2):
                            x = xy[:, ds(t * 4 + (2 * s + j), 1), 0:NX].rearrange("p a n -> p (a n)")
                            if gate is None:
                                vector.tensor_tensor(x, ps[:, 2 * s + j, :], x, ALU.add).then_inc(added[s].sem, 1)
                            else:
                                g = gate[:, ds(t * 4 + (2 * s + j), 1), 0:1].rearrange("p a n -> p (a n)")
                                vector.scalar_tensor_tensor(x, ps[:, 2 * s + j, :], g, x, ALU.mult, ALU.add)\
                                    .then_inc(added[s].sem, 1)
                for s in range(2):
                    vector.wait_ge(added[s].sem, r0[s] + 2 * turns)
        for s in range(2):
            ring.n[s] += turns
        advance(down_done, turns)
        advance(added, 2 * turns)

    def second_gains():
        t0 = tables.at
        with nc.Block() as block:
            @block.sync
            def _(sync):
                sync.dma_start(gains2[:], io["gains2"]).then_inc(tables.sem, 16)
                sync.wait_ge(tables.sem, t0 + 16)
        tables.at += 16

    def fourier(F):
        groups, TT = 4, NX // P
        C = 2 * (D // groups)
        Y = big[:, 0:TT * groups * C].rearrange("p (t g n) -> p t g n", t=TT, g=groups)
        cd = big[:, TT * groups * C:TT * groups * C + 2 * C].rearrange("p (k n) -> p k n", k=2)
        cn = big[:, 9216:9216 + 2 * TT * NX].rearrange("p (c t n) -> p c t n", c=2, t=TT)
        t0, p0, w0 = tables.at, [c.at for c in proj_done], [c.at for c in raw_done]
        units = TT * groups
        with nc.Block() as block:
            @block.sync
            def _(sync):
                sync.dma_start(cd, io["dft_feature"]).then_inc(tables.sem, 16)
                sync.dma_start(cn, io["dft_token"]).then_inc(tables.sem, 16)

            @block.tensor
            def _(pe):
                pe.wait_ge(tables.sem, t0 + 32)
                for u in range(units):
                    t, g = u // groups, u % groups
                    if u >= 8:
                        pe.wait_ge(raw_done[u % 2].sem, w0[u % 2] + (u - 8) // 2 + 1)
                    for k in range(2):
                        mm = pe.matmul(ps[:, u % 8, :], h[:, 2 * g + k, t * P:(t + 1) * P], cd[:, k, :],
                                       start=(k == 0), stop=(k == 1))
                    mm.then_inc(proj_done[u % 2].sem, 1)
                for s in range(2):
                    pe.wait_ge(raw_done[s].sem, w0[s] + units // 2)
                for m in range(KD):
                    g, half = m // 2, (m % 2) * P
                    for n in range(2 * TT):
                        c, t = n // TT, n % TT
                        a = c * (C // 2) + half
                        mm = pe.matmul(ps[:, m, :], Y[:, t, g, a:a + P], cn[:, c, t, :],
                                       start=(n == 0), stop=(n == 2 * TT - 1))
                    mm.then_inc(proj_done[m % 2].sem, 1)

            def copies(eng, s, copy):
                for u in range(s, units, 2):
                    eng.wait_ge(proj_done[s].sem, p0[s] + u // 2 + 1)
                    copy(Y[:, u // groups, u % groups, :], ps[:, u % 8, :]).then_inc(raw_done[s].sem, 1)
                for m in range(s, KD, 2):
                    eng.wait_ge(proj_done[s].sem, p0[s] + units // 2 + m // 2 + 1)
                    copy(F[:, m, :], ps[:, m, :]).then_inc(raw_done[s].sem, 1)

            @block.scalar
            def _(scalar):
                copies(scalar, 0, scalar.copy)

            @block.vector
            def _(vector):
                copies(vector, 1, vector.tensor_copy)
        tables.at += 32
        advance(proj_done, (units + KD) // 2)
        advance(raw_done, (units + KD) // 2)

    def project(w, slab0, turns, dst, scale_of, func, nxt):
        n0 = list(ring.n)
        p0, w0 = ([c.at for c in cs] for cs in (proj_done, raw_done))
        with nc.Block() as block:
            @block.sync
            def _(sync):
                with sync.Fori(0, turns - 1) as t:
                    for s in range(2):
                        sync.wait_ge(ring.used[s], t + (n0[s] + 1))
                        sync.dma_start(ring.buf[:, s, 0:2 * KD * P],
                                       w[ds(t * 2 + (slab0 + 2 + s), 1)].rearrange("a p n -> (a p) n"))\
                            .then_inc(ring.landed[s], 16)
                prefetch(sync, nxt, [n + (turns if s < 2 else 0) for s, n in enumerate(n0)])

            @block.tensor
            def _(pe):
                with pe.Fori(0, turns) as t:
                    for s in range(2):
                        wv = ring.view(s, 2, KD, P)
                        pe.wait_ge(ring.landed[s], t * 16 + 16 * (n0[s] + 1))
                        pe.wait_ge(raw_done[s].sem, t * 2 + w0[s])
                        for j in range(2):
                            for k in range(KD):
                                mm = pe.matmul(ps[:, 2 * s + j, :], wv[:, j, k, :], h[:, k, 0:NX],
                                               start=(k == 0), stop=(k == KD - 1))
                            mm.then_inc(proj_done[s].sem, 1)
                        pe.wait_ge(proj_done[s].sem, t * 2 + (p0[s] + 2))
                        pe.sem_inc(ring.used[s], 1)

            @block.scalar
            def _(scalar):
                with scalar.Fori(0, turns) as t:
                    for s in range(2):
                        for j in range(2):
                            scalar.wait_ge(proj_done[s].sem, t * 2 + (p0[s] + j + 1))
                            scalar.activation(dst[:, ds(t * 4 + (2 * s + j), 1), :].rearrange("p a n -> p (a n)"),
                                              ps[:, 2 * s + j, :], func, scale=scale_of).then_inc(raw_done[s].sem, 1)
                for s in range(2):
                    scalar.wait_ge(raw_done[s].sem, w0[s] + 2 * turns)
        for s in range(2):
            ring.n[s] += turns
        advance(proj_done, 2 * turns)
        advance(raw_done, 2 * turns)

    def values_and_gates(F, V2):
        TT = NX // P
        wv = work[:, 0:KD * 3 * P].rearrange("p (k n) -> p k n", k=KD)
        t0, p0, w0, u0, v0 = tables.at, proj_done[0].at, raw_done[0].at, turn_done[0].at, turn_ev[0].at
        with nc.Block() as block:
            @block.sync
            def _(sync):
                sync.dma_start(wv, io["w_v2"]).then_inc(tables.sem, 16)
                for dst, name in ((dist, "dist"), (dist_c[:], "dist_cmp"), (slopes[:], "slopes"), (sinks[:], "sinks")):
                    sync.dma_start(dst, io[name]).then_inc(tables.sem, 16)

            @block.tensor
            def _(pe):
                for m in range(TT):
                    mm = pe.transpose(ps[:, 4, m * P:(m + 1) * P], F[:, 15, m * P:(m + 1) * P], ident[:])
                mm.then_inc(turn_done[0].sem, 1)
                pe.wait_ge(tables.sem, t0 + 5 * 16)
                for m in range(TT):
                    for k in range(KD):
                        mm = pe.matmul(ps[:, m, 0:3 * P], h[:, k, m * P:(m + 1) * P], wv[:, k, :],
                                       start=(k == 0), stop=(k == KD - 1))
                    mm.then_inc(proj_done[0].sem, 1)

            @block.scalar
            def _(scalar):
                scalar.wait_ge(turn_done[0].sem, u0 + 1)
                scalar.activation(gates[:].rearrange("p h b t -> p t (h b)"),
                                  ps[:, 4, :].rearrange("p (t n) -> p t n", t=TT)[:, :, 0:3 * HEADS],
                                  ACT.Sigmoid).then_inc(turn_ev[0].sem, 1)
                for m in range(TT):
                    scalar.wait_ge(proj_done[0].sem, p0 + m + 1)
                    scalar.activation(V2[:, m, :], ps[:, m, 0:3 * P], ACT.Copy).then_inc(raw_done[0].sem, 1)
                scalar.wait_ge(raw_done[0].sem, w0 + TT)
                scalar.wait_ge(turn_ev[0].sem, v0 + 1)
        tables.at += 5 * 16
        proj_done[0].at += TT
        raw_done[0].at += TT
        turn_done[0].at += 1
        turn_ev[0].at += 1

    def compress(F, kcT, vc):
        LP, NB = CMP_LEN // 2, CMP_BLOCKS
        w1 = work[:, 0:2 * LP * CMP_HIDDEN].rearrange("p (v l n) -> p v l n", v=2, l=LP)
        o = [0]

        def part(n):
            o[0] += n
            return hbuf[:, o[0] - n:o[0]]

        blk = part(2 * LP * 2 * NB).rearrange("p (v l c) -> p v l c", v=2, l=LP)
        pos = part(2 * LP * NB).rearrange("p (v l c) -> p v l c", v=2, l=LP)
        w2 = part(2 * 2 * HD).rearrange("p (v k n) -> p v k n", v=2, k=2)
        hid = part(2 * CMP_HIDDEN).rearrange("p (v n) -> p v n", v=2)
        hidT = part(2 * 2 * 2 * NB).rearrange("p (v k n) -> p v k n", v=2, k=2)
        t0, k0, p0, w0, u0, v0 = (c.at for c in (tables, t1_done[0], proj_done[0], raw_done[0], turn_done[0], turn_ev[0]))
        with nc.Block() as block:
            @block.sync
            def _(sync):
                sync.dma_start(pos, io["cmp_pos"]).then_inc(tables.sem, 16)
                sync.dma_start(w1, io["cmp_w1"]).then_inc(tables.sem, 16)
                sync.dma_start(w2, io["cmp_w2"]).then_inc(tables.sem, 16)

            @block.vector
            def _(vector):
                vector.wait_ge(tables.sem, t0 + 48)
                for v in range(2):
                    for g in range(2):
                        for a in range(2):
                            half = slice(a * HD, (a + 1) * HD)
                            for e in range(2):
                                src = F[half, 11 + 2 * v + g, e * CMP_STRIDE:e * CMP_STRIDE + NB * CMP_STRIDE]
                                src = src.rearrange("p (c l) -> p l c", l=CMP_STRIDE)[:, a::2, :]
                                lp = slice(e * LP // 2, (e + 1) * LP // 2)
                                vector.tensor_tensor(blk[half, v, lp, g * NB:(g + 1) * NB], src, pos[half, v, lp, :],
                                                     ALU.add).then_inc(t1_done[0].sem, 1)

            @block.tensor
            def _(pe):
                pe.wait_ge(tables.sem, t0 + 48)
                for v in range(2):
                    pe.wait_ge(t1_done[0].sem, k0 + 8 * (v + 1))
                    for l in range(LP):
                        mm = pe.matmul(ps[0:2 * NB, v, 0:CMP_HIDDEN], blk[:, v, l, :], w1[:, v, l, :],
                                       start=(l == 0), stop=(l == LP - 1))
                    mm.then_inc(proj_done[0].sem, 1)
                for v in range(2):
                    pe.wait_ge(raw_done[0].sem, w0 + v + 1)
                    for k in range(2):
                        mm = pe.transpose(ps[:, 2 + v, k * 2 * NB:(k + 1) * 2 * NB], hid[0:2 * NB, v, k * P:(k + 1) * P],
                                          ident[0:2 * NB, 0:2 * NB])
                    mm.then_inc(turn_done[0].sem, 1)
                pe.wait_ge(turn_ev[0].sem, v0 + 2)
                for g in range(2):
                    for k in range(2):
                        mm = pe.matmul(ps[g * HD:(g + 1) * HD, 4, 0:NB], w2[:, 0, k, :], hidT[:, 0, k, g * NB:(g + 1) * NB],
                                       start=(k == 0), stop=(k == 1))
                for g in range(2):
                    for k in range(2):
                        mm = pe.matmul(ps[0:NB, 5 + g, 0:HD], hidT[:, 1, k, g * NB:(g + 1) * NB], w2[:, 1, k, :],
                                       start=(k == 0), stop=(k == 1))
                mm.then_inc(proj_done[0].sem, 1)

            @block.scalar
            def _(scalar):
                for v in range(2):
                    scalar.wait_ge(proj_done[0].sem, p0 + v + 1)
                    scalar.activation(hid[0:2 * NB, v, :], ps[0:2 * NB, v, 0:CMP_HIDDEN], ACT.Silu)\
                        .then_inc(raw_done[0].sem, 1)
                for v in range(2):
                    scalar.wait_ge(turn_done[0].sem, u0 + v + 1)
                    scalar.activation(hidT[:, v, :, :], ps[:, 2 + v, 0:4 * NB].rearrange("p (k n) -> p k n", k=2),
                                      ACT.Copy).then_inc(turn_ev[0].sem, 1)
                scalar.wait_ge(proj_done[0].sem, p0 + 3)
                scalar.activation(kcT, ps[:, 4, 0:NB], ACT.Copy).then_inc(raw_done[0].sem, 1)
                scalar.activation(vc, ps[0:NB, 5:7, 0:HD], ACT.Copy).then_inc(raw_done[0].sem, 1)
                scalar.wait_ge(raw_done[0].sem, w0 + 4)
        tables.at += 48
        t1_done[0].at += 16
        proj_done[0].at += 3
        raw_done[0].at += 4
        turn_done[0].at += 2
        turn_ev[0].at += 2

    def branches(F, V2, kcT, vc, Oa, Ob):
        TT = NX // P
        TURNS = 4
        back = {1: TT, 2: NSA_WINDOW // P, 3: SWA_WINDOW // P}

        def width(br, q):
            return CMP_BLOCKS if br == 0 else (min(q, back[br]) + 1) * P

        where, total = {}, 0
        for br in range(4):
            for q in range(TT):
                where[br, q] = total
                total += width(br, q)
        S = [work[:, b * total:(b + 1) * total] for b in range(2)]
        PT = ring.buf[:, 2, 0:2 * 1280].rearrange("p (b n) -> p b n", b=2)
        turned = {1: 0, 2: 512, 3: 896, 0: 896 + 256}
        qt = qt_buf
        names = (staged, score_done, prob_done, max_done, exp_done, hstep, turn_done, turn_ev, pv_done, o_done)
        g0, s0, b0, m0, e0, h0, u0, v0, p0, o0 = ([c.at for c in cs] for cs in names)

        def tile(t, base):
            return F[:, ds(t + base, 1), :].rearrange("p a n -> p (a n)")

        def score_bank(br, q):
            n = width(br, q)
            if br == 0:
                return ps[:, 2, 384:384 + n]
            return ps[:, br - 1, 0:n]

        def keys(br, half, q):
            if br == 0:
                return kcT[half, :]
            first = (q + 1) * P - width(br, q)
            return F[half, 7 + br, first:(q + 1) * P]

        with nc.Block() as block:
            @block.gpsimd
            def _(gpsimd):
                with gpsimd.Fori(0, TURNS) as t:
                    gpsimd.wait_ge(score_done[1].sem, t * TT + s0[1])
                    gpsimd.tensor_copy(qt[:, 0, :], tile(t, 0)).then_inc(staged[0].sem, 1)
                    gpsimd.tensor_copy(qt[:, 1, :], tile(t, 4)).then_inc(staged[0].sem, 1)

            @block.tensor
            def _(pe):
                def scores(t, b, q):
                    half = slice(b * HD, (b + 1) * HD)
                    if q > 0:
                        pe.wait_ge(prob_done[b].sem, t * TT + (b0[b] + q))
                    elif b == 1:
                        pe.wait_ge(prob_done[0].sem, t * TT + (b0[0] + TT))
                    else:
                        pe.wait_ge(prob_done[1].sem, t * TT + b0[1])
                    for br in range(4):
                        mm = pe.matmul(score_bank(br, q), qt[half, br // 3, q * P:(q + 1) * P], keys(br, half, q),
                                       start=True, stop=True)
                    mm.then_inc(score_done[b].sem, 1)

                def turn(t, b, q):
                    if q > 0:
                        pe.wait_ge(turn_ev[b].sem, t * TT + (v0[b] + q))
                    elif b == 1:
                        pe.wait_ge(turn_ev[0].sem, t * TT + (v0[0] + TT))
                    else:
                        pe.wait_ge(turn_ev[1].sem, t * TT + v0[1])
                    pe.wait_ge(hstep[b].sem, t * BSTEPS + (h0[b] + BSTEPS - TT + q + 1))
                    for br in range(4):
                        n = width(br, q)
                        bank = {1: 3, 2: 4, 3: 5, 0: 5}[br]
                        c = 256 if br == 0 else 0
                        for a in range(0, n, P):
                            w = min(P, n - a)
                            src = S[b][:, where[br, q] + a:where[br, q] + a + w]
                            mm = pe.transpose(ps[0:w, bank, c + a:c + a + P], src, ident[:])
                    mm.then_inc(turn_done[b].sem, 1)

                def weigh(t, b, q):
                    half = slice(b * HD, (b + 1) * HD)
                    pe.wait_ge(turn_ev[b].sem, t * TT + (v0[b] + q + 1))
                    if q == 0:
                        pe.wait_ge(o_done[b].sem, t + o0[b])
                    cols = slice(q * P, (q + 1) * P)
                    jobs = [(6, vc[:, b, :], PT[0:CMP_BLOCKS, q % 2, turned[0]:turned[0] + P])]
                    for br in (1, 2, 3):
                        n = width(br, q) // P
                        for a in range(n):
                            jobs.append((7 if br == 3 else 6,
                                         V2[:, q + 1 - n + a, (br - 1) * P + b * HD:(br - 1) * P + (b + 1) * HD],
                                         PT[:, q % 2, turned[br] + a * P:turned[br] + (a + 1) * P]))
                    for bank in (6, 7):
                        own = [j for j in jobs if j[0] == bank]
                        for n, (_, w, p) in enumerate(own):
                            mm = pe.matmul(ps[half, bank, cols], w, p, start=(n == 0), stop=(n == len(own) - 1))
                    mm.then_inc(pv_done[b].sem, 1)

                with pe.Fori(0, TURNS) as t:
                    for b in range(2):
                        if b == 0:
                            pe.wait_ge(staged[0].sem, t * 2 + (g0[0] + 2))
                        for q in range(TT):
                            scores(t, b, q)
                    for b in range(2):
                        turn(t, b, 0)
                        for q in range(TT):
                            if q + 1 < TT:
                                turn(t, b, q + 1)
                            weigh(t, b, q)

            @block.vector
            def _(vector):
                with vector.Fori(0, TURNS) as t:
                    for b in range(2):
                        head = t + 4 * b
                        st = stat2[:, b]
                        k = [0]

                        def sstep(ins):
                            ins.then_inc(hstep[b].sem, 1)
                            k[0] += 1

                        def sdone():
                            vector.wait_ge(hstep[b].sem, t * BSTEPS + (h0[b] + k[0]))

                        vector.wait_ge(turn_done[b].sem, t * TT + u0[b])
                        for q in range(TT):
                            vector.wait_ge(score_done[b].sem, t * TT + (s0[b] + q + 1))
                            for br in range(4):
                                n = width(br, q)
                                slope = slopes[:, ds(head + (8 if br == 3 else 0), 1)]
                                if br == 0:
                                    d = dist_c[:, q, :]
                                else:
                                    end = {1: 512, 2: 896, 3: 1152}[br]
                                    d = dist[:, end - n:end]
                                ins = vector.scalar_tensor_tensor(S[b][:, where[br, q]:where[br, q] + n], d, slope,
                                                                  score_bank(br, q), ALU.mult, ALU.add)
                                sstep(ins)
                            sdone()
                            vector.sem_inc(prob_done[b].sem, 1)
                            for br in range(4):
                                n = width(br, q)
                                sstep(vector.reduce_max(st[:, 0, br * TT + q:br * TT + q + 1],
                                                        S[b][:, where[br, q]:where[br, q] + n], AX_X))
                        sdone()
                        sink = sinks[:, ds(head, 1)]
                        sstep(vector.tensor_scalar(st[:, 0, 12:16], st[:, 0, 12:16], sink, None, ALU.max))
                        sdone()
                        sstep(vector.tensor_scalar(st[:, 1, :], st[:, 0, :], -1e20, -1.0, ALU.max, ALU.mult))
                        sdone()
                        vector.sem_inc(max_done[b].sem, 1)
                        vector.wait_ge(exp_done[b].sem, t + (e0[b] + 1))
                        sstep(vector.tensor_tensor(st[:, 2, 12:16], st[:, 2, 12:16], st[:, 3, 0:4], ALU.add))
                        sdone()
                        sstep(vector.tensor_scalar(st[:, 2, :], st[:, 2, :], 1e-30, None, ALU.max))
                        sdone()
                        sstep(vector.reciprocal(st[:, 2, :], st[:, 2, :]))
                        sdone()
                        sstep(vector.tensor_tensor(st[:, 2, 0:12], st[:, 2, 0:12],
                                                   gates[:, ds(head, 1), :, :].rearrange("p a b t -> p (a b t)"), ALU.mult))
                        sdone()
                        for q in range(TT):
                            for br in range(4):
                                n = width(br, q)
                                c = S[b][:, where[br, q]:where[br, q] + n]
                                ins = vector.tensor_scalar(c, c, st[:, 2, br * TT + q:br * TT + q + 1], None, ALU.mult)
                                if br < 3:
                                    ins.then_inc(scaled_part.sem, 1)
                            ins.then_inc(scaled_part.sem, 1)
                            vector.wait_ge(scaled_part.sem, t * (8 * TT) + (c0 + 4 * TT * b + 4 * (q + 1)))
                            vector.sem_inc(hstep[b].sem, 1)
                            k[0] += 1
                        assert k[0] == BSTEPS

            @block.scalar
            def _(scalar):
                with scalar.Fori(0, TURNS) as t:
                    for b in range(2):
                        st = stat2[:, b]
                        scalar.wait_ge(max_done[b].sem, t + (m0[b] + 1))
                        for br in range(4):
                            for q in range(TT):
                                i = br * TT + q
                                c = S[b][:, where[br, q]:where[br, q] + width(br, q)]
                                scalar.activation(c, c, ACT.Exp, bias=st[:, 1, i:i + 1], accum_out=st[:, 2, i:i + 1])\
                                    .then_inc(exp_part.sem, 1)
                        scalar.activation(st[:, 3, 0:4], st[:, 1, 12:16], ACT.Exp, bias=sinks[:, ds(t + 4 * b, 1)])\
                            .then_inc(exp_part.sem, 1)
                        scalar.wait_ge(exp_part.sem, t * 34 + (x0 + 17 * (b + 1)))
                        scalar.sem_inc(exp_done[b].sem, 1)
                    for b in range(2):
                        for q in range(TT):
                            scalar.wait_ge(turn_done[b].sem, t * TT + (u0[b] + q + 1))
                            if q >= 2:
                                scalar.wait_ge(pv_done[b].sem, t * TT + (p0[b] + q - 1))
                            elif b == 1:
                                scalar.wait_ge(pv_done[0].sem, t * TT + (p0[0] + TT - 1 + q))
                            else:
                                scalar.wait_ge(pv_done[1].sem, t * TT + p0[1])
                            for n, (bank, a) in enumerate(((3, 0), (4, 512), (5, 896))):
                                wide = width(n + 1, q)
                                scalar.activation(PT[:, q % 2, a:a + wide], ps[:, bank, 0:wide], ACT.Copy)\
                                    .then_inc(ev_part.sem, 1)
                            scalar.activation(PT[0:CMP_BLOCKS, q % 2, turned[0]:turned[0] + P],
                                              ps[0:CMP_BLOCKS, 5, 256:256 + P], ACT.Copy).then_inc(ev_part.sem, 1)
                            scalar.wait_ge(ev_part.sem, t * (8 * TT) + (y0 + 4 * TT * b + 4 * (q + 1)))
                            scalar.sem_inc(turn_ev[b].sem, 1)
                        half = slice(b * HD, (b + 1) * HD)
                        scalar.wait_ge(pv_done[b].sem, t * TT + (p0[b] + TT))
                        scalar.activation(Oa[half, ds(t, 1), :].rearrange("p a n -> p (a n)"), ps[half, 6, :], ACT.Copy)\
                            .then_inc(o_part.sem, 1)
                        scalar.activation(Ob[half, ds(t, 1), :].rearrange("p a n -> p (a n)"), ps[half, 7, :], ACT.Copy)\
                            .then_inc(o_part.sem, 1)
                        scalar.wait_ge(o_part.sem, t * 4 + (z0 + 2 * (b + 1)))
                        scalar.sem_inc(o_done[b].sem, 1)
        advance(staged[:1], 2 * TURNS)
        for cs, n in zip(names[1:], (TT, TT, 1, 1, BSTEPS, TT, TT, TT, 1)):
            advance(cs, n * TURNS)

    BSTEPS = 8 * 4 + 6 + 4
    scaled_part, exp_part, ev_part, o_part = (count(n) for n in ("scaled_part", "exp_part", "turned_part", "output_part"))
    c0 = x0 = y0 = z0 = 0

    def merge(Oab, G, U, nxt):
        turns = 2
        w = io["w_ab"]
        n0 = list(ring.n)
        d0, r0 = ([c.at for c in cs] for cs in (down_done, added))
        k0 = dve_chain.at
        with nc.Block() as block:
            @block.sync
            def _(sync):
                with sync.Fori(0, turns - 1) as t:
                    for s in range(2):
                        sync.wait_ge(ring.used[s], t + (n0[s] + 1))
                        sync.dma_start(ring.buf[:, s, 0:2 * KD * P], w[ds(t * 2 + (2 + s), 1)].rearrange("a p n -> (a p) n"))\
                            .then_inc(ring.landed[s], 16)
                prefetch(sync, nxt, [n + (turns if s < 2 else 0) for s, n in enumerate(n0)])

            @block.tensor
            def _(pe):
                with pe.Fori(0, turns) as t:
                    for s in range(2):
                        wv = ring.view(s, 2, KD, P)
                        pe.wait_ge(ring.landed[s], t * 16 + 16 * (n0[s] + 1))
                        pe.wait_ge(added[s].sem, t * 2 + r0[s])
                        for j in range(2):
                            for k in range(KD):
                                mm = pe.matmul(ps[:, 4 * s + 2 * j + k // 4, :], wv[:, j, k, :], Oab[:, k, :],
                                               start=(k % 4 == 0), stop=(k % 4 == 3))
                        mm.then_inc(down_done[s].sem, 1)
                        pe.wait_ge(down_done[s].sem, t + (d0[s] + 1))
                        pe.sem_inc(ring.used[s], 1)

            @block.vector
            def _(vector):
                with vector.Fori(0, turns) as t:
                    for s in range(2):
                        vector.wait_ge(down_done[s].sem, t + (d0[s] + 1))
                        for j in range(2):
                            m = t * 4 + (2 * s + j)

                            def at(buf, i):
                                return buf[:, ds(i, 1), :].rearrange("p a n -> p (a n)")
                            k = 4 * s + 2 * j
                            vector.tensor_tensor(at(U, m), ps[:, k, :], at(G, m), ALU.mult).then_inc(dve_chain.sem, 1)
                            vector.tensor_tensor(tmp[:, 0, 0:NX], ps[:, k + 1, :], at(G, m + 8), ALU.mult)\
                                .then_inc(dve_chain.sem, 1)
                            vector.wait_ge(dve_chain.sem, t * 12 + (k0 + 6 * s + 3 * j + 2))
                            vector.tensor_tensor(at(U, m), at(U, m), tmp[:, 0, 0:NX], ALU.add).then_inc(dve_chain.sem, 1)
                            vector.wait_ge(dve_chain.sem, t * 12 + (k0 + 6 * s + 3 * j + 3))
                            vector.sem_inc(added[s].sem, 1)
        for s in range(2):
            ring.n[s] += turns
        dve_chain.at += 12 * turns
        advance(down_done, turns)
        advance(added, 2 * turns)

    def route(WT):
        TT = NX // P
        NE, NG, PER = EXPERTS, GROUPS, EXPERTS // GROUPS
        o = [0]

        def part(n):
            o[0] += n
            return work[:, o[0] - n:o[0]]

        wr = part(KD * (NG + NE)).rearrange("p (k n) -> p k n", k=KD)
        rb = part(NG + NE)
        rev = part(NE)
        L = part(TT * (NG + NE)).rearrange("p (t n) -> p t n", t=TT)
        eq = part(TT * NE).rearrange("p (t n) -> p t n", t=TT)
        em = part(TT * NE).rearrange("p (t n) -> p t n", t=TT)
        oh1 = part(TT * NE).rearrange("p (t n) -> p t n", t=TT)
        oh2 = part(TT * NE).rearrange("p (t n) -> p t n", t=TT)
        gs = part(TT * 16).rearrange("p (t n) -> p t n", t=TT)
        v = part(TT * 16).rearrange("p (t n) -> p t n", t=TT)
        t0, p0, e0, u0, v0 = (c.at for c in (tables, proj_done[0], exp_done[0], turn_done[0], turn_ev[0]))
        mark = []
        with nc.Block() as block:
            @block.sync
            def _(sync):
                sync.dma_start(wr, io["w_route"]).then_inc(tables.sem, 16)
                sync.dma_start(rb, io["b_route"]).then_inc(tables.sem, 16)
                sync.dma_start(rev, io["rev"]).then_inc(tables.sem, 16)

            @block.vector
            def _(vector):
                vector.wait_ge(tables.sem, t0 + 48)
                tiles = range(TT)

                def each(f):
                    for i in tiles:
                        step(f(i))
                    steps_done(vector)

                def first_of_max(dst, src, m, n, t2):
                    each(lambda i: vector.scalar_tensor_tensor(eq[:, i, 0:n], src(i), m(i), rev[:, NE - n:NE],
                                                               ALU.is_ge, ALU.mult))
                    each(lambda i: vector.reduce_max(t2(i), eq[:, i, 0:n], AX_X))
                    each(lambda i: vector.tensor_scalar(dst(i), eq[:, i, 0:n], t2(i), None, ALU.is_ge))

                for i in tiles:
                    vector.wait_ge(proj_done[0].sem, p0 + i + 1)
                    step(vector.tensor_tensor(L[:, i, :], ps[:, i, 0:NG + NE], rb, ALU.add))
                steps_done(vector)
                each(lambda i: vector.reduce_max(v[:, i, 0:1], L[:, i, 0:NG], AX_X))
                each(lambda i: vector.tensor_scalar(v[:, i, 1:2], v[:, i, 0:1], -1.0, None, ALU.mult))
                mark.append(dve_chain.at)
                first_of_max(lambda i: gs[:, i, 0:NG], lambda i: L[:, i, 0:NG], lambda i: v[:, i, 0:1], NG,
                             lambda i: v[:, i, 2:3])
                each(lambda i: vector.tensor_scalar(gs[:, i, NG:2 * NG], gs[:, i, 0:NG], -1.0, 1e30, ALU.add, ALU.mult))
                for g in range(NG):
                    a = slice(g * PER, (g + 1) * PER)
                    each(lambda i: vector.tensor_scalar(em[:, i, a], L[:, i, NG + g * PER:NG + (g + 1) * PER],
                                                        gs[:, i, NG + g:NG + g + 1], None, ALU.add))
                each(lambda i: vector.reduce_max(v[:, i, 3:4], em[:, i, :], AX_X))
                first_of_max(lambda i: oh1[:, i, :], lambda i: em[:, i, :], lambda i: v[:, i, 3:4], NE,
                             lambda i: v[:, i, 4:5])
                each(lambda i: vector.scalar_tensor_tensor(em[:, i, :], oh1[:, i, :], -1e30, em[:, i, :],
                                                           ALU.mult, ALU.add))
                each(lambda i: vector.reduce_max(v[:, i, 5:6], em[:, i, :], AX_X))
                first_of_max(lambda i: oh2[:, i, :], lambda i: em[:, i, :], lambda i: v[:, i, 5:6], NE,
                             lambda i: v[:, i, 6:7])
                each(lambda i: vector.tensor_tensor(v[:, i, 7:8], v[:, i, 5:6], v[:, i, 3:4], ALU.subtract))
                mark.append(dve_chain.at)
                vector.wait_ge(exp_done[0].sem, e0 + 2 * TT)
                each(lambda i: vector.tensor_scalar(v[:, i, 10:11], v[:, i, 8:9], 1.0, v[:, i, 9:10], ALU.add, ALU.mult))
                each(lambda i: vector.reciprocal(v[:, i, 11:12], v[:, i, 10:11]))
                each(lambda i: vector.tensor_tensor(v[:, i, 12:13], v[:, i, 11:12], v[:, i, 8:9], ALU.mult))
                each(lambda i: vector.tensor_scalar(oh1[:, i, :], oh1[:, i, :], v[:, i, 11:12], None, ALU.mult))
                each(lambda i: vector.scalar_tensor_tensor(oh1[:, i, :], oh2[:, i, :], v[:, i, 12:13], oh1[:, i, :],
                                                           ALU.mult, ALU.add))
                mark.append(dve_chain.at)

            @block.scalar
            def _(scalar):
                scalar.wait_ge(dve_chain.sem, mark[0])
                for i in range(TT):
                    scalar.activation(gs[:, i, 8:8 + NG], L[:, i, 0:NG], ACT.Exp, bias=v[:, i, 1:2],
                                      accum_out=v[:, i, 9:10]).then_inc(exp_done[0].sem, 1)
                scalar.wait_ge(dve_chain.sem, mark[1])
                for i in range(TT):
                    scalar.activation(v[:, i, 8:9], v[:, i, 7:8], ACT.Exp).then_inc(exp_done[0].sem, 1)
                for i in range(TT):
                    scalar.wait_ge(turn_done[0].sem, u0 + 1)
                scalar.activation(WT, ps[0:NE, 4, :], ACT.Copy).then_inc(turn_ev[0].sem, 1)
                scalar.wait_ge(turn_ev[0].sem, v0 + 1)

            @block.tensor
            def _(pe):
                pe.wait_ge(tables.sem, t0 + 48)
                for i in range(TT):
                    for k in range(KD):
                        mm = pe.matmul(ps[:, i, 0:NG + NE], h[:, k, i * P:(i + 1) * P], wr[:, k, :],
                                       start=(k == 0), stop=(k == KD - 1))
                    mm.then_inc(proj_done[0].sem, 1)
                pe.wait_ge(dve_chain.sem, mark[2])
                for i in range(TT):
                    mm = pe.transpose(ps[0:NE, 4, i * P:(i + 1) * P], oh1[:, i, :], ident[:])
                mm.then_inc(turn_done[0].sem, 1)
        tables.at += 48
        proj_done[0].at += TT
        exp_done[0].at += 2 * TT
        turn_done[0].at += 1
        turn_ev[0].at += 1

    def experts(WT, nxt):
        NE = EXPERTS
        n0 = list(ring.n)
        act = work[:, 0:2 * NX].rearrange("p (j n) -> p j n", j=2)
        sg = work[:, 2 * NX:4 * NX].rearrange("p (j n) -> p j n", j=2)
        wsel = work[0:NE, 4 * NX:5 * NX]
        names = (gu_done, silu_g, act_done, down_done, added)
        g0, s0, a0, d0, r0 = ([c.at for c in cs] for cs in names)
        w0, k0, y0 = t1_done[0].at, proj_done[0].at, t1_done[1].at
        with nc.Block() as block:
            @block.sync
            def _(sync):
                with sync.Fori(0, NE - 1) as t:
                    for s in range(3):
                        sync.wait_ge(ring.used[s], t + (n0[s] + 1))
                        sync.dma_start(ring.buf[:, s, 0:2 * KD * P],
                                       io["w_exp"][ds(t * 3 + (3 + s), 1)].rearrange("a p n -> (a p) n"))\
                            .then_inc(ring.landed[s], 16)
                prefetch(sync, nxt, [n + NE for n in n0])

            @block.tensor
            def _(pe):
                def gate_up(e, s):
                    w = ring.view(s, 2, KD, P)
                    pe.wait_ge(ring.landed[s], e * 16 + 16 * (n0[s] + 1))
                    pe.wait_ge(act_done[s].sem, e + a0[s])
                    for j in range(2):
                        for k in range(KD):
                            mm = pe.matmul(ps[:, 2 * s + j, :], w[:, j, k, :], h[:, k, 0:NX],
                                           start=(k == 0), stop=(k == KD - 1))
                    mm.then_inc(gu_done[s].sem, 1)
                    pe.wait_ge(gu_done[s].sem, e + (g0[s] + 1))
                    pe.sem_inc(ring.used[s], 1)

                def weights(e):
                    pe.wait_ge(t1_done[0].sem, e + (w0 + 1))
                    pe.wait_ge(act_done[1].sem, e + a0[1])
                    pe.matmul(ps[:, 4, :], ones[0:NE, :], wsel, start=True, stop=True).then_inc(proj_done[0].sem, 1)

                def down(e):
                    w = ring.view(2, KD, 2, P)
                    pe.wait_ge(ring.landed[2], e * 16 + 16 * (n0[2] + 1))
                    for s in range(2):
                        pe.wait_ge(act_done[s].sem, e + (a0[s] + 1))
                    for m in range(KD):
                        b = m % 2
                        if m >= 2:
                            pe.wait_ge(added[b].sem, e * 4 + (r0[b] + m // 2))
                        else:
                            pe.wait_ge(added[b].sem, e * 4 + r0[b])
                        for j in range(2):
                            mm = pe.matmul(ps[:, 5 + b, :], w[:, m, j, :], act[:, j, :], start=(j == 0), stop=(j == 1))
                        mm.then_inc(down_done[b].sem, 1)
                    pe.wait_ge(down_done[1].sem, e * 4 + (d0[1] + 4))
                    pe.sem_inc(ring.used[2], 1)

                weights(0)
                gate_up(0, 0)
                gate_up(0, 1)
                with pe.Fori(1, NE) as t:
                    weights(t)
                    gate_up(t, 0)
                    down(t - 1)
                    gate_up(t, 1)
                down(NE - 1)

            @block.scalar
            def _(scalar):
                with scalar.Fori(0, NE) as t:
                    for s in range(2):
                        scalar.wait_ge(gu_done[s].sem, t + (g0[s] + 1))
                        scalar.wait_ge(act_done[s].sem, t + a0[s])
                        scalar.activation(sg[:, s, :], ps[:, 2 * s, :], ACT.Silu).then_inc(silu_g[s].sem, 1)

            @block.vector
            def _(vector):
                def own_weights(e):
                    vector.wait_ge(proj_done[0].sem, e + k0)
                    vector.tensor_scalar(wsel, WT, ident[0:NE, ds(e, 1)], None, ALU.mult).then_inc(t1_done[0].sem, 1)

                def hidden(e, s):
                    vector.wait_ge(silu_g[s].sem, e + (s0[s] + 1))
                    vector.wait_ge(proj_done[0].sem, e + (k0 + 1))
                    vector.tensor_tensor(sg[:, s, :], sg[:, s, :], ps[:, 4, :], ALU.mult).then_inc(t1_done[1].sem, 1)
                    vector.wait_ge(t1_done[1].sem, e * 2 + (y0 + s + 1))
                    vector.tensor_tensor(act[:, s, :], sg[:, s, :], ps[:, 2 * s + 1, :], ALU.mult)\
                        .then_inc(act_done[s].sem, 1)

                def add(e):
                    for m in range(KD):
                        b = m % 2
                        vector.wait_ge(down_done[b].sem, e * 4 + (d0[b] + m // 2 + 1))
                        vector.tensor_tensor(xy[:, m, 0:NX], ps[:, 5 + b, :], xy[:, m, 0:NX], ALU.add)\
                            .then_inc(added[b].sem, 1)

                own_weights(0)
                hidden(0, 0)
                hidden(0, 1)
                with vector.Fori(1, NE) as t:
                    own_weights(t)
                    add(t - 1)
                    hidden(t, 0)
                    hidden(t, 1)
                add(NE - 1)
                for s in range(2):
                    vector.wait_ge(added[s].sem, r0[s] + 4 * NE)
        for s in range(3):
            ring.n[s] += NE
        for cs, n in zip(names, (1, 1, 1, 4, 4)):
            advance(cs, n * NE)
        t1_done[0].at += NE
        t1_done[1].at += 2 * NE
        proj_done[0].at += NE

    def two(w, a=0):
        return [(s, w[a + s]) for s in range(2)]

    def chunk(j):
        return mods[:, j * KD:(j + 1) * KD, :]

    start(first_mod(0))
    modulation(0, first_gu("ffn1", 0))
    norm(NT, modA[:, 0], chunk(0))
    feed_forward("ffn1", 0, NT, chunk(2), two(io["w_qk"]))
    attention_tables()
    norm(NT, modA[:, 1], chunk(3))
    Qh = big[:, 0:HEADS * NX].rearrange("p (a n) -> p a n", a=HEADS)
    Kh = big[:, HEADS * NX:HEADS * (NX + NT)].rearrange("p (a n) -> p a n", a=HEADS)
    Vh = big[:, HEADS * (NX + NT):HEADS * (NX + NT) + KT * D].rearrange("p (m n) -> p m n", m=KT)
    Oh = hbuf[:, 0:HEADS * NX].rearrange("p (a n) -> p a n", a=HEADS)
    head_inputs(0, Qh, two(io["w_qk"], 4))
    head_inputs(1, Kh, two(io["w_v"]))
    values(Vh, two(io["w_o"]))
    attention(Qh, Kh, Vh, Oh)
    output_norm(Oh, subg[:, 1:2])
    project_residual(io["w_o"], Oh, chunk(5), first_gu("ffn2", 0))
    norm(NX, modA[:, 2], chunk(6))
    feed_forward("ffn2", 0, NX, chunk(8), first_mod(1))
    modulation(1, first_gu("ffn1", 1))
    norm(NX, modA[:, 0], chunk(0))
    feed_forward("ffn1", 1, NX, chunk(2), two(io["w_f"]))
    norm(NX, modA[:, 1], chunk(3))
    F = work[:, 0:KD * NX].rearrange("p (k n) -> p k n", k=KD)
    fourier(F)
    project_residual(io["w_f"], F, chunk(5), first_gu("ffn2", 1))
    norm(NX, modA[:, 2], chunk(6))
    feed_forward("ffn2", 1, NX, chunk(8), two(io["w_in"]))
    second_gains()
    norm(NX, gains2[:, 0], None)
    F = big[:, 0:16 * NX].rearrange("p (k n) -> p k n", k=16)
    G = big[:, 16 * NX:32 * NX].rearrange("p (k n) -> p k n", k=16)
    V2 = rope[:].rearrange("p a n -> p (a n)")[:, 0:12 * P].rearrange("p (t n) -> p t n", t=4)
    project(io["w_in"], 0, 2, F[:, 0:8], HD ** -0.5, ACT.Copy, two(io["w_in"], 4))
    project(io["w_in"], 4, 2, F[:, 8:16], 1.0, ACT.Copy, two(io["w_in"], 8))
    project(io["w_in"], 8, 4, G, 1.0, ACT.Sigmoid, two(io["w_ab"]))
    values_and_gates(F, V2)
    compress(F, kc_sb[:], vc_sb[:])
    Oab = hbuf[:, 0:KD * NX].rearrange("p (k n) -> p k n", k=KD)
    qt_buf = hbuf[:, KD * NX:(KD + 2) * NX].rearrange("p (a n) -> p a n", a=2)
    branches(F, V2, kc_sb[:], vc_sb[:], Oab[:, 0:4], Oab[:, 4:8])
    U = work[:, 0:KD * NX].rearrange("p (k n) -> p k n", k=KD)
    merge(Oab, G, U, two(io["w_o2"]))
    project_residual(io["w_o2"], U, None, [(s, io["w_exp"][s]) for s in range(3)])
    norm(NX, gains2[:, 1], None)
    WT = big[0:EXPERTS, 0:NX]
    route(WT)
    experts(WT, [])
    norm(NX, gains2[:, 2], None)
    finish(h[:, :, 0:NX], io["out"])


def slabs(w, per):
    k, m = w.shape
    w = w.reshape(k // P, P, m // P // per, per, P)
    return np.ascontiguousarray(w.transpose(2, 1, 3, 0, 4)).reshape(m // P // per, P, per * k)


def columns(v):
    v = v.reshape(v.shape[:-1] + (-1, P))
    return np.ascontiguousarray(np.moveaxis(v, -1, 0))


def layouts(a):
    L = {}
    n = np.arange(P)
    L["bones"] = (n[:, None] // HD == n[None, :] // HD).astype(np.float32)
    L["ident"] = np.eye(P, dtype=np.float32)
    L["lam"] = np.broadcast_to(np.stack([a["attn_lam_" + i][0] for i in ("q1", "k1", "q2", "k2")]), (P, 4, HD))
    L["qk_gain"] = np.stack([np.tile(a["attn_" + i + "_g"][0], 2) for i in "qk"], axis=1)
    L["sub_gain"] = a["attn_sub_g"][0][:, None]
    pairs = HD // 4
    inv_freq = np.float32(10000.0) ** (-(np.arange(pairs, dtype=np.float32) / pairs))
    tok = np.arange(NX)
    place = np.stack([tok // 64, tok % 64]).astype(np.float32)
    angle = (place[(n % HD) // 32] * inv_freq[n % pairs][:, None]).astype(np.float32)
    L["rope"] = np.stack([np.cos(angle), np.sin(angle)], axis=1).astype(np.float32)
    r = np.zeros((P, P), np.float32)
    for p in range(P):
        if (p // pairs) % 2:
            r[p, p - pairs] = -1.0
        else:
            r[p, p + pairs] = 1.0
    L["rot"] = r
    qkv = a["attn_w_qkv"][0]
    L["w_qk"] = slabs(qkv[:, 0:2 * D], 2)
    L["w_v"] = np.ascontiguousarray(qkv[:, 2 * D:].reshape(KD, P, 4, 2 * P).transpose(2, 1, 0, 3)).reshape(4, P, -1)
    L["w_o"] = slabs(a["attn_w_o"][0], 2)
    L["w_f"] = slabs(a["fourier_w"][0], 2)
    W = D // 4
    f, t = np.arange(W), np.arange(NX)
    af, at = 2 * np.pi * (np.outer(f, f) % W) / W, 2 * np.pi * (np.outer(t, t) % NX) / NX
    L["dft_feature"] = (np.concatenate([np.cos(af), np.sin(af)], 1) / np.sqrt(W)).astype(np.float32)\
        .reshape(2, P, 2 * W).transpose(1, 0, 2)
    L["dft_token"] = (np.stack([np.cos(at), -np.sin(at)]) / np.sqrt(NX)).astype(np.float32)\
        .reshape(2, NX // P, P, NX).transpose(2, 0, 1, 3)
    L["gains2"] = np.stack([columns(a[k].reshape(D)) for k in ("norm_mix_g_2", "norm_ffn_g_2", "norm_final_g_2")],
                           axis=1)[..., None]
    w = a["w_in_2"][0]
    edges = np.cumsum([0, 512, 128, 128, 128, 128, 128, 128, 24, 512, 128, 128, 2048])
    qa, kcmp, vcmp, kslc, vslc, kwin, vwin, gn, qb, kb, vb, gm = (w[:, x:y] for x, y in zip(edges[:-1], edges[1:]))

    def paired(m):
        return m.reshape(-1, 2, 4, HD).transpose(0, 2, 1, 3).reshape(-1, 8 * HD)

    def doubled(m):
        return np.repeat(m.reshape(-1, 2, 1, HD), 2, axis=2).reshape(-1, 4 * HD)

    pad = np.zeros((D, P - gn.shape[1]), np.float32)
    L["w_in"] = slabs(np.concatenate([paired(qa), paired(qb), kslc, kwin, kb, doubled(kcmp), doubled(vcmp), gn, pad, gm],
                                     axis=1), 2)
    L["w_v2"] = np.concatenate([vslc, vwin, vb], axis=1).reshape(KD, P, 3 * P).transpose(1, 0, 2)
    L["w_ab"] = slabs(np.concatenate([paired(a[k][0].T).T for k in ("w_a_2", "w_b_2")], axis=0), 2)
    L["w_o2"] = slabs(a["w_o_2"][0], 2)
    LP = CMP_LEN // 2
    L["cmp_w1"] = np.stack([a[f"cmp_w1_{v}_2"][0].reshape(LP, P, CMP_HIDDEN).transpose(1, 0, 2) for v in "kv"], axis=1)
    L["cmp_w2"] = np.stack([a[f"cmp_w2_{v}_2"][0].reshape(2, P, HD).transpose(1, 0, 2) for v in "kv"], axis=1)
    pos = np.stack([a[f"cmp_pos_{v}_2"][0].reshape(LP, P).T for v in "kv"], axis=1)
    L["cmp_pos"] = np.repeat(pos[..., None], CMP_BLOCKS, axis=3)
    p = np.arange(P)[:, None]

    def distances(before, window):
        d = before + p - np.arange(before + P)[None, :]
        return np.where((d >= 0) & (d < window), d, 1e35)

    L["dist"] = np.concatenate([distances(NX - P, NX), distances(NSA_WINDOW, NSA_WINDOW),
                                distances(SWA_WINDOW, SWA_WINDOW)], axis=1).astype(np.float32)
    end = np.arange(CMP_BLOCKS) * CMP_STRIDE + CMP_LEN - 1
    dc = (np.arange(4)[None, :, None] * P + p[:, :, None]) - end
    L["dist_cmp"] = np.where(dc >= 0, dc, 1e35).astype(np.float32)
    slope = 2.0 ** (-8.0 * np.arange(1, 17) / 16)
    L["slopes"] = np.broadcast_to(-np.concatenate([slope[8:], slope[:8]]).astype(np.float32), (P, 16))
    L["sinks"] = np.broadcast_to(a["sinks_2"][0], (P, 8))
    L["w_route"] = np.concatenate([a["w_group_2"][0], a["w_expert_2"][0]], axis=1).reshape(KD, P, -1).transpose(1, 0, 2)
    L["b_route"] = np.broadcast_to(np.concatenate([a["b_group_2"][0], a["b_expert_2"][0]]), (P, GROUPS + EXPERTS))
    L["rev"] = np.broadcast_to(np.arange(EXPERTS, 0, -1, dtype=np.float32), (P, EXPERTS))
    FE = 2
    gu = np.stack([a["w_gate_e_2"][0], a["w_up_e_2"][0]], axis=1)
    gu = gu.reshape(EXPERTS, 2, KD, P, FE, P).transpose(0, 4, 3, 1, 2, 5).reshape(EXPERTS, FE, P, 2 * KD * P)
    dn = a["w_down_e_2"][0].reshape(EXPERTS, FE, P, KD, P).transpose(0, 2, 3, 1, 4).reshape(EXPERTS, 1, P, 2 * KD * P)
    L["w_exp"] = np.concatenate([gu, dn], axis=1).reshape(3 * EXPERTS, P, 2 * KD * P)
    cols = np.concatenate([a["x"][0], a["ctx"][0]]).T
    L["xy"] = cols.reshape(KD, P, NT).transpose(1, 0, 2)
    L["cond"] = np.stack([a["c"][0], a["c_ctx"]]).reshape(2, KD, P).transpose(2, 1, 0)
    L["w_mod"] = np.stack([slabs(w, 2) for w in a["w_mod"]])
    b = a["b_mod"].reshape(2, NMOD * KD, P).transpose(0, 2, 1)
    L["b_mod"] = np.repeat(b[..., None], 2, axis=3)
    g = a["norm_g"].reshape(2, 3 * KD, P).transpose(0, 2, 1)
    L["norm_g"] = np.repeat(g[..., None], 2, axis=3)
    for n in ("ffn1", "ffn2"):
        gu = a[n + "_w_gu"].reshape(2, KD, P, 2, KF, P)
        L[n + "_gu"] = np.ascontiguousarray(gu.transpose(0, 4, 2, 3, 1, 5)).reshape(2, KF, P, 2 * KD * P)
        L[n + "_d"] = np.stack([slabs(w, 1) for w in a[n + "_w_d"]])
    return L


def kernel(**inputs):
    import concourse.bacc as bacc
    from concourse.bass_utils import run_bass_kernel_spmd

    nc = bacc.Bacc("TRN2", target_bir_lowering=False, num_devices=1)
    arrays, io = {}, {}
    for name, a in layouts({k: np.asarray(v) for k, v in inputs.items()}).items():
        arrays[f"in_{name}"] = np.ascontiguousarray(a)
        io[name] = nc.dram_tensor(f"in_{name}", a.shape, F32, kind="ExternalInput").ap()
    io["out"] = nc.dram_tensor("out", (P, KD, NX), F32, kind="ExternalOutput").ap()
    program(nc, io)
    r = run_bass_kernel_spmd(nc, [arrays], core_ids=[0])
    return r.results[0]["out"].transpose(2, 1, 0).reshape(1, NX, D)
```

```python
from contextlib import ExitStack

import numpy as np

import concourse.bass as bass
from concourse import mybir

F32 = mybir.dt.float32
ALU = mybir.AluOpType
ACT = mybir.ActivationFunctionType
AX_X = mybir.AxisListType.X
ds = bass.ds

P = 128
D = 1024
KD = D // P
NX = 512
NY = 256
NT = NX + NY
FF = 2816
KF = FF // P
NMOD = 9
EPS = 1e-6
CMP_LEN, CMP_STRIDE, CMP_HIDDEN = 32, 16, 256
CMP_BLOCKS = NX // CMP_STRIDE - CMP_LEN // CMP_STRIDE + 1
NSA_WINDOW, SWA_WINDOW = 256, 128
EXPERTS, GROUPS = 32, 4
MOE_BLOCKS = EXPERTS + 2 * NX // P - 1
HEADS = 8
HD = 64
KT = NT // P
LAMBDA_INIT = 0.2
SLOTS = 3
SLOT = KF * P


class Count:

    def __init__(self, ctx, nc, name):
        self.sem = ctx.enter_context(nc.semaphore(name))
        self.at = 0


class Ring:

    def __init__(self, ctx, nc):
        self.buf = ctx.enter_context(nc.sbuf_tensor("weights", [P, SLOTS, SLOT], F32))
        self.landed = [ctx.enter_context(nc.semaphore(f"slab_landed{s}")) for s in range(SLOTS)]
        self.used = [ctx.enter_context(nc.semaphore(f"slab_used{s}")) for s in range(SLOTS)]
        self.n = [0] * SLOTS

    def view(self, s, *dims):
        size = int(np.prod(dims))
        names = "abcd"[:len(dims)]
        flat = self.buf[:, s, 0:size]
        if len(dims) == 1:
            return flat
        return flat.rearrange(f"p ({' '.join(names)}) -> p {' '.join(names)}",
                              **{a: n for a, n in zip(names, dims)})


def program(nc, io):
    with ExitStack() as ctx:
        build(nc, io, ctx)


def build(nc, io, ctx):
    def sb(name, shape):
        return ctx.enter_context(nc.sbuf_tensor(name, shape, F32))

    def count(name):
        return Count(ctx, nc, name)

    ring = Ring(ctx, nc)
    ps = ctx.enter_context(nc.psum_tensor("ps", [P, 8, 512], F32))

    xy = sb("xy", [P, KD, NT])
    hbuf = sb("hbuf", [P, KD * NT])
    h = hbuf[:].rearrange("p (k n) -> p k n", k=KD)
    big = sb("big", [P, KF * NT])
    ones = sb("ones", [P, P])
    eps = sb("eps", [P, 1])
    cond = sb("cond", [P, KD, 2])
    scond = sb("scond", [P, KD, 2])
    mods = sb("mods", [P, NMOD * KD, 2])
    bmod = sb("bmod", [P, NMOD * KD, 2])
    normg = sb("normg", [P, 3 * KD, 2])
    modA = sb("modA", [P, 3, KD, 2])
    rstd = sb("rstd", [P, NT])
    tmp = sb("tmp", [P, 2, NT])

    work = sb("work", [P, 12 * NT])
    bones = sb("bones", [P, P])
    ident = sb("ident", [P, P])
    rope = sb("rope", [P, 4, NX])
    rot = sb("rot", [P, 3, P])
    qkg = sb("qkg", [P, 2])
    lamv = work[:, 0:4 * HD].rearrange("p (a n) -> p a n", a=4)
    lamt = sb("lamt", [P, 8])
    subg = sb("subg", [P, 2])
    stat = sb("stat", [P, 2, 8])
    gains2 = sb("gains2", [P, 3, KD, 1])
    dist = tmp[:].rearrange("p a n -> p (a n)")[:, 0:1152]
    dist_c = sb("dist_c", [P, 4, CMP_BLOCKS])
    slopes = sb("slopes", [P, 16])
    sinks = sb("sinks", [P, 8])
    gates = sb("gates", [P, HEADS, 3, 4])
    stat2 = sb("stat2", [P, 2, 4, 16])
    kc_sb = sb("kc", [P, CMP_BLOCKS])
    vc_sb = sb("vc", [CMP_BLOCKS, 2, HD])

    dest = ctx.enter_context(nc.sbuf_tensor("dest", [P, 2 * NX // P], mybir.dt.uint32))
    share = sb("share", [P, 2, NX // P])
    block_expert = ctx.enter_context(nc.sbuf_tensor("block_expert", [1, MOE_BLOCKS + 1], mybir.dt.int32))

    def wset(s):
        if s == 0:
            return ring.buf[:, :, 0:2 * KD * P]
        return big[:, 4 * D + (s - 1) * 6 * D:4 * D + s * 6 * D].rearrange("p (a n) -> p a n", a=3)

    def xin(s):
        return work[:, 6 * D + s * D:7 * D + s * D]

    loaded = count("inputs_loaded")
    tables = count("tables_landed")
    proj_done = [count(f"head_product{s}") for s in range(2)]
    raw_done = [count(f"head_copied{s}") for s in range(2)]
    hss_done = [count(f"head_square_sums{s}") for s in range(2)]
    hroot = [count(f"head_roots{s}") for s in range(2)]
    t1_done = [count(f"rope_cos_part{s}") for s in range(2)]
    head_done = [count(f"head_normalised{s}") for s in range(2)]
    staged = [count(f"head_staged{s}") for s in range(2)]
    score_done = [count(f"scores{s}") for s in range(2)]
    max_done = [count(f"score_max{s}") for s in range(2)]
    exp_done = [count(f"exponentials{s}") for s in range(2)]
    prob_done = [count(f"probabilities{s}") for s in range(2)]
    turn_done = [count(f"turned{s}") for s in range(2)]
    turn_ev = [count(f"turned_copied{s}") for s in range(2)]
    pv_done = [count(f"values_product{s}") for s in range(2)]
    o_done = [count(f"output_copied{s}") for s in range(2)]
    const_set = count("constants_set")
    silu_done = count("condition_silu")
    mod_mm = [count(f"mod_product{s}") for s in range(SLOTS)]
    mod_ev = [count(f"mod_stored{s}") for s in range(SLOTS)]
    small_landed = count("mod_tables_landed")
    dve_chain = count("vector_step")
    sq_done = count("squares")
    ss_done = count("square_sums")
    root_done = count("roots")
    rstd_done = count("inverse_roots")
    scaled = count("scaled")
    shifted = count("shifted")
    gu_done = [count(f"gate_up_product{s}") for s in range(2)]
    silu_g = [count(f"gate_silu{s}") for s in range(2)]
    act_done = [count(f"hidden{s}") for s in range(2)]
    down_done = [count(f"down_product{s}") for s in range(2)]
    added = [count(f"residual_added{s}") for s in range(2)]
    out_done = count("out_stored")
    zeroed = count("slots_zeroed")
    counted = count("assignments_counted")
    scattered = count("tokens_scattered")
    gathered = [count(f"results_gathered{i}") for i in range(NX // P)]
    x_landed = [count(f"block_rows_landed{s}") for s in range(3)]
    set_landed = [count(f"expert_weights_landed{s}") for s in range(3)]
    rows_turned = count("block_rows_turned")
    rows_by_act = count("block_rows_copied_by_scalar")
    rows_by_vec = count("block_rows_copied_by_vector")
    hidden_mm = count("expert_gate_and_up_products")
    gate_done = count("expert_gate_silu")
    hidden_done = count("expert_hidden")
    y_mm = count("expert_down_products")
    y_by_act = count("block_result_copied_by_scalar")
    y_by_vec = count("block_result_copied_by_vector")
    y_stored = [count(f"block_result_stored{s}") for s in range(3)]
    room = count("staging_room_found")

    def step(ins):
        ins.then_inc(dve_chain.sem, 1)
        dve_chain.at += 1

    def steps_done(eng):
        eng.wait_ge(dve_chain.sem, dve_chain.at)

    def prefetch(sync, first, used):
        for s, src in first:
            sync.wait_ge(ring.used[s], used[s])
            sync.dma_start(ring.buf[:, s, 0:src.shape[1]], src).then_inc(ring.landed[s], 16)

    def first_mod(i):
        return [(s, io["w_mod"][i, s]) for s in range(3)]

    def first_gu(name, i):
        return [(s, io[name + "_gu"][i, s]) for s in range(2)]

    def open_counts(eng, counts):
        for c in counts:
            eng.sem_inc(c.sem, 1)
            c.at = 1

    def start(nxt):
        with nc.Block() as block:
            @block.sync
            def _(sync):
                prefetch(sync, nxt, ring.n)
                sync.dma_start(cond[:], io["cond"]).then_inc(loaded.sem, 16)
                sync.dma_start(xy[:], io["xy"]).then_inc(loaded.sem, 16)

            @block.gpsimd
            def _(gpsimd):
                n = MOE_BLOCKS * D // 3
                gpsimd.memset(big[:, 0:n], 0.0).then_inc(const_set.sem, 1)
                gpsimd.wait_ge(const_set.sem, 3)
                for j in range(3):
                    rows = io["slots"][j * (MOE_BLOCKS // 3) * P:(j + 1) * (MOE_BLOCKS // 3) * P, :]
                    gpsimd.dma_start(rows.rearrange("(p a) n -> p (a n)", p=P), big[:, 0:n]).then_inc(zeroed.sem, 16)

            @block.tensor
            def _(pe):
                open_counts(pe, pv_done + turn_done + proj_done + score_done)

            @block.vector
            def _(vector):
                open_counts(vector, [rows_by_act, rows_by_vec, y_by_act, y_by_vec] + y_stored)
                open_counts(vector, mod_ev + act_done + added + head_done + prob_done + o_done)
                vector.memset(ones[:], 1.0).then_inc(const_set.sem, 1)
                vector.memset(eps[:], EPS).then_inc(const_set.sem, 1)

            @block.scalar
            def _(scalar):
                open_counts(scalar, raw_done + exp_done + turn_ev)
                scalar.wait_ge(loaded.sem, 32)
                scalar.activation(scond[:], cond[:], ACT.Silu).then_inc(silu_done.sem, 1)
        loaded.at = 32

    def slots_zeroed():
        with nc.Block() as block:
            @block.sync
            def _(sync):
                sync.wait_ge(zeroed.sem, 48)

    def modulation(i, nxt):
        turns = NMOD * KD // 2 // SLOTS
        n0 = list(ring.n)
        m0 = [c.at for c in mod_mm]
        e0 = [c.at for c in mod_ev]
        t0 = small_landed.at
        with nc.Block() as block:
            @block.sync
            def _(sync):
                sync.dma_start(bmod[:], io["b_mod"][i]).then_inc(small_landed.sem, 16)
                sync.dma_start(normg[:], io["norm_g"][i]).then_inc(small_landed.sem, 16)
                with sync.Fori(0, turns - 1) as t:
                    for s in range(SLOTS):
                        sync.wait_ge(ring.used[s], t + (n0[s] + 1))
                        sync.dma_start(ring.buf[:, s, 0:2 * KD * P],
                                       io["w_mod"][i, ds(t * SLOTS + (SLOTS + s), 1)].rearrange("a p n -> (a p) n"))\
                            .then_inc(ring.landed[s], 16)
                prefetch(sync, nxt, [n + turns for n in n0])

            @block.tensor
            def _(pe):
                pe.wait_ge(silu_done.sem, 1)
                with pe.Fori(0, turns) as t:
                    for s in range(SLOTS):
                        w = ring.view(s, 2, KD, P)
                        pe.wait_ge(ring.landed[s], t * 16 + 16 * (n0[s] + 1))
                        pe.wait_ge(mod_ev[s].sem, t + e0[s])
                        for j in range(2):
                            for k in range(KD):
                                mm = pe.matmul(ps[:, s, 2 * j:2 * j + 2], w[:, j, k, :], scond[:, k, :],
                                               start=(k == 0), stop=(k == KD - 1))
                        mm.then_inc(mod_mm[s].sem, 1)
                        pe.wait_ge(mod_mm[s].sem, t + (m0[s] + 1))
                        pe.sem_inc(ring.used[s], 1)

            @block.vector
            def _(vector):
                vector.wait_ge(small_landed.sem, t0 + 32)
                with vector.Fori(0, turns) as t:
                    for s in range(SLOTS):
                        at = ds(t * (2 * SLOTS) + 2 * s, 2)
                        vector.wait_ge(mod_mm[s].sem, t + (m0[s] + 1))
                        vector.tensor_tensor(mods[:, at, :], ps[:, s, 0:4].rearrange("p (a b) -> p a b", a=2),
                                             bmod[:, at, :], ALU.add).then_inc(mod_ev[s].sem, 1)
                for s in range(SLOTS):
                    vector.wait_ge(mod_ev[s].sem, e0[s] + turns)
                for j in range(3):
                    a = (3 * j + 1) * KD
                    step(vector.scalar_tensor_tensor(modA[:, j], mods[:, a:a + KD, :], 1.0,
                                                     normg[:, j * KD:(j + 1) * KD, :], ALU.add, ALU.mult))
                for j in (2, 8):
                    step(vector.tensor_scalar(mods[:, j * KD:(j + 1) * KD, :], mods[:, j * KD:(j + 1) * KD, :],
                                              0.5, None, ALU.mult))
                steps_done(vector)
        for s in range(SLOTS):
            ring.n[s] += turns
            mod_mm[s].at += turns
            mod_ev[s].at += turns
        small_landed.at += 32

    def norm(cols, gain, shift):
        s0, q0, r0, i0, c0, f0 = (c.at for c in (sq_done, ss_done, root_done, rstd_done, scaled, shifted))
        sq = big[:, 0:KD * NT].rearrange("p (k n) -> p k n", k=KD)
        parts = [(0, NX, 0), (NX, NY, 1)][:1 if cols == NX else 2]
        with nc.Block() as block:
            @block.scalar
            def _(scalar):
                for k in range(KD):
                    scalar.activation(sq[:, k, 0:cols], xy[:, k, 0:cols], ACT.Square).then_inc(sq_done.sem, 1)
                scalar.wait_ge(ss_done.sem, q0 + 1)
                for a, n, c in parts:
                    scalar.activation(tmp[:, 0, a:a + n], ps[:, c, 0:n], ACT.Sqrt, bias=eps[:, 0:1],
                                      scale=1.0 / D).then_inc(root_done.sem, 1)
                if shift is not None:
                    for k in range(KD):
                        for a, n, c in parts:
                            scalar.wait_ge(scaled.sem, c0 + k * len(parts) + c + 1)
                            scalar.activation(h[:, k, a:a + n], h[:, k, a:a + n], ACT.Identity,
                                              bias=shift[:, k, c:c + 1]).then_inc(shifted.sem, 1)
                    scalar.wait_ge(shifted.sem, f0 + KD * len(parts))

            @block.tensor
            def _(pe):
                pe.wait_ge(const_set.sem, 3)
                for k in range(KD):
                    pe.wait_ge(sq_done.sem, s0 + k + 1)
                    for a, n, c in parts:
                        mm = pe.matmul(ps[:, c, 0:n], ones[:], sq[:, k, a:a + n],
                                       start=(k == 0), stop=(k == KD - 1))
                mm.then_inc(ss_done.sem, 1)

            @block.vector
            def _(vector):
                vector.wait_ge(root_done.sem, r0 + len(parts))
                vector.reciprocal(rstd[:, 0:cols], tmp[:, 0, 0:cols]).then_inc(rstd_done.sem, 1)
                vector.wait_ge(rstd_done.sem, i0 + 1)
                for k in range(KD):
                    for a, n, c in parts:
                        vector.scalar_tensor_tensor(h[:, k, a:a + n], xy[:, k, a:a + n], gain[:, k, c:c + 1],
                                                    rstd[:, a:a + n], ALU.mult, ALU.mult)\
                            .then_inc(scaled.sem, 1)
                vector.wait_ge(scaled.sem, c0 + KD * len(parts))
        sq_done.at += KD
        ss_done.at += 1
        root_done.at += len(parts)
        rstd_done.at += 1
        scaled.at += KD * len(parts)
        if shift is not None:
            shifted.at += KD * len(parts)

    def feed_forward(name, i, cols, gate, nxt):
        act = big[:].rearrange("p (f n) -> p f n", f=KF)
        parts = [(0, NX), (NX, NY)][:1 if cols == NX else 2]
        wgu, wd = io[name + "_gu"], io[name + "_d"]
        turns, dturns = KF // 2, KD // 2
        n0 = list(ring.n)
        g0, s0, a0, d0, r0 = ([c.at for c in cs] for cs in (gu_done, silu_g, act_done, down_done, added))

        def gate_up(s, j, a, n):
            return ps[:, 3 * s + j, 0:n] if a == 0 else ps[:, 3 * s + 2, j * NY:(j + 1) * NY]

        with nc.Block() as block:
            @block.sync
            def _(sync):
                with sync.Fori(0, turns - 1) as t:
                    for s in range(2):
                        sync.wait_ge(ring.used[s], t + (n0[s] + 1))
                        sync.dma_start(ring.buf[:, s, 0:2 * KD * P],
                                       wgu[i, ds(t * 2 + (2 + s), 1)].rearrange("a p n -> (a p) n"))\
                            .then_inc(ring.landed[s], 16)
                prefetch(sync, [(s, wd[i, s]) for s in range(2)], [n + turns for n in n0])
                with sync.Fori(0, dturns - 1) as t:
                    for s in range(2):
                        sync.wait_ge(ring.used[s], t + (n0[s] + turns + 1))
                        sync.dma_start(ring.buf[:, s, :], wd[i, ds(t * 2 + (2 + s), 1)].rearrange("a p n -> (a p) n"))\
                            .then_inc(ring.landed[s], 16)
                prefetch(sync, nxt, [n + (turns + dturns if s < 2 else 0) for s, n in enumerate(n0)])

            @block.tensor
            def _(pe):
                with pe.Fori(0, turns) as t:
                    for s in range(2):
                        w = ring.view(s, 2, KD, P)
                        pe.wait_ge(ring.landed[s], t * 16 + 16 * (n0[s] + 1))
                        pe.wait_ge(act_done[s].sem, t * len(parts) + a0[s])
                        for j in range(2):
                            for a, n in parts:
                                for k in range(KD):
                                    mm = pe.matmul(gate_up(s, j, a, n), w[:, j, k, :], h[:, k, a:a + n],
                                                   start=(k == 0), stop=(k == KD - 1))
                        mm.then_inc(gu_done[s].sem, 1)
                        pe.wait_ge(gu_done[s].sem, t + (g0[s] + 1))
                        pe.sem_inc(ring.used[s], 1)
                for s in range(2):
                    pe.wait_ge(act_done[s].sem, a0[s] + turns * len(parts))
                with pe.Fori(0, dturns) as t:
                    for s in range(2):
                        w = ring.view(s, KF, P)
                        pe.wait_ge(ring.landed[s], t * 16 + 16 * (n0[s] + turns + 1))
                        pe.wait_ge(added[s].sem, t * len(parts) + r0[s])
                        for c, (a, n) in enumerate(parts):
                            for f in range(KF):
                                mm = pe.matmul(ps[:, 3 * s + c, 0:n], w[:, f, :], act[:, f, a:a + n],
                                               start=(f == 0), stop=(f == KF - 1))
                        mm.then_inc(down_done[s].sem, 1)
                        pe.wait_ge(down_done[s].sem, t + (d0[s] + 1))
                        pe.sem_inc(ring.used[s], 1)

            @block.scalar
            def _(scalar):
                with scalar.Fori(0, turns) as t:
                    for s in range(2):
                        scalar.wait_ge(gu_done[s].sem, t + (g0[s] + 1))
                        scalar.wait_ge(act_done[s].sem, t * len(parts) + a0[s])
                        for a, n in parts:
                            scalar.activation(tmp[:, s, a:a + n], gate_up(s, 0, a, n), ACT.Silu)\
                                .then_inc(silu_g[s].sem, 1)

            @block.vector
            def _(vector):
                with vector.Fori(0, turns) as t:
                    for s in range(2):
                        for c, (a, n) in enumerate(parts):
                            vector.wait_ge(silu_g[s].sem, t * len(parts) + (s0[s] + c + 1))
                            vector.tensor_tensor(act[:, ds(t * 2 + s, 1), a:a + n].rearrange("p a n -> p (a n)"),
                                                 gate_up(s, 1, a, n), tmp[:, s, a:a + n], ALU.mult)\
                                .then_inc(act_done[s].sem, 1)
                with vector.Fori(0, dturns) as t:
                    for s in range(2):
                        vector.wait_ge(down_done[s].sem, t + (d0[s] + 1))
                        for c, (a, n) in enumerate(parts):
                            x = xy[:, ds(t * 2 + s, 1), a:a + n].rearrange("p a n -> p (a n)")
                            g = gate[:, ds(t * 2 + s, 1), c:c + 1].rearrange("p a n -> p (a n)")
                            vector.scalar_tensor_tensor(x, ps[:, 3 * s + c, 0:n], g, x, ALU.mult, ALU.add)\
                                .then_inc(added[s].sem, 1)
                for s in range(2):
                    vector.wait_ge(added[s].sem, r0[s] + dturns * len(parts))
        for s in range(2):
            ring.n[s] += turns + dturns
            gu_done[s].at += turns
            silu_g[s].at += turns * len(parts)
            act_done[s].at += turns * len(parts)
            down_done[s].at += dturns
            added[s].at += dturns * len(parts)

    def finish(src, dst):
        o0 = out_done.at
        with nc.Block() as block:
            @block.sync
            def _(sync):
                sync.dma_start(dst, src).then_inc(out_done.sem, 16)
                sync.wait_ge(out_done.sem, o0 + 16)
        out_done.at += 16

    def own_rows(c):
        return bones[:, c * HD:c * HD + 1].to_broadcast([P, NX])

    def advance(counts, n):
        for c in counts:
            c.at += n

    def attention_tables():
        t0, e0 = tables.at, exp_done[0].at
        with nc.Block() as block:
            @block.sync
            def _(sync):
                for dst, name in ((bones[:], "bones"), (ident[:], "ident"), (lamv, "lam"), (qkg[:], "qk_gain"),
                                  (subg[:, 0:1], "sub_gain"), (rope[:, 0:2], "rope"), (rot[:, 0], "rot")):
                    sync.dma_start(dst, io[name]).then_inc(tables.sem, 16)

            @block.vector
            def _(vector):
                vector.wait_ge(tables.sem, t0 + 16 * 7)
                for j in range(2):
                    step(vector.tensor_scalar(rope[:, 2 + j, :], rope[:, 0, :], qkg[:, j:j + 1], None, ALU.mult))
                    step(vector.tensor_scalar(rot[:, 1 + j, :], rot[:, 0, :], qkg[:, j:j + 1], None, ALU.mult))
                    step(vector.tensor_tensor(lamv[:, 2 * j, :], lamv[:, 2 * j, :], lamv[:, 2 * j + 1, :], ALU.mult))
                step(vector.tensor_scalar(subg[:, 1:2], subg[:, 0:1], 1.0 - LAMBDA_INIT, None, ALU.mult))
                steps_done(vector)
                for j in range(2):
                    step(vector.reduce_sum(lamt[:, j:j + 1], lamv[:, 2 * j, :], AX_X))
                lam_sum = dve_chain.at
                vector.wait_ge(exp_done[0].sem, e0 + 1)
                step(vector.tensor_tensor(lamt[:, 4:5], lamt[:, 3:4], lamt[:, 2:3], ALU.subtract))
                steps_done(vector)
                step(vector.tensor_scalar(lamt[:, 5:6], lamt[:, 4:5], -LAMBDA_INIT, None, ALU.add))
                steps_done(vector)
                lam_at.append(lam_sum)

            @block.scalar
            def _(scalar):
                scalar.wait_ge(dve_chain.sem, lam_at[0])
                scalar.activation(lamt[:, 2:4], lamt[:, 0:2], ACT.Exp).then_inc(exp_done[0].sem, 1)
        exp_done[0].at += 1
        tables.at += 16 * 7

    lam_at = []

    def head_inputs(which, dst, nxt):
        turns, slab0 = 2, 4 * which
        has_ctx = which == 1
        HSTEPS = 4 if has_ctx else 3
        n0 = list(ring.n)
        x0 = [c.at for c in hstep]
        p0, w0, q0, r0, t0, d0 = ([c.at for c in cs] for cs in (proj_done, raw_done, hss_done, hroot, t1_done, head_done))
        width = NT if has_ctx else NX
        raw = work[:, 4 * NT:8 * NT].rearrange("p (s j n) -> p s j n", s=2, j=2)
        sq = work[:, 0:4 * NT].rearrange("p (s j n) -> p s j n", s=2, j=2)
        root = work[:, 8 * NT:12 * NT].rearrange("p (s j n) -> p s j n", s=2, j=2)
        with nc.Block() as block:
            @block.sync
            def _(sync):
                with sync.Fori(0, turns - 1) as t:
                    for s in range(2):
                        sync.wait_ge(ring.used[s], t + (n0[s] + 1))
                        sync.dma_start(ring.buf[:, s, 0:2 * KD * P],
                                       io["w_qk"][ds(t * 2 + (slab0 + 2 + s), 1)].rearrange("a p n -> (a p) n"))\
                            .then_inc(ring.landed[s], 16)
                prefetch(sync, nxt, [n + (turns if s < 2 else 0) for s, n in enumerate(n0)])

            @block.tensor
            def _(pe):
                with pe.Fori(0, turns) as t:
                    for s in range(2):
                        w = ring.view(s, 2, KD, P)
                        pe.wait_ge(ring.landed[s], t * 16 + 16 * (n0[s] + 1))
                        if s == 1:
                            pe.wait_ge(raw_done[0].sem, t * 2 + (w0[0] + 2))
                        else:
                            pe.wait_ge(raw_done[1].sem, t * 2 + w0[1])
                        for j in range(2):
                            for k in range(KD):
                                mm = pe.matmul(ps[:, j, :], w[:, j, k, :], h[:, k, 0:NX], start=(k == 0), stop=(k == KD - 1))
                            if has_ctx:
                                for k in range(KD):
                                    mm = pe.matmul(ps[:, 2, j * NY:(j + 1) * NY], w[:, j, k, :], h[:, k, NX:NT],
                                                   start=(k == 0), stop=(k == KD - 1))
                        mm.then_inc(proj_done[s].sem, 1)
                        pe.wait_ge(proj_done[s].sem, t + (p0[s] + 1))
                        pe.sem_inc(ring.used[s], 1)
                        if s == 1:
                            pe.wait_ge(head_done[0].sem, t * 2 + (d0[0] + 2))
                        else:
                            pe.wait_ge(head_done[1].sem, t * 2 + d0[1])
                        for j in range(2):
                            pe.wait_ge(raw_done[s].sem, t * 2 + (w0[s] + j + 1))
                            pe.matmul(ps[:, 3 + j, :], rot[:, 1 + which, :], raw[:, s, j, 0:NX], start=True, stop=True)
                            mm = pe.matmul(ps[:, 5 + j, :], bones[:], sq[:, s, j, 0:NX], start=True, stop=True)
                            if has_ctx:
                                mm = pe.matmul(ps[:, 7, j * NY:(j + 1) * NY], bones[:], sq[:, s, j, NX:NT],
                                               start=True, stop=True)
                        mm.then_inc(hss_done[s].sem, 1)

            @block.scalar
            def _(scalar):
                with scalar.Fori(0, turns) as t:
                    for s in range(2):
                        scalar.wait_ge(proj_done[s].sem, t + (p0[s] + 1))
                        scalar.wait_ge(head_done[s].sem, t * 2 + d0[s])
                        for j in range(2):
                            ctx_ps = ps[:, 2, j * NY:(j + 1) * NY]
                            scalar.activation(raw[:, s, j, 0:NX], ps[:, j, :], ACT.Copy)
                            if has_ctx:
                                scalar.activation(raw[:, s, j, NX:NT], ctx_ps, ACT.Copy)
                                scalar.activation(sq[:, s, j, NX:NT], ctx_ps, ACT.Square)
                            scalar.activation(sq[:, s, j, 0:NX], ps[:, j, :], ACT.Square).then_inc(raw_done[s].sem, 1)
                        scalar.wait_ge(hss_done[s].sem, t + (q0[s] + 1))
                        for j in range(2):
                            if has_ctx:
                                scalar.activation(root[:, s, j, NX:NT], ps[:, 7, j * NY:(j + 1) * NY], ACT.Sqrt,
                                                  bias=eps[:, 0:1], scale=1.0 / HD)
                            scalar.activation(root[:, s, j, 0:NX], ps[:, 5 + j, :], ACT.Sqrt,
                                              bias=eps[:, 0:1], scale=1.0 / HD).then_inc(hroot[s].sem, 1)

            @block.gpsimd
            def _(gpsimd):
                with gpsimd.Fori(0, turns) as t:
                    for s in range(2):
                        for j in range(2):
                            gpsimd.wait_ge(raw_done[s].sem, t * 2 + (w0[s] + j + 1))
                            gpsimd.wait_ge(hss_done[s].sem, t + (q0[s] + 1))
                            gpsimd.tensor_tensor(sq[:, s, j, 0:NX], raw[:, s, j, 0:NX], rope[:, 2 + which, :], ALU.mult)\
                                .then_inc(t1_done[s].sem, 1)

            @block.vector
            def _(vector):
                with vector.Fori(0, turns) as t:
                    for s in range(2):
                        for j in range(2):
                            out = ds(t * 4 + (2 * s + j), 1)
                            r = root[:, s, j, 0:width]
                            vector.wait_ge(hroot[s].sem, t * 2 + (r0[s] + j + 1))
                            vector.reciprocal(r, r).then_inc(hstep[s].sem, 1)
                            vector.wait_ge(t1_done[s].sem, t * 2 + (t0[s] + j + 1))
                            vector.tensor_tensor(raw[:, s, j, 0:NX], ps[:, 3 + j, :], rope[:, 1, :], ALU.mult)\
                                .then_inc(hstep[s].sem, 1)
                            vector.wait_ge(hstep[s].sem, t * (2 * HSTEPS) + (x0[s] + HSTEPS * j + 2))
                            vector.tensor_tensor(raw[:, s, j, 0:NX], raw[:, s, j, 0:NX], sq[:, s, j, 0:NX], ALU.add)\
                                .then_inc(hstep[s].sem, 1)
                            if has_ctx:
                                vector.scalar_tensor_tensor(dst[:, out, NX:NT].rearrange("p a n -> p (a n)"),
                                                            raw[:, s, j, NX:NT], qkg[:, 1:2], r[:, NX:NT],
                                                            ALU.mult, ALU.mult).then_inc(hstep[s].sem, 1)
                            vector.wait_ge(hstep[s].sem, t * (2 * HSTEPS) + (x0[s] + HSTEPS * j + HSTEPS))
                            vector.tensor_tensor(dst[:, out, 0:NX].rearrange("p a n -> p (a n)"),
                                                 raw[:, s, j, 0:NX], r[:, 0:NX], ALU.mult).then_inc(head_done[s].sem, 1)
                for s in range(2):
                    vector.wait_ge(head_done[s].sem, d0[s] + 2 * turns)
        for s in range(2):
            ring.n[s] += turns
        for cs, n in ((proj_done, turns), (raw_done, 2 * turns), (hss_done, turns), (hroot, 2 * turns),
                      (t1_done, 2 * turns), (head_done, 2 * turns), (hstep, 2 * HSTEPS * turns)):
            advance(cs, n)

    hstep = [count(f"head_step{s}") for s in range(2)]

    def values(V, nxt):
        turns, C = 2, 2 * P
        n0 = list(ring.n)
        p0, w0 = ([c.at for c in cs] for cs in (proj_done, raw_done))
        with nc.Block() as block:
            @block.sync
            def _(sync):
                with sync.Fori(0, turns - 1) as t:
                    for s in range(2):
                        sync.wait_ge(ring.used[s], t + (n0[s] + 1))
                        sync.dma_start(ring.buf[:, s, 0:KD * C],
                                       io["w_v"][ds(t * 2 + (2 + s), 1)].rearrange("a p n -> (a p) n"))\
                            .then_inc(ring.landed[s], 16)
                prefetch(sync, nxt, [n + (turns if s < 2 else 0) for s, n in enumerate(n0)])

            @block.tensor
            def _(pe):
                with pe.Fori(0, turns) as t:
                    for s in range(2):
                        w = ring.view(s, KD, C)
                        pe.wait_ge(ring.landed[s], t * 16 + 16 * (n0[s] + 1))
                        for m in range(KT):
                            if s == 1:
                                pe.wait_ge(raw_done[0].sem, t * KT + (w0[0] + m + 1))
                            else:
                                pe.wait_ge(raw_done[1].sem, t * KT + w0[1])
                            for k in range(KD):
                                mm = pe.matmul(ps[:, m, 0:C], h[:, k, m * P:(m + 1) * P], w[:, k, :],
                                               start=(k == 0), stop=(k == KD - 1))
                            mm.then_inc(proj_done[s].sem, 1)
                        pe.wait_ge(proj_done[s].sem, t * KT + (p0[s] + KT))
                        pe.sem_inc(ring.used[s], 1)

            @block.scalar
            def _(scalar):
                with scalar.Fori(0, turns) as t:
                    for s in range(2):
                        for m in range(KT):
                            scalar.wait_ge(proj_done[s].sem, t * KT + (p0[s] + m + 1))
                            scalar.activation(V[:, m, ds(t * 2 * C + s * C, C)], ps[:, m, 0:C], ACT.Copy)\
                                .then_inc(raw_done[s].sem, 1)
                for s in range(2):
                    scalar.wait_ge(raw_done[s].sem, w0[s] + turns * KT)
        for s in range(2):
            ring.n[s] += turns
        advance(proj_done, KT * turns)
        advance(raw_done, KT * turns)

    def attention(Q, K, V, O):
        QT = NX // P
        turns = HEADS // 2
        VS = 6
        names = (staged, score_done, max_done, exp_done, prob_done, turn_done, turn_ev, pv_done, o_done, hstep)
        g0, s0, m0, e0, b0, u0, v0, p0, o0, h0 = ([c.at for c in cs] for cs in names)
        at = [0]

        def part(n):
            at[0] += n
            return work[:, at[0] - n:at[0]]

        qs = [hbuf[:, (HEADS + 2 * b) * NX:(HEADS + 2 * b + 2) * NX].rearrange("p (c n) -> p c n", c=2) for b in range(2)]
        ks = [part(NT) for _ in range(2)]
        vs = [part(NT).rearrange("p (m n) -> p m n", m=KT) for _ in range(2)]
        pr = [part(2 * NT).rearrange("p (c n) -> p c n", c=2) for _ in range(2)]
        aT = part(KT * NX).rearrange("p (m n) -> p m n", m=KT)
        sc = ps[:, 0:4, :].rearrange("p (c b) n -> p c (b n)", c=2)
        tp = ps[:, 4:6, :].rearrange("p b n -> p (b n)")

        with nc.Block() as block:
            @block.gpsimd
            def _(gpsimd):
                with gpsimd.Fori(0, turns) as t:
                    for b in range(2):
                        hd = ds(t * 2 + b, 1)
                        gpsimd.wait_ge(pv_done[b].sem, t + p0[b])
                        gpsimd.sem_inc(room.sem, 1)
                        for c in range(2):
                            gpsimd.tensor_tensor(qs[b][:, c, :], Q[:, hd, :].rearrange("p a n -> p (a n)"), own_rows(c),
                                                 ALU.mult).then_inc(staged[b].sem, 1)
                        gpsimd.tensor_copy(ks[b], K[:, hd, :].rearrange("p a n -> p (a n)")).then_inc(staged[b].sem, 1)
                        gpsimd.tensor_copy(vs[b], V[:, :, ds(t * 2 * P + b * P, P)]).then_inc(staged[b].sem, 1)

            @block.tensor
            def _(pe):
                def scores(t, b, q):
                    for c in range(2):
                        if q > 0:
                            pe.wait_ge(exp_done[b].sem, t * (2 * QT) + (e0[b] + 2 * q + c - 1))
                        elif b == 1:
                            pe.wait_ge(exp_done[0].sem, t * (2 * QT) + (e0[0] + 2 * QT + c - 1))
                        else:
                            pe.wait_ge(exp_done[1].sem, t * (2 * QT) + e0[1])
                        for a, n in ((0, NX), (NX, NY)):
                            mm = pe.matmul(sc[:, c, a:a + n], qs[b][:, c, q * P:(q + 1) * P], ks[b][:, a:a + n],
                                           start=True, stop=True)
                        mm.then_inc(score_done[b].sem, 1)

                def turn(t, b, q):
                    pe.wait_ge(prob_done[b].sem, t * QT + (b0[b] + q + 1))
                    if q > 0:
                        pe.wait_ge(turn_ev[b].sem, t * QT + (v0[b] + q))
                    elif b == 1:
                        pe.wait_ge(turn_ev[0].sem, t * QT + (v0[0] + QT))
                    else:
                        pe.wait_ge(turn_ev[1].sem, t * QT + v0[1])
                    for m in range(KT):
                        mm = pe.transpose(tp[:, m * P:(m + 1) * P], pr[q % 2][:, 0, m * P:(m + 1) * P], ident[:])
                    mm.then_inc(turn_done[b].sem, 1)

                with pe.Fori(0, turns) as t:
                    for b in range(2):
                        pe.wait_ge(staged[b].sem, t * 4 + (g0[b] + 4))
                        scores(t, b, 0)
                        for q in range(QT):
                            if q + 1 < QT:
                                scores(t, b, q + 1)
                            turn(t, b, q)
                        pe.wait_ge(turn_ev[b].sem, t * QT + (v0[b] + QT))
                        pe.wait_ge(o_done[b].sem, t + o0[b])
                        for m in range(KT):
                            mm = pe.matmul(ps[:, 6 + b, :], vs[b][:, m, :], aT[:, m, :], start=(m == 0), stop=(m == KT - 1))
                        mm.then_inc(pv_done[b].sem, 1)

            @block.scalar
            def _(scalar):
                with scalar.Fori(0, turns) as t:
                    for b in range(2):
                        for q in range(QT):
                            if q >= 2:
                                scalar.wait_ge(turn_done[b].sem, t * QT + (u0[b] + q - 1))
                            elif b == 1:
                                scalar.wait_ge(turn_done[0].sem, t * QT + (u0[0] + QT - 1 + q))
                            for c in range(2):
                                if q < 2 and b == 0 and c == 0:
                                    scalar.wait_ge(turn_done[1].sem, t * QT + u0[1])
                                scalar.wait_ge(max_done[b].sem, t * (2 * QT) + (m0[b] + 2 * q + c + 1))
                                scalar.activation(pr[q % 2][:, c, :], sc[:, c, 0:NT], ACT.Exp,
                                                  bias=stat[:, q % 2, 2 + c:3 + c], scale=HD ** -0.5,
                                                  accum_out=stat[:, q % 2, 4 + c:5 + c]).then_inc(exp_done[b].sem, 1)
                            if q > 0:
                                scalar.wait_ge(turn_done[b].sem, t * QT + (u0[b] + q))
                                if q == 1:
                                    if b == 1:
                                        scalar.wait_ge(pv_done[0].sem, t + (p0[0] + 1))
                                    else:
                                        scalar.wait_ge(pv_done[1].sem, t + p0[1])
                                scalar.activation(aT[:, :, (q - 1) * P:q * P], tp[:, 0:NT].rearrange("p (m n) -> p m n", m=KT),
                                                  ACT.Copy).then_inc(turn_ev[b].sem, 1)
                        scalar.wait_ge(turn_done[b].sem, t * QT + (u0[b] + QT))
                        scalar.activation(aT[:, :, (QT - 1) * P:QT * P], tp[:, 0:NT].rearrange("p (m n) -> p m n", m=KT),
                                          ACT.Copy).then_inc(turn_ev[b].sem, 1)

            @block.vector
            def _(vector):
                def softmax(t, b, q):
                    def sstep(ins, n):
                        ins.then_inc(hstep[b].sem, 1)
                        vector.wait_ge(hstep[b].sem, t * (VS * QT) + (h0[b] + VS * q + n))
                    st = stat[:, q % 2]
                    for c in range(2):
                        vector.wait_ge(score_done[b].sem, t * (2 * QT) + (s0[b] + 2 * q + c + 1))
                        sstep(vector.reduce_max(st[:, c:c + 1], sc[:, c, 0:NT], AX_X), c + 1)
                        vector.tensor_scalar(st[:, 2 + c:3 + c], st[:, c:c + 1], -HD ** -0.5, None, ALU.mult)\
                            .then_inc(max_done[b].sem, 1)
                    vector.wait_ge(exp_done[b].sem, t * (2 * QT) + (e0[b] + 2 * q + 1))
                    sstep(vector.reciprocal(st[:, 6:7], st[:, 4:5]), 3)
                    sstep(vector.tensor_scalar(pr[q % 2][:, 0, :], pr[q % 2][:, 0, :], st[:, 6:7], None, ALU.mult), 4)
                    vector.wait_ge(exp_done[b].sem, t * (2 * QT) + (e0[b] + 2 * q + 2))
                    sstep(vector.reciprocal(st[:, 7:8], st[:, 5:6]), 5)
                    sstep(vector.tensor_scalar(st[:, 7:8], st[:, 7:8], lamt[:, 5:6], None, ALU.mult), 6)
                    vector.scalar_tensor_tensor(pr[q % 2][:, 0, :], pr[q % 2][:, 1, :], st[:, 7:8],
                                                pr[q % 2][:, 0, :], ALU.mult, ALU.add).then_inc(prob_done[b].sem, 1)

                with vector.Fori(0, turns) as t:
                    for b in range(2):
                        for q in range(QT):
                            softmax(t, b, q)
                        vector.wait_ge(pv_done[b].sem, t + (p0[b] + 1))
                        vector.tensor_copy(O[:, ds(t * 2 + b, 1), :].rearrange("p a n -> p (a n)"), ps[:, 6 + b, :])\
                            .then_inc(o_done[b].sem, 1)
                for b in range(2):
                    vector.wait_ge(o_done[b].sem, o0[b] + turns)
        for cs, n in zip(names, (4, 2 * QT, 2 * QT, 2 * QT, QT, QT, QT, 1, 1, VS * QT)):
            advance(cs, n * turns)

    def output_norm(O, gain):
        q0, r0, s0, h0, d0 = (c.at for c in (sq_done, root_done, ss_done, rstd_done, scaled))
        sq = work[:, 0:2 * NX].rearrange("p (b n) -> p b n", b=2)
        with nc.Block() as block:
            @block.scalar
            def _(scalar):
                for j in range(HEADS):
                    if j >= 2:
                        scalar.wait_ge(ss_done.sem, s0 + j - 1)
                    scalar.activation(sq[:, j % 2, :], O[:, j, :], ACT.Square).then_inc(sq_done.sem, 1)
                for j in range(HEADS):
                    scalar.wait_ge(ss_done.sem, s0 + j + 1)
                    if j >= 2:
                        scalar.wait_ge(scaled.sem, d0 + j - 1)
                    scalar.activation(tmp[:, j % 2, 0:NX], ps[:, j, :], ACT.Sqrt, bias=eps[:, 0:1], scale=1.0 / P)\
                        .then_inc(root_done.sem, 1)

            @block.tensor
            def _(pe):
                for j in range(HEADS):
                    pe.wait_ge(sq_done.sem, q0 + j + 1)
                    pe.matmul(ps[:, j, :], ones[:], sq[:, j % 2, :], start=True, stop=True).then_inc(ss_done.sem, 1)

            @block.vector
            def _(vector):
                for j in range(HEADS):
                    vector.wait_ge(root_done.sem, r0 + j + 1)
                    vector.reciprocal(tmp[:, j % 2, 0:NX], tmp[:, j % 2, 0:NX]).then_inc(rstd_done.sem, 1)
                    vector.wait_ge(rstd_done.sem, h0 + j + 1)
                    vector.scalar_tensor_tensor(O[:, j, :], O[:, j, :], gain, tmp[:, j % 2, 0:NX], ALU.mult, ALU.mult)\
                        .then_inc(scaled.sem, 1)
                vector.wait_ge(scaled.sem, d0 + HEADS)
        for c in (sq_done, root_done, ss_done, rstd_done, scaled):
            c.at += HEADS

    def project_residual(w, src, gate, nxt):
        turns = 2
        n0 = list(ring.n)
        d0, r0 = ([c.at for c in cs] for cs in (down_done, added))
        with nc.Block() as block:
            @block.sync
            def _(sync):
                with sync.Fori(0, turns - 1) as t:
                    for s in range(2):
                        sync.wait_ge(ring.used[s], t + (n0[s] + 1))
                        sync.dma_start(ring.buf[:, s, 0:2 * KD * P], w[ds(t * 2 + (2 + s), 1)].rearrange("a p n -> (a p) n"))\
                            .then_inc(ring.landed[s], 16)
                prefetch(sync, nxt, [n + (turns if s < 2 else 0) for s, n in enumerate(n0)])

            @block.tensor
            def _(pe):
                with pe.Fori(0, turns) as t:
                    for s in range(2):
                        wv = ring.view(s, 2, KD, P)
                        pe.wait_ge(ring.landed[s], t * 16 + 16 * (n0[s] + 1))
                        pe.wait_ge(added[s].sem, t * 2 + r0[s])
                        for j in range(2):
                            for k in range(KD):
                                mm = pe.matmul(ps[:, 2 * s + j, :], wv[:, j, k, :], src[:, k, 0:NX],
                                               start=(k == 0), stop=(k == KD - 1))
                        mm.then_inc(down_done[s].sem, 1)
                        pe.wait_ge(down_done[s].sem, t + (d0[s] + 1))
                        pe.sem_inc(ring.used[s], 1)

            @block.vector
            def _(vector):
                with vector.Fori(0, turns) as t:
                    for s in range(2):
                        vector.wait_ge(down_done[s].sem, t + (d0[s] + 1))
                        for j in range(2):
                            x = xy[:, ds(t * 4 + (2 * s + j), 1), 0:NX].rearrange("p a n -> p (a n)")
                            if gate is None:
                                vector.tensor_tensor(x, ps[:, 2 * s + j, :], x, ALU.add).then_inc(added[s].sem, 1)
                            else:
                                g = gate[:, ds(t * 4 + (2 * s + j), 1), 0:1].rearrange("p a n -> p (a n)")
                                vector.scalar_tensor_tensor(x, ps[:, 2 * s + j, :], g, x, ALU.mult, ALU.add)\
                                    .then_inc(added[s].sem, 1)
                for s in range(2):
                    vector.wait_ge(added[s].sem, r0[s] + 2 * turns)
        for s in range(2):
            ring.n[s] += turns
        advance(down_done, turns)
        advance(added, 2 * turns)

    def second_gains():
        t0 = tables.at
        with nc.Block() as block:
            @block.sync
            def _(sync):
                sync.dma_start(gains2[:], io["gains2"]).then_inc(tables.sem, 16)
                sync.wait_ge(tables.sem, t0 + 16)
        tables.at += 16

    def fourier(F):
        groups, TT = 4, NX // P
        C = 2 * (D // groups)
        Y = big[:, 0:TT * groups * C].rearrange("p (t g n) -> p t g n", t=TT, g=groups)
        cd = big[:, TT * groups * C:TT * groups * C + 2 * C].rearrange("p (k n) -> p k n", k=2)
        cn = big[:, 9216:9216 + 2 * TT * NX].rearrange("p (c t n) -> p c t n", c=2, t=TT)
        t0, p0, w0 = tables.at, [c.at for c in proj_done], [c.at for c in raw_done]
        units = TT * groups
        with nc.Block() as block:
            @block.sync
            def _(sync):
                sync.dma_start(cd, io["dft_feature"]).then_inc(tables.sem, 16)
                sync.dma_start(cn, io["dft_token"]).then_inc(tables.sem, 16)

            @block.tensor
            def _(pe):
                pe.wait_ge(tables.sem, t0 + 32)
                for u in range(units):
                    t, g = u // groups, u % groups
                    if u >= 8:
                        pe.wait_ge(raw_done[u % 2].sem, w0[u % 2] + (u - 8) // 2 + 1)
                    for k in range(2):
                        mm = pe.matmul(ps[:, u % 8, :], h[:, 2 * g + k, t * P:(t + 1) * P], cd[:, k, :],
                                       start=(k == 0), stop=(k == 1))
                    mm.then_inc(proj_done[u % 2].sem, 1)
                for s in range(2):
                    pe.wait_ge(raw_done[s].sem, w0[s] + units // 2)
                for m in range(KD):
                    g, half = m // 2, (m % 2) * P
                    for n in range(2 * TT):
                        c, t = n // TT, n % TT
                        a = c * (C // 2) + half
                        mm = pe.matmul(ps[:, m, :], Y[:, t, g, a:a + P], cn[:, c, t, :],
                                       start=(n == 0), stop=(n == 2 * TT - 1))
                    mm.then_inc(proj_done[m % 2].sem, 1)

            def copies(eng, s, copy):
                for u in range(s, units, 2):
                    eng.wait_ge(proj_done[s].sem, p0[s] + u // 2 + 1)
                    copy(Y[:, u // groups, u % groups, :], ps[:, u % 8, :]).then_inc(raw_done[s].sem, 1)
                for m in range(s, KD, 2):
                    eng.wait_ge(proj_done[s].sem, p0[s] + units // 2 + m // 2 + 1)
                    copy(F[:, m, :], ps[:, m, :]).then_inc(raw_done[s].sem, 1)

            @block.scalar
            def _(scalar):
                copies(scalar, 0, scalar.copy)

            @block.vector
            def _(vector):
                copies(vector, 1, vector.tensor_copy)
        tables.at += 32
        advance(proj_done, (units + KD) // 2)
        advance(raw_done, (units + KD) // 2)

    def project(w, slab0, turns, dst, scale_of, func, nxt):
        n0 = list(ring.n)
        p0, w0 = ([c.at for c in cs] for cs in (proj_done, raw_done))
        with nc.Block() as block:
            @block.sync
            def _(sync):
                with sync.Fori(0, turns - 1) as t:
                    for s in range(2):
                        sync.wait_ge(ring.used[s], t + (n0[s] + 1))
                        sync.dma_start(ring.buf[:, s, 0:2 * KD * P],
                                       w[ds(t * 2 + (slab0 + 2 + s), 1)].rearrange("a p n -> (a p) n"))\
                            .then_inc(ring.landed[s], 16)
                prefetch(sync, nxt, [n + (turns if s < 2 else 0) for s, n in enumerate(n0)])

            @block.tensor
            def _(pe):
                with pe.Fori(0, turns) as t:
                    for s in range(2):
                        wv = ring.view(s, 2, KD, P)
                        pe.wait_ge(ring.landed[s], t * 16 + 16 * (n0[s] + 1))
                        pe.wait_ge(raw_done[s].sem, t * 2 + w0[s])
                        for j in range(2):
                            for k in range(KD):
                                mm = pe.matmul(ps[:, 2 * s + j, :], wv[:, j, k, :], h[:, k, 0:NX],
                                               start=(k == 0), stop=(k == KD - 1))
                            mm.then_inc(proj_done[s].sem, 1)
                        pe.wait_ge(proj_done[s].sem, t * 2 + (p0[s] + 2))
                        pe.sem_inc(ring.used[s], 1)

            @block.scalar
            def _(scalar):
                with scalar.Fori(0, turns) as t:
                    for s in range(2):
                        for j in range(2):
                            scalar.wait_ge(proj_done[s].sem, t * 2 + (p0[s] + j + 1))
                            scalar.activation(dst[:, ds(t * 4 + (2 * s + j), 1), :].rearrange("p a n -> p (a n)"),
                                              ps[:, 2 * s + j, :], func, scale=scale_of).then_inc(raw_done[s].sem, 1)
                for s in range(2):
                    scalar.wait_ge(raw_done[s].sem, w0[s] + 2 * turns)
        for s in range(2):
            ring.n[s] += turns
        advance(proj_done, 2 * turns)
        advance(raw_done, 2 * turns)

    def values_and_gates(F, V2):
        TT = NX // P
        wv = work[:, 0:KD * 3 * P].rearrange("p (k n) -> p k n", k=KD)
        t0, p0, w0, u0, v0 = tables.at, proj_done[0].at, raw_done[0].at, turn_done[0].at, turn_ev[0].at
        with nc.Block() as block:
            @block.sync
            def _(sync):
                sync.dma_start(wv, io["w_v2"]).then_inc(tables.sem, 16)
                for dst, name in ((dist, "dist"), (dist_c[:], "dist_cmp"), (slopes[:], "slopes"), (sinks[:], "sinks")):
                    sync.dma_start(dst, io[name]).then_inc(tables.sem, 16)

            @block.tensor
            def _(pe):
                for m in range(TT):
                    mm = pe.transpose(ps[:, 4, m * P:(m + 1) * P], F[:, 15, m * P:(m + 1) * P], ident[:])
                mm.then_inc(turn_done[0].sem, 1)
                pe.wait_ge(tables.sem, t0 + 5 * 16)
                for m in range(TT):
                    for k in range(KD):
                        mm = pe.matmul(ps[:, m, 0:3 * P], h[:, k, m * P:(m + 1) * P], wv[:, k, :],
                                       start=(k == 0), stop=(k == KD - 1))
                    mm.then_inc(proj_done[0].sem, 1)

            @block.scalar
            def _(scalar):
                scalar.wait_ge(turn_done[0].sem, u0 + 1)
                scalar.activation(gates[:].rearrange("p h b t -> p t (h b)"),
                                  ps[:, 4, :].rearrange("p (t n) -> p t n", t=TT)[:, :, 0:3 * HEADS],
                                  ACT.Sigmoid).then_inc(turn_ev[0].sem, 1)
                for m in range(TT):
                    scalar.wait_ge(proj_done[0].sem, p0 + m + 1)
                    scalar.activation(V2[:, m, :], ps[:, m, 0:3 * P], ACT.Copy).then_inc(raw_done[0].sem, 1)
                scalar.wait_ge(raw_done[0].sem, w0 + TT)
                scalar.wait_ge(turn_ev[0].sem, v0 + 1)
        tables.at += 5 * 16
        proj_done[0].at += TT
        raw_done[0].at += TT
        turn_done[0].at += 1
        turn_ev[0].at += 1

    def compress(F, kcT, vc):
        LP, NB = CMP_LEN // 2, CMP_BLOCKS
        w1 = work[:, 0:2 * LP * CMP_HIDDEN].rearrange("p (v l n) -> p v l n", v=2, l=LP)
        o = [0]

        def part(n):
            o[0] += n
            return hbuf[:, o[0] - n:o[0]]

        blk = part(2 * LP * 2 * NB).rearrange("p (v l c) -> p v l c", v=2, l=LP)
        pos = part(2 * LP * NB).rearrange("p (v l c) -> p v l c", v=2, l=LP)
        w2 = part(2 * 2 * HD).rearrange("p (v k n) -> p v k n", v=2, k=2)
        hid = part(2 * CMP_HIDDEN).rearrange("p (v n) -> p v n", v=2)
        hidT = part(2 * 2 * 2 * NB).rearrange("p (v k n) -> p v k n", v=2, k=2)
        t0, k0, p0, w0, u0, v0 = (c.at for c in (tables, t1_done[0], proj_done[0], raw_done[0], turn_done[0], turn_ev[0]))
        with nc.Block() as block:
            @block.sync
            def _(sync):
                sync.dma_start(pos, io["cmp_pos"]).then_inc(tables.sem, 16)
                sync.dma_start(w1, io["cmp_w1"]).then_inc(tables.sem, 16)
                sync.dma_start(w2, io["cmp_w2"]).then_inc(tables.sem, 16)

            @block.vector
            def _(vector):
                vector.wait_ge(tables.sem, t0 + 48)
                for v in range(2):
                    for g in range(2):
                        for a in range(2):
                            half = slice(a * HD, (a + 1) * HD)
                            for e in range(2):
                                src = F[half, 11 + 2 * v + g, e * CMP_STRIDE:e * CMP_STRIDE + NB * CMP_STRIDE]
                                src = src.rearrange("p (c l) -> p l c", l=CMP_STRIDE)[:, a::2, :]
                                lp = slice(e * LP // 2, (e + 1) * LP // 2)
                                vector.tensor_tensor(blk[half, v, lp, g * NB:(g + 1) * NB], src, pos[half, v, lp, :],
                                                     ALU.add).then_inc(t1_done[0].sem, 1)

            @block.tensor
            def _(pe):
                pe.wait_ge(tables.sem, t0 + 48)
                for v in range(2):
                    pe.wait_ge(t1_done[0].sem, k0 + 8 * (v + 1))
                    for l in range(LP):
                        mm = pe.matmul(ps[0:2 * NB, v, 0:CMP_HIDDEN], blk[:, v, l, :], w1[:, v, l, :],
                                       start=(l == 0), stop=(l == LP - 1))
                    mm.then_inc(proj_done[0].sem, 1)
                for v in range(2):
                    pe.wait_ge(raw_done[0].sem, w0 + v + 1)
                    for k in range(2):
                        mm = pe.transpose(ps[:, 2 + v, k * 2 * NB:(k + 1) * 2 * NB], hid[0:2 * NB, v, k * P:(k + 1) * P],
                                          ident[0:2 * NB, 0:2 * NB])
                    mm.then_inc(turn_done[0].sem, 1)
                pe.wait_ge(turn_ev[0].sem, v0 + 2)
                for g in range(2):
                    for k in range(2):
                        mm = pe.matmul(ps[g * HD:(g + 1) * HD, 4, 0:NB], w2[:, 0, k, :], hidT[:, 0, k, g * NB:(g + 1) * NB],
                                       start=(k == 0), stop=(k == 1))
                for g in range(2):
                    for k in range(2):
                        mm = pe.matmul(ps[0:NB, 5 + g, 0:HD], hidT[:, 1, k, g * NB:(g + 1) * NB], w2[:, 1, k, :],
                                       start=(k == 0), stop=(k == 1))
                mm.then_inc(proj_done[0].sem, 1)

            @block.scalar
            def _(scalar):
                for v in range(2):
                    scalar.wait_ge(proj_done[0].sem, p0 + v + 1)
                    scalar.activation(hid[0:2 * NB, v, :], ps[0:2 * NB, v, 0:CMP_HIDDEN], ACT.Silu)\
                        .then_inc(raw_done[0].sem, 1)
                for v in range(2):
                    scalar.wait_ge(turn_done[0].sem, u0 + v + 1)
                    scalar.activation(hidT[:, v, :, :], ps[:, 2 + v, 0:4 * NB].rearrange("p (k n) -> p k n", k=2),
                                      ACT.Copy).then_inc(turn_ev[0].sem, 1)
                scalar.wait_ge(proj_done[0].sem, p0 + 3)
                scalar.activation(kcT, ps[:, 4, 0:NB], ACT.Copy).then_inc(raw_done[0].sem, 1)
                scalar.activation(vc, ps[0:NB, 5:7, 0:HD], ACT.Copy).then_inc(raw_done[0].sem, 1)
                scalar.wait_ge(raw_done[0].sem, w0 + 4)
        tables.at += 48
        t1_done[0].at += 16
        proj_done[0].at += 3
        raw_done[0].at += 4
        turn_done[0].at += 2
        turn_ev[0].at += 2

    def branches(F, V2, kcT, vc, Oa, Ob):
        TT = NX // P
        TURNS = 4
        back = {1: TT, 2: NSA_WINDOW // P, 3: SWA_WINDOW // P}

        def width(br, q):
            return CMP_BLOCKS if br == 0 else (min(q, back[br]) + 1) * P

        where, total = {}, 0
        for br in range(4):
            for q in range(TT):
                where[br, q] = total
                total += width(br, q)
        S = [work[:, b * total:(b + 1) * total] for b in range(2)]
        PT = ring.buf[:, 2, 0:2 * 1280].rearrange("p (b n) -> p b n", b=2)
        turned = {1: 0, 2: 512, 3: 896, 0: 896 + 256}
        qt = hbuf[:, KD * NX:(KD + 4) * NX].rearrange("p (b k n) -> p b k n", b=2, k=2)
        names = (staged, score_done, prob_done, max_done, exp_done, hstep, turn_done, turn_ev, pv_done, o_done)
        g0, s0, b0, m0, e0, h0, u0, v0, p0, o0 = ([c.at for c in cs] for cs in names)

        def tile(t, base):
            return F[:, ds(t + base, 1), :].rearrange("p a n -> p (a n)")

        def score_bank(br, q):
            n = width(br, q)
            if br == 0:
                return ps[:, 2, 384:384 + n]
            return ps[:, br - 1, 0:n]

        def keys(br, q):
            if br == 0:
                return kcT
            first = (q + 1) * P - width(br, q)
            return F[:, 7 + br, first:(q + 1) * P]

        with nc.Block() as block:
            @block.gpsimd
            def _(gpsimd):
                with gpsimd.Fori(0, TURNS) as t:
                    for b in range(2):
                        gpsimd.wait_ge(score_done[b].sem, t * TT + s0[b])
                        gpsimd.sem_inc(room.sem, 1)
                        for k in range(2):
                            gpsimd.tensor_tensor(qt[:, b, k, :], tile(t, 4 * k), own_rows(b), ALU.mult)\
                                .then_inc(staged[b].sem, 1)

            @block.tensor
            def _(pe):
                def scores(t, b, q):
                    if q > 0:
                        pe.wait_ge(prob_done[b].sem, t * TT + (b0[b] + q))
                    elif b == 1:
                        pe.wait_ge(prob_done[0].sem, t * TT + (b0[0] + TT))
                    else:
                        pe.wait_ge(prob_done[1].sem, t * TT + b0[1])
                    for br in range(4):
                        mm = pe.matmul(score_bank(br, q), qt[:, b, br // 3, q * P:(q + 1) * P], keys(br, q),
                                       start=True, stop=True)
                    mm.then_inc(score_done[b].sem, 1)

                def turn(t, b, q):
                    if q > 0:
                        pe.wait_ge(turn_ev[b].sem, t * TT + (v0[b] + q))
                    elif b == 1:
                        pe.wait_ge(turn_ev[0].sem, t * TT + (v0[0] + TT))
                    else:
                        pe.wait_ge(turn_ev[1].sem, t * TT + v0[1])
                    pe.wait_ge(hstep[b].sem, t * BSTEPS + (h0[b] + BSTEPS - 4 * (TT - 1 - q)))
                    for br in range(4):
                        n = width(br, q)
                        bank = {1: 3, 2: 4, 3: 5, 0: 5}[br]
                        c = 256 if br == 0 else 0
                        for a in range(0, n, P):
                            w = min(P, n - a)
                            src = S[b][:, where[br, q] + a:where[br, q] + a + w]
                            mm = pe.transpose(ps[0:w, bank, c + a:c + a + P], src, ident[:])
                    mm.then_inc(turn_done[b].sem, 1)

                def weigh(t, b, q):
                    half = slice(b * HD, (b + 1) * HD)
                    pe.wait_ge(turn_ev[b].sem, t * TT + (v0[b] + q + 1))
                    if q == 0:
                        pe.wait_ge(o_done[b].sem, t + o0[b])
                    cols = slice(q * P, (q + 1) * P)
                    jobs = [(6, vc[:, b, :], PT[0:CMP_BLOCKS, q % 2, turned[0]:turned[0] + P])]
                    for br in (1, 2, 3):
                        n = width(br, q) // P
                        for a in range(n):
                            jobs.append((7 if br == 3 else 6,
                                         V2[:, q + 1 - n + a, (br - 1) * P + b * HD:(br - 1) * P + (b + 1) * HD],
                                         PT[:, q % 2, turned[br] + a * P:turned[br] + (a + 1) * P]))
                    for bank in (6, 7):
                        own = [j for j in jobs if j[0] == bank]
                        for n, (_, w, p) in enumerate(own):
                            mm = pe.matmul(ps[half, bank, cols], w, p, start=(n == 0), stop=(n == len(own) - 1))
                    mm.then_inc(pv_done[b].sem, 1)

                def front(t, b):
                    pe.wait_ge(staged[b].sem, t * 2 + (g0[b] + 2))
                    for q in range(TT):
                        scores(t, b, q)

                def rear(t, b):
                    turn(t, b, 0)
                    for q in range(TT):
                        if q + 1 < TT:
                            turn(t, b, q + 1)
                        weigh(t, b, q)

                front(0, 0)
                with pe.Fori(0, TURNS - 1) as t:
                    front(t, 1)
                    rear(t, 0)
                    front(t + 1, 0)
                    rear(t, 1)
                front(TURNS - 1, 1)
                rear(TURNS - 1, 0)
                rear(TURNS - 1, 1)

            @block.vector
            def _(vector):
                FRONT = 8 * TT + 2

                def counted(t, b, at):
                    k = [at]

                    def sstep(ins):
                        ins.then_inc(hstep[b].sem, 1)
                        k[0] += 1

                    def sdone():
                        vector.wait_ge(hstep[b].sem, t * BSTEPS + (h0[b] + k[0]))
                    return k, sstep, sdone

                def front(t, b):
                    head = t + 4 * b
                    st = stat2[:, b]
                    k, sstep, sdone = counted(t, b, 0)
                    vector.wait_ge(turn_done[b].sem, t * TT + u0[b])
                    for q in range(TT):
                        vector.wait_ge(score_done[b].sem, t * TT + (s0[b] + q + 1))
                        for br in range(4):
                            n = width(br, q)
                            slope = slopes[:, ds(head + (8 if br == 3 else 0), 1)]
                            if br == 0:
                                d = dist_c[:, q, :]
                            else:
                                end = {1: 512, 2: 896, 3: 1152}[br]
                                d = dist[:, end - n:end]
                            sstep(vector.scalar_tensor_tensor(S[b][:, where[br, q]:where[br, q] + n], d, slope,
                                                              score_bank(br, q), ALU.mult, ALU.add))
                        sdone()
                        vector.sem_inc(prob_done[b].sem, 1)
                        for br in range(4):
                            n = width(br, q)
                            sstep(vector.reduce_max(st[:, 0, br * TT + q:br * TT + q + 1],
                                                    S[b][:, where[br, q]:where[br, q] + n], AX_X))
                    sdone()
                    sstep(vector.tensor_scalar(st[:, 0, 12:16], st[:, 0, 12:16], sinks[:, ds(head, 1)], None, ALU.max))
                    sdone()
                    sstep(vector.tensor_scalar(st[:, 1, :], st[:, 0, :], -1e20, -1.0, ALU.max, ALU.mult))
                    sdone()
                    vector.sem_inc(max_done[b].sem, 1)
                    assert k[0] == FRONT

                def rear(t, b):
                    head = t + 4 * b
                    st = stat2[:, b]
                    k, sstep, sdone = counted(t, b, FRONT)
                    vector.wait_ge(exp_done[b].sem, t + (e0[b] + 1))
                    sstep(vector.tensor_tensor(st[:, 2, 12:16], st[:, 2, 12:16], st[:, 3, 0:4], ALU.add))
                    sdone()
                    sstep(vector.tensor_scalar(st[:, 2, :], st[:, 2, :], 1e-30, None, ALU.max))
                    sdone()
                    sstep(vector.reciprocal(st[:, 2, :], st[:, 2, :]))
                    sdone()
                    sstep(vector.tensor_tensor(st[:, 2, 0:12], st[:, 2, 0:12],
                                               gates[:, ds(head, 1), :, :].rearrange("p a b t -> p (a b t)"), ALU.mult))
                    sdone()
                    for q in range(TT):
                        for br in range(4):
                            c = S[b][:, where[br, q]:where[br, q] + width(br, q)]
                            sstep(vector.tensor_scalar(c, c, st[:, 2, br * TT + q:br * TT + q + 1], None, ALU.mult))
                    assert k[0] == BSTEPS

                front(0, 0)
                with vector.Fori(0, TURNS - 1) as t:
                    front(t, 1)
                    rear(t, 0)
                    front(t + 1, 0)
                    rear(t, 1)
                front(TURNS - 1, 1)
                rear(TURNS - 1, 0)
                rear(TURNS - 1, 1)

            @block.scalar
            def _(scalar):
                def front(t, b):
                    st = stat2[:, b]
                    scalar.wait_ge(max_done[b].sem, t + (m0[b] + 1))
                    for br in range(4):
                        for q in range(TT):
                            i = br * TT + q
                            c = S[b][:, where[br, q]:where[br, q] + width(br, q)]
                            scalar.activation(c, c, ACT.Exp, bias=st[:, 1, i:i + 1], accum_out=st[:, 2, i:i + 1])\
                                .then_inc(exp_part.sem, 1)
                    scalar.activation(st[:, 3, 0:4], st[:, 1, 12:16], ACT.Exp, bias=sinks[:, ds(t + 4 * b, 1)])\
                        .then_inc(exp_part.sem, 1)
                    scalar.wait_ge(exp_part.sem, t * 34 + (x0 + 17 * (b + 1)))
                    scalar.sem_inc(exp_done[b].sem, 1)

                def rear(t, b):
                    for q in range(TT):
                        scalar.wait_ge(turn_done[b].sem, t * TT + (u0[b] + q + 1))
                        if q >= 2:
                            scalar.wait_ge(pv_done[b].sem, t * TT + (p0[b] + q - 1))
                        elif b == 1:
                            scalar.wait_ge(pv_done[0].sem, t * TT + (p0[0] + TT - 1 + q))
                        else:
                            scalar.wait_ge(pv_done[1].sem, t * TT + p0[1])
                        for n, (bank, a) in enumerate(((3, 0), (4, 512), (5, 896))):
                            wide = width(n + 1, q)
                            scalar.activation(PT[:, q % 2, a:a + wide], ps[:, bank, 0:wide], ACT.Copy)\
                                .then_inc(ev_part.sem, 1)
                        scalar.activation(PT[0:CMP_BLOCKS, q % 2, turned[0]:turned[0] + P],
                                          ps[0:CMP_BLOCKS, 5, 256:256 + P], ACT.Copy).then_inc(ev_part.sem, 1)
                        scalar.wait_ge(ev_part.sem, t * (8 * TT) + (y0 + 4 * TT * b + 4 * (q + 1)))
                        scalar.sem_inc(turn_ev[b].sem, 1)
                    half = slice(b * HD, (b + 1) * HD)
                    scalar.wait_ge(pv_done[b].sem, t * TT + (p0[b] + TT))
                    scalar.activation(Oa[half, ds(t, 1), :].rearrange("p a n -> p (a n)"), ps[half, 6, :], ACT.Copy)\
                        .then_inc(o_part.sem, 1)
                    scalar.activation(Ob[half, ds(t, 1), :].rearrange("p a n -> p (a n)"), ps[half, 7, :], ACT.Copy)\
                        .then_inc(o_part.sem, 1)
                    scalar.wait_ge(o_part.sem, t * 4 + (z0 + 2 * (b + 1)))
                    scalar.sem_inc(o_done[b].sem, 1)

                front(0, 0)
                with scalar.Fori(0, TURNS - 1) as t:
                    rear(t, 0)
                    front(t, 1)
                    rear(t, 1)
                    front(t + 1, 0)
                rear(TURNS - 1, 0)
                front(TURNS - 1, 1)
                rear(TURNS - 1, 1)
        advance(staged, 2 * TURNS)
        for cs, n in zip(names[1:], (TT, TT, 1, 1, BSTEPS, TT, TT, TT, 1)):
            advance(cs, n * TURNS)

    BSTEPS = 8 * 4 + 2 + 4 + 4 * 4
    exp_part, ev_part, o_part = (count(n) for n in ("exp_part", "turned_part", "output_part"))
    x0 = y0 = z0 = 0

    def merge(Oab, G, U, nxt):
        turns = 2
        w = io["w_ab"]
        n0 = list(ring.n)
        d0, r0 = ([c.at for c in cs] for cs in (down_done, added))
        k0 = dve_chain.at
        with nc.Block() as block:
            @block.sync
            def _(sync):
                with sync.Fori(0, turns - 1) as t:
                    for s in range(2):
                        sync.wait_ge(ring.used[s], t + (n0[s] + 1))
                        sync.dma_start(ring.buf[:, s, 0:2 * KD * P], w[ds(t * 2 + (2 + s), 1)].rearrange("a p n -> (a p) n"))\
                            .then_inc(ring.landed[s], 16)
                prefetch(sync, nxt, [n + (turns if s < 2 else 0) for s, n in enumerate(n0)])

            @block.tensor
            def _(pe):
                with pe.Fori(0, turns) as t:
                    for s in range(2):
                        wv = ring.view(s, 2, KD, P)
                        pe.wait_ge(ring.landed[s], t * 16 + 16 * (n0[s] + 1))
                        pe.wait_ge(added[s].sem, t * 2 + r0[s])
                        for j in range(2):
                            for k in range(KD):
                                mm = pe.matmul(ps[:, 4 * s + 2 * j + k // 4, :], wv[:, j, k, :], Oab[:, k, :],
                                               start=(k % 4 == 0), stop=(k % 4 == 3))
                        mm.then_inc(down_done[s].sem, 1)
                        pe.wait_ge(down_done[s].sem, t + (d0[s] + 1))
                        pe.sem_inc(ring.used[s], 1)

            @block.vector
            def _(vector):
                with vector.Fori(0, turns) as t:
                    for s in range(2):
                        vector.wait_ge(down_done[s].sem, t + (d0[s] + 1))
                        for j in range(2):
                            m = t * 4 + (2 * s + j)

                            def at(buf, i):
                                return buf[:, ds(i, 1), :].rearrange("p a n -> p (a n)")
                            k = 4 * s + 2 * j
                            vector.tensor_tensor(at(U, m), ps[:, k, :], at(G, m), ALU.mult).then_inc(dve_chain.sem, 1)
                            vector.tensor_tensor(tmp[:, 0, 0:NX], ps[:, k + 1, :], at(G, m + 8), ALU.mult)\
                                .then_inc(dve_chain.sem, 1)
                            vector.wait_ge(dve_chain.sem, t * 12 + (k0 + 6 * s + 3 * j + 2))
                            vector.tensor_tensor(at(U, m), at(U, m), tmp[:, 0, 0:NX], ALU.add).then_inc(dve_chain.sem, 1)
                            vector.wait_ge(dve_chain.sem, t * 12 + (k0 + 6 * s + 3 * j + 3))
                            vector.sem_inc(added[s].sem, 1)
        for s in range(2):
            ring.n[s] += turns
        dve_chain.at += 12 * turns
        advance(down_done, turns)
        advance(added, 2 * turns)

    def route():
        TT = NX // P
        NE, NG, PER = EXPERTS, GROUPS, EXPERTS // GROUPS
        o = [0]

        def part(n):
            o[0] += n
            return work[:, o[0] - n:o[0]]

        wr = part(KD * (NG + NE)).rearrange("p (k n) -> p k n", k=KD)
        rb = part(NG + NE)
        rev = part(NE)
        base = part(NE)
        slot_no = part(MOE_BLOCKS + 1)
        before = part(P)
        hot = part(TT * NE).rearrange("p (t n) -> p t n", t=TT)
        row = part(TT * NE).rearrange("p (t n) -> p t n", t=TT)
        shift = part(NE)
        extra = part(P)
        past = part(8)
        expert = part(MOE_BLOCKS + 1)
        rowf = part(2 * TT).rearrange("p (r t) -> p r t", r=2)
        hT = big[:, 0:TT * D].rearrange("p (t d) -> p t d", t=TT)
        nearer = ps[:, 1, 0:TT * NE].rearrange("p (t n) -> p t n", t=TT)
        L = part(TT * (NG + NE)).rearrange("p (t n) -> p t n", t=TT)
        eq = part(TT * NE).rearrange("p (t n) -> p t n", t=TT)
        em = part(TT * NE).rearrange("p (t n) -> p t n", t=TT)
        oh1 = part(TT * NE).rearrange("p (t n) -> p t n", t=TT)
        oh2 = part(TT * NE).rearrange("p (t n) -> p t n", t=TT)
        gs = part(TT * 16).rearrange("p (t n) -> p t n", t=TT)
        v = part(TT * 16).rearrange("p (t n) -> p t n", t=TT)
        t0, p0, e0, u0, v0 = (c.at for c in (tables, proj_done[0], exp_done[0], turn_done[0], turn_ev[0]))
        c0 = counted.at
        mark = []

        def turned(i):
            return ps[:, 2 + 2 * (i % 3):4 + 2 * (i % 3), :].rearrange("p b n -> p (b n)")

        with nc.Block() as block:
            @block.sync
            def _(sync):
                sync.dma_start(wr, io["w_route"]).then_inc(tables.sem, 16)
                sync.dma_start(rb, io["b_route"]).then_inc(tables.sem, 16)
                sync.dma_start(rev, io["rev"]).then_inc(tables.sem, 16)
                sync.dma_start(base, io["expert_base"]).then_inc(tables.sem, 16)
                sync.dma_start(slot_no, io["block_numbers"]).then_inc(tables.sem, 16)
                sync.dma_start(before, io["before"]).then_inc(tables.sem, 16)
                for s in range(3):
                    sync.dma_start(wset(s), io["w_exp"][s].rearrange("p (a n) -> p a n", a=3)).then_inc(set_landed[s].sem, 16)
                sync.wait_ge(scattered.sem, 32 * TT)
                for s in range(3):
                    sync.dma_start(xin(s), io["slots"][s * P:(s + 1) * P, :]).then_inc(x_landed[s].sem, 16)

            @block.vector
            def _(vector):
                vector.wait_ge(tables.sem, t0 + 96)
                tiles = range(TT)

                def each(f):
                    for i in tiles:
                        step(f(i))
                    steps_done(vector)

                def first_of_max(dst, src, m, n, t2):
                    each(lambda i: vector.scalar_tensor_tensor(eq[:, i, 0:n], src(i), m(i), rev[:, NE - n:NE],
                                                               ALU.is_ge, ALU.mult))
                    each(lambda i: vector.reduce_max(t2(i), eq[:, i, 0:n], AX_X))
                    each(lambda i: vector.tensor_scalar(dst(i), eq[:, i, 0:n], t2(i), None, ALU.is_ge))

                vector.wait_ge(proj_done[0].sem, p0 + TT)
                for i in tiles:
                    step(vector.tensor_tensor(L[:, i, :], ps[:, 0, i * (NG + NE):(i + 1) * (NG + NE)], rb, ALU.add))
                steps_done(vector)
                each(lambda i: vector.reduce_max(v[:, i, 0:1], L[:, i, 0:NG], AX_X))
                each(lambda i: vector.tensor_scalar(v[:, i, 1:2], v[:, i, 0:1], -1.0, None, ALU.mult))
                mark.append(dve_chain.at)
                first_of_max(lambda i: gs[:, i, 0:NG], lambda i: L[:, i, 0:NG], lambda i: v[:, i, 0:1], NG,
                             lambda i: v[:, i, 2:3])
                each(lambda i: vector.tensor_scalar(gs[:, i, NG:2 * NG], gs[:, i, 0:NG], -1.0, 1e30, ALU.add, ALU.mult))
                for g in range(NG):
                    a = slice(g * PER, (g + 1) * PER)
                    each(lambda i: vector.tensor_scalar(em[:, i, a], L[:, i, NG + g * PER:NG + (g + 1) * PER],
                                                        gs[:, i, NG + g:NG + g + 1], None, ALU.add))
                each(lambda i: vector.reduce_max(v[:, i, 3:4], em[:, i, :], AX_X))
                first_of_max(lambda i: oh1[:, i, :], lambda i: em[:, i, :], lambda i: v[:, i, 3:4], NE,
                             lambda i: v[:, i, 4:5])
                each(lambda i: vector.scalar_tensor_tensor(em[:, i, :], oh1[:, i, :], -1e30, em[:, i, :],
                                                           ALU.mult, ALU.add))
                each(lambda i: vector.reduce_max(v[:, i, 5:6], em[:, i, :], AX_X))
                first_of_max(lambda i: oh2[:, i, :], lambda i: em[:, i, :], lambda i: v[:, i, 5:6], NE,
                             lambda i: v[:, i, 6:7])
                step(vector.tensor_tensor(hot, oh1, oh2, ALU.add))
                mark.append(dve_chain.at)
                each(lambda i: vector.tensor_tensor(v[:, i, 7:8], v[:, i, 5:6], v[:, i, 3:4], ALU.subtract))
                mark.append(dve_chain.at)
                vector.wait_ge(counted.sem, c0 + 1)
                step(vector.tensor_scalar(extra[0:NE], ps[0:NE, 1, P:2 * P], P + 0.5, None, ALU.is_ge))
                steps_done(vector)
                for j in range(2, TT):
                    step(vector.scalar_tensor_tensor(extra[0:NE], ps[0:NE, 1, P:2 * P], j * P + 0.5, extra[0:NE],
                                                     ALU.is_ge, ALU.add))
                    steps_done(vector)
                mark.append(dve_chain.at)
                vector.wait_ge(counted.sem, c0 + 2)
                step(vector.tensor_tensor(past[0:NE], slot_no[0:NE, 0:8], ps[0:NE, 1, 2 * P:2 * P + 8], ALU.is_ge))
                mark.append(dve_chain.at)
                step(vector.tensor_scalar(shift, ps[:, 1, 3 * P:3 * P + NE], float(P), float((NE - 1) * P),
                                          ALU.mult, ALU.add))
                steps_done(vector)
                step(vector.tensor_tensor(shift, shift, base, ALU.subtract))
                steps_done(vector)
                each(lambda i: vector.scalar_tensor_tensor(row[:, i, :], nearer[:, i, :], P - 0.5, shift,
                                                           ALU.is_ge, ALU.mult))
                each(lambda i: vector.tensor_tensor(row[:, i, :], row[:, i, :], nearer[:, i, :], ALU.add))
                each(lambda i: vector.tensor_tensor(row[:, i, :], row[:, i, :], base, ALU.add))
                for r, oh in enumerate((oh1, oh2)):
                    step(vector.tensor_tensor(eq, oh, row, ALU.mult))
                    steps_done(vector)
                    step(vector.reduce_sum(rowf[:, r, :], eq, AX_X))
                    steps_done(vector)
                step(vector.tensor_copy(dest[:], rowf.rearrange("p r t -> p (r t)")))
                mark.append(dve_chain.at)
                vector.wait_ge(counted.sem, c0 + 3)
                step(vector.tensor_scalar(expert[0:1, 0:NE], slot_no[0:1, 0:NE], 0.0, None, ALU.add))
                step(vector.tensor_scalar(expert[0:1, NE:NE + 8], ps[0:1, 0, 0:8], float(NE - 1),
                                          None, ALU.min))
                steps_done(vector)
                step(vector.tensor_copy(block_expert[:], expert[0:1, :]))
                vector.wait_ge(exp_done[0].sem, e0 + 2 * TT)
                each(lambda i: vector.tensor_scalar(v[:, i, 10:11], v[:, i, 8:9], 1.0, v[:, i, 9:10], ALU.add, ALU.mult))
                each(lambda i: vector.reciprocal(share[:, 0, i:i + 1], v[:, i, 10:11]))
                each(lambda i: vector.tensor_tensor(share[:, 1, i:i + 1], share[:, 0, i:i + 1], v[:, i, 8:9], ALU.mult))

            @block.scalar
            def _(scalar):
                for i in range(TT):
                    scalar.wait_ge(turn_done[0].sem, u0 + i + 1)
                    scalar.activation(hT[:, i, :], turned(i), ACT.Copy).then_inc(turn_ev[0].sem, 1)
                scalar.wait_ge(dve_chain.sem, mark[0])
                for i in range(TT):
                    scalar.activation(gs[:, i, 8:8 + NG], L[:, i, 0:NG], ACT.Exp, bias=v[:, i, 1:2],
                                      accum_out=v[:, i, 9:10]).then_inc(exp_done[0].sem, 1)
                scalar.wait_ge(dve_chain.sem, mark[2])
                for i in range(TT):
                    scalar.activation(v[:, i, 8:9], v[:, i, 7:8], ACT.Exp).then_inc(exp_done[0].sem, 1)
            @block.tensor
            def _(pe):
                pe.wait_ge(tables.sem, t0 + 96)
                for i in range(TT):
                    for k in range(KD):
                        mm = pe.matmul(ps[:, 0, i * (NG + NE):(i + 1) * (NG + NE)], h[:, k, i * P:(i + 1) * P], wr[:, k, :],
                                       start=(k == 0), stop=(k == KD - 1))
                    mm.then_inc(proj_done[0].sem, 1)
                for i in range(TT):
                    if i == 3:
                        pe.wait_ge(turn_ev[0].sem, v0 + 1)
                    for k in range(KD):
                        mm = pe.transpose(turned(i)[:, k * P:(k + 1) * P], h[:, k, i * P:(i + 1) * P], ident[:])
                    mm.then_inc(turn_done[0].sem, 1)
                pe.wait_ge(dve_chain.sem, mark[1])
                for i in range(TT):
                    for j in range(i + 1):
                        pe.matmul(nearer[:, i, :], before if j == i else ones[:], hot[:, j, :],
                                  start=(j == 0), stop=(j == i))
                for i in range(TT):
                    mm = pe.matmul(ps[0:NE, 1, P:2 * P], hot[:, i, :], ones[:], start=(i == 0), stop=(i == TT - 1))
                mm.then_inc(counted.sem, 1)
                pe.wait_ge(dve_chain.sem, mark[3])
                pe.matmul(ps[0:NE, 1, 2 * P:3 * P], before[0:NE, 0:NE], extra[0:NE], start=True, stop=False)
                pe.matmul(ps[0:NE, 1, 2 * P:3 * P], ident[0:NE, 0:NE], extra[0:NE], start=False, stop=True)
                pe.matmul(ps[:, 1, 3 * P:3 * P + NE], extra[0:NE], before[0:NE, 0:NE], start=True, stop=True)\
                    .then_inc(counted.sem, 1)
                pe.wait_ge(dve_chain.sem, mark[4])
                pe.matmul(ps[:, 0, 0:8], ones[0:NE, :], past[0:NE], start=True, stop=True)\
                    .then_inc(counted.sem, 1)

            @block.gpsimd
            def _(gpsimd):
                gpsimd.wait_ge(zeroed.sem, 48)
                gpsimd.wait_ge(turn_ev[0].sem, v0 + TT)
                gpsimd.wait_ge(dve_chain.sem, mark[5])
                for r in range(2):
                    for i in range(TT):
                        c = r * TT + i
                        gpsimd.indirect_dma_start(io["slots"], bass.IndirectOffsetOnAxis(dest[:, c:c + 1], 0),
                                                  hT[:, i, :], None).then_inc(scattered.sem, 16)
        tables.at += 96
        proj_done[0].at += TT
        exp_done[0].at += 2 * TT
        turn_done[0].at += TT
        turn_ev[0].at += TT
        counted.at += 3

    def experts():
        LAST = MOE_BLOCKS // 3 - 1
        gT = work[:, 0:D].rearrange("p (k n) -> p k n", k=KD)
        gate = [work[:, D + s * 2 * P:D + (s + 1) * 2 * P] for s in range(3)]
        act = [work[:, D + (3 + s) * 2 * P:D + (4 + s) * 2 * P].rearrange("p (f n) -> p f n", f=2) for s in range(3)]
        y = [work[:, 3 * D + s * D:4 * D + s * D] for s in range(3)]
        rows_ps = ps[:, 0:2, :].rearrange("p b n -> p (b n)")
        y_ps = ps[:, 5:7, :].rearrange("p b n -> p (b n)")
        HF = D // 2

        def in_order(eng, turn, gate_up, down):
            turn(0, 0)
            gate_up(0, 0)
            turn(0, 1)
            with eng.Fori(0, LAST) as t:
                for s in range(3):
                    gate_up(t + (s + 1) // 3, (s + 1) % 3)
                    turn(t + (s + 2) // 3, (s + 2) % 3)
                    down(t, s)
            gate_up(LAST, 1)
            turn(LAST, 2)
            down(LAST, 0)
            gate_up(LAST, 2)
            down(LAST, 1)
            down(LAST, 2)

        with nc.Block() as block:
            @block.sync
            def _(sync):
                def store(t, s):
                    for c in (y_by_act, y_by_vec):
                        sync.wait_ge(c.sem, t * 3 + (s + 2))
                    sync.dma_start(io["slots_out"][ds(t * (3 * P) + s * P, P), :], y[s]).then_inc(y_stored[s].sem, 16)

                with sync.Fori(0, LAST) as t:
                    for s in range(3):
                        sync.wait_ge(rows_turned.sem, t * 3 + (s + 1))
                        sync.dma_start(xin(s), io["slots"][ds(t * (3 * P) + (3 + s) * P, P), :]).then_inc(x_landed[s].sem, 16)
                        store(t, s)
                        e = sync.value_load(block_expert[0:1, ds(t * 3 + (3 + s), 1)], min_val=0, max_val=EXPERTS - 1)
                        sync.dma_start(wset(s), io["w_exp"][ds(e, 1)].rearrange("a p (c n) -> (a p) c n", c=3))\
                            .then_inc(set_landed[s].sem, 16)
                for s in range(3):
                    store(LAST, s)
                for s in range(3):
                    sync.wait_ge(y_stored[s].sem, 16 * (LAST + 1) + 1)

            @block.tensor
            def _(pe):
                def turn(t, s):
                    pe.wait_ge(x_landed[s].sem, t * 16 + 16)
                    for c in (rows_by_act, rows_by_vec):
                        pe.wait_ge(c.sem, t * 3 + (s + 1))
                    for k in range(KD):
                        mm = pe.transpose(rows_ps[:, k * P:(k + 1) * P], xin(s)[:, k * P:(k + 1) * P], ident[:])
                    mm.then_inc(rows_turned.sem, 1)

                def gate_up(t, s):
                    w = wset(s)[:, 0:2].rearrange("p f (j k n) -> p f j k n", j=2, k=KD)
                    pe.wait_ge(set_landed[s].sem, t * 16 + 16)
                    for c in (rows_by_act, rows_by_vec):
                        pe.wait_ge(c.sem, t * 3 + (s + 2))
                    for j in range(2):
                        for f in range(2):
                            for k in range(KD):
                                mm = pe.matmul(ps[:, 2 + s, (2 * j + f) * P:(2 * j + f + 1) * P], w[:, f, j, k, :],
                                               gT[:, k, :], start=(k == 0), stop=(k == KD - 1))
                    mm.then_inc(hidden_mm.sem, 1)

                def down(t, s):
                    w = wset(s)[:, 2].rearrange("p (f n) -> p f n", f=2)
                    pe.wait_ge(hidden_done.sem, t * 3 + (s + 1))
                    for c in (y_by_act, y_by_vec):
                        pe.wait_ge(c.sem, t * 3 + (s + 1))
                    for a in range(2):
                        for f in range(2):
                            mm = pe.matmul(y_ps[:, a * HF:(a + 1) * HF], act[s][:, f, :], w[:, f, a * HF:(a + 1) * HF],
                                           start=(f == 0), stop=(f == 1))
                        mm.then_inc(y_mm.sem, 1)

                in_order(pe, turn, gate_up, down)

            @block.scalar
            def _(scalar):
                def turn(t, s):
                    scalar.wait_ge(rows_turned.sem, t * 3 + (s + 1))
                    scalar.activation(gT[:, 0:KD // 2, :].rearrange("p k n -> p (k n)"), rows_ps[:, 0:HF], ACT.Copy)\
                        .then_inc(rows_by_act.sem, 1)

                def gate_up(t, s):
                    scalar.wait_ge(hidden_mm.sem, t * 3 + (s + 1))
                    scalar.activation(gate[s], ps[:, 2 + s, 0:2 * P], ACT.Silu).then_inc(gate_done.sem, 1)

                def down(t, s):
                    scalar.wait_ge(y_mm.sem, t * 6 + (2 * s + 1))
                    scalar.wait_ge(y_stored[s].sem, t * 16 + 1)
                    scalar.activation(y[s][:, 0:HF], y_ps[:, 0:HF], ACT.Copy).then_inc(y_by_act.sem, 1)

                in_order(scalar, turn, gate_up, down)

            @block.vector
            def _(vector):
                def turn(t, s):
                    vector.wait_ge(rows_turned.sem, t * 3 + (s + 1))
                    vector.tensor_copy(gT[:, KD // 2:KD, :].rearrange("p k n -> p (k n)"), rows_ps[:, HF:D])\
                        .then_inc(rows_by_vec.sem, 1)

                def gate_up(t, s):
                    vector.wait_ge(gate_done.sem, t * 3 + (s + 1))
                    vector.tensor_tensor(act[s].rearrange("p f n -> p (f n)"), gate[s], ps[:, 2 + s, 2 * P:4 * P],
                                         ALU.mult).then_inc(hidden_done.sem, 1)

                def down(t, s):
                    vector.wait_ge(y_mm.sem, t * 6 + (2 * s + 2))
                    vector.wait_ge(y_stored[s].sem, t * 16 + 1)
                    vector.tensor_copy(y[s][:, HF:D], y_ps[:, HF:D]).then_inc(y_by_vec.sem, 1)

                in_order(vector, turn, gate_up, down)

    def combine():
        TT = NX // P
        Y = big[:, 0:2 * TT * D].rearrange("p (r t d) -> p r t d", r=2, t=TT)
        m0, u0, a0 = dve_chain.at, turn_done[0].at, added[0].at

        def turned(i):
            return ps[:, 2 * (i % 2):2 + 2 * (i % 2), :].rearrange("p b n -> p (b n)")

        with nc.Block() as block:
            @block.gpsimd
            def _(gpsimd):
                for i in range(TT):
                    for r in range(2):
                        c = r * TT + i
                        gpsimd.indirect_dma_start(Y[:, r, i, :], None, io["slots_out"],
                                                  bass.IndirectOffsetOnAxis(dest[:, c:c + 1], 0)).then_inc(gathered[i].sem, 16)

            @block.tensor
            def _(pe):
                for i in range(TT):
                    pe.wait_ge(dve_chain.sem, m0 + 2 * i + 2)
                    if i >= 2:
                        pe.wait_ge(added[0].sem, a0 + i - 1)
                    for k in range(KD):
                        mm = pe.transpose(turned(i)[:, k * P:(k + 1) * P], Y[:, 0, i, k * P:(k + 1) * P], ident[:])
                    mm.then_inc(turn_done[0].sem, 1)

            @block.vector
            def _(vector):
                def weigh(i):
                    vector.wait_ge(gathered[i].sem, 32)
                    step(vector.tensor_scalar(Y[:, 0, i, :], Y[:, 0, i, :], share[:, 0, i:i + 1], None, ALU.mult))
                    steps_done(vector)
                    step(vector.scalar_tensor_tensor(Y[:, 0, i, :], Y[:, 1, i, :], share[:, 1, i:i + 1], Y[:, 0, i, :],
                                                     ALU.mult, ALU.add))

                def add(i):
                    vector.wait_ge(turn_done[0].sem, u0 + i + 1)
                    cols = xy[:, :, i * P:(i + 1) * P]
                    vector.tensor_tensor(cols, turned(i).rearrange("p (k n) -> p k n", k=KD), cols, ALU.add)\
                        .then_inc(added[0].sem, 1)

                for i in range(TT):
                    weigh(i)
                    if i > 0:
                        add(i - 1)
                add(TT - 1)
        turn_done[0].at += TT
        added[0].at += TT

    def two(w, a=0):
        return [(s, w[a + s]) for s in range(2)]

    def chunk(j):
        return mods[:, j * KD:(j + 1) * KD, :]

    start(first_mod(0))
    modulation(0, first_gu("ffn1", 0))
    slots_zeroed()
    norm(NT, modA[:, 0], chunk(0))
    feed_forward("ffn1", 0, NT, chunk(2), two(io["w_qk"]))
    attention_tables()
    norm(NT, modA[:, 1], chunk(3))
    Qh = big[:, 0:HEADS * NX].rearrange("p (a n) -> p a n", a=HEADS)
    Kh = big[:, HEADS * NX:HEADS * (NX + NT)].rearrange("p (a n) -> p a n", a=HEADS)
    Vh = big[:, HEADS * (NX + NT):HEADS * (NX + NT) + KT * D].rearrange("p (m n) -> p m n", m=KT)
    Oh = hbuf[:, 0:HEADS * NX].rearrange("p (a n) -> p a n", a=HEADS)
    head_inputs(0, Qh, two(io["w_qk"], 4))
    head_inputs(1, Kh, two(io["w_v"]))
    values(Vh, two(io["w_o"]))
    attention(Qh, Kh, Vh, Oh)
    output_norm(Oh, subg[:, 1:2])
    project_residual(io["w_o"], Oh, chunk(5), first_gu("ffn2", 0))
    norm(NX, modA[:, 2], chunk(6))
    feed_forward("ffn2", 0, NX, chunk(8), first_mod(1))
    modulation(1, first_gu("ffn1", 1))
    norm(NX, modA[:, 0], chunk(0))
    feed_forward("ffn1", 1, NX, chunk(2), two(io["w_f"]))
    norm(NX, modA[:, 1], chunk(3))
    F = work[:, 0:KD * NX].rearrange("p (k n) -> p k n", k=KD)
    fourier(F)
    project_residual(io["w_f"], F, chunk(5), first_gu("ffn2", 1))
    norm(NX, modA[:, 2], chunk(6))
    feed_forward("ffn2", 1, NX, chunk(8), two(io["w_in"]))
    second_gains()
    norm(NX, gains2[:, 0], None)
    F = big[:, 0:16 * NX].rearrange("p (k n) -> p k n", k=16)
    G = big[:, 16 * NX:32 * NX].rearrange("p (k n) -> p k n", k=16)
    V2 = rope[:].rearrange("p a n -> p (a n)")[:, 0:12 * P].rearrange("p (t n) -> p t n", t=4)
    project(io["w_in"], 0, 2, F[:, 0:8], HD ** -0.5, ACT.Copy, two(io["w_in"], 4))
    project(io["w_in"], 4, 2, F[:, 8:16], 1.0, ACT.Copy, two(io["w_in"], 8))
    project(io["w_in"], 8, 4, G, 1.0, ACT.Sigmoid, two(io["w_ab"]))
    values_and_gates(F, V2)
    compress(F, kc_sb[:], vc_sb[:])
    Oab = hbuf[:, 0:KD * NX].rearrange("p (k n) -> p k n", k=KD)
    branches(F, V2, kc_sb[:], vc_sb[:], Oab[:, 0:4], Oab[:, 4:8])
    U = work[:, 0:KD * NX].rearrange("p (k n) -> p k n", k=KD)
    merge(Oab, G, U, two(io["w_o2"]))
    project_residual(io["w_o2"], U, None, [])
    norm(NX, gains2[:, 1], None)
    route()
    experts()
    combine()
    norm(NX, gains2[:, 2], None)
    finish(h[:, :, 0:NX], io["out"])


def slabs(w, per):
    k, m = w.shape
    w = w.reshape(k // P, P, m // P // per, per, P)
    return np.ascontiguousarray(w.transpose(2, 1, 3, 0, 4)).reshape(m // P // per, P, per * k)


def columns(v):
    v = v.reshape(v.shape[:-1] + (-1, P))
    return np.ascontiguousarray(np.moveaxis(v, -1, 0))


def layouts(a):
    L = {}
    n = np.arange(P)
    L["bones"] = (n[:, None] // HD == n[None, :] // HD).astype(np.float32)
    L["ident"] = np.eye(P, dtype=np.float32)
    L["lam"] = np.broadcast_to(np.stack([a["attn_lam_" + i][0] for i in ("q1", "k1", "q2", "k2")]), (P, 4, HD))
    L["qk_gain"] = np.stack([np.tile(a["attn_" + i + "_g"][0], 2) for i in "qk"], axis=1)
    L["sub_gain"] = a["attn_sub_g"][0][:, None]
    pairs = HD // 4
    inv_freq = np.float32(10000.0) ** (-(np.arange(pairs, dtype=np.float32) / pairs))
    tok = np.arange(NX)
    place = np.stack([tok // 64, tok % 64]).astype(np.float32)
    angle = (place[(n % HD) // 32] * inv_freq[n % pairs][:, None]).astype(np.float32)
    L["rope"] = np.stack([np.cos(angle), np.sin(angle)], axis=1).astype(np.float32)
    r = np.zeros((P, P), np.float32)
    for p in range(P):
        if (p // pairs) % 2:
            r[p, p - pairs] = -1.0
        else:
            r[p, p + pairs] = 1.0
    L["rot"] = r
    qkv = a["attn_w_qkv"][0]
    L["w_qk"] = slabs(qkv[:, 0:2 * D], 2)
    L["w_v"] = np.ascontiguousarray(qkv[:, 2 * D:].reshape(KD, P, 4, 2 * P).transpose(2, 1, 0, 3)).reshape(4, P, -1)
    L["w_o"] = slabs(a["attn_w_o"][0], 2)
    L["w_f"] = slabs(a["fourier_w"][0], 2)
    W = D // 4
    f, t = np.arange(W), np.arange(NX)
    af, at = 2 * np.pi * (np.outer(f, f) % W) / W, 2 * np.pi * (np.outer(t, t) % NX) / NX
    L["dft_feature"] = (np.concatenate([np.cos(af), np.sin(af)], 1) / np.sqrt(W)).astype(np.float32)\
        .reshape(2, P, 2 * W).transpose(1, 0, 2)
    L["dft_token"] = (np.stack([np.cos(at), -np.sin(at)]) / np.sqrt(NX)).astype(np.float32)\
        .reshape(2, NX // P, P, NX).transpose(2, 0, 1, 3)
    L["gains2"] = np.stack([columns(a[k].reshape(D)) for k in ("norm_mix_g_2", "norm_ffn_g_2", "norm_final_g_2")],
                           axis=1)[..., None]
    w = a["w_in_2"][0]
    edges = np.cumsum([0, 512, 128, 128, 128, 128, 128, 128, 24, 512, 128, 128, 2048])
    qa, kcmp, vcmp, kslc, vslc, kwin, vwin, gn, qb, kb, vb, gm = (w[:, x:y] for x, y in zip(edges[:-1], edges[1:]))

    def paired(m):
        return m.reshape(-1, 2, 4, HD).transpose(0, 2, 1, 3).reshape(-1, 8 * HD)

    def doubled(m):
        return np.repeat(m.reshape(-1, 2, 1, HD), 2, axis=2).reshape(-1, 4 * HD)

    pad = np.zeros((D, P - gn.shape[1]), np.float32)
    L["w_in"] = slabs(np.concatenate([paired(qa), paired(qb), kslc, kwin, kb, doubled(kcmp), doubled(vcmp), gn, pad, gm],
                                     axis=1), 2)
    L["w_v2"] = np.concatenate([vslc, vwin, vb], axis=1).reshape(KD, P, 3 * P).transpose(1, 0, 2)
    L["w_ab"] = slabs(np.concatenate([paired(a[k][0].T).T for k in ("w_a_2", "w_b_2")], axis=0), 2)
    L["w_o2"] = slabs(a["w_o_2"][0], 2)
    LP = CMP_LEN // 2
    L["cmp_w1"] = np.stack([a[f"cmp_w1_{v}_2"][0].reshape(LP, P, CMP_HIDDEN).transpose(1, 0, 2) for v in "kv"], axis=1)
    L["cmp_w2"] = np.stack([a[f"cmp_w2_{v}_2"][0].reshape(2, P, HD).transpose(1, 0, 2) for v in "kv"], axis=1)
    pos = np.stack([a[f"cmp_pos_{v}_2"][0].reshape(LP, P).T for v in "kv"], axis=1)
    L["cmp_pos"] = np.repeat(pos[..., None], CMP_BLOCKS, axis=3)
    p = np.arange(P)[:, None]

    def distances(before, window):
        d = before + p - np.arange(before + P)[None, :]
        return np.where((d >= 0) & (d < window), d, 1e35)

    L["dist"] = np.concatenate([distances(NX - P, NX), distances(NSA_WINDOW, NSA_WINDOW),
                                distances(SWA_WINDOW, SWA_WINDOW)], axis=1).astype(np.float32)
    end = np.arange(CMP_BLOCKS) * CMP_STRIDE + CMP_LEN - 1
    dc = (np.arange(4)[None, :, None] * P + p[:, :, None]) - end
    L["dist_cmp"] = np.where(dc >= 0, dc, 1e35).astype(np.float32)
    slope = 2.0 ** (-8.0 * np.arange(1, 17) / 16)
    L["slopes"] = np.broadcast_to(-np.concatenate([slope[8:], slope[:8]]).astype(np.float32), (P, 16))
    L["sinks"] = np.broadcast_to(a["sinks_2"][0], (P, 8))
    L["w_route"] = np.concatenate([a["w_group_2"][0], a["w_expert_2"][0]], axis=1).reshape(KD, P, -1).transpose(1, 0, 2)
    L["b_route"] = np.broadcast_to(np.concatenate([a["b_group_2"][0], a["b_expert_2"][0]]), (P, GROUPS + EXPERTS))
    L["rev"] = np.broadcast_to(np.arange(EXPERTS, 0, -1, dtype=np.float32), (P, EXPERTS))
    FE = 2
    gu = np.stack([a["w_gate_e_2"][0], a["w_up_e_2"][0]], axis=1)
    gu = gu.reshape(EXPERTS, 2, KD, P, FE, P).transpose(0, 4, 3, 1, 2, 5).reshape(EXPERTS, FE, P, 2 * KD * P)
    dn = a["w_down_e_2"][0].reshape(EXPERTS, FE, P, D).transpose(0, 2, 1, 3).reshape(EXPERTS, 1, P, FE * D)
    L["w_exp"] = np.concatenate([gu, dn], axis=1).transpose(0, 2, 1, 3).reshape(EXPERTS, P, 3 * 2 * KD * P)
    L["expert_base"] = np.broadcast_to(P * np.arange(EXPERTS, dtype=np.float32), (P, EXPERTS))
    L["block_numbers"] = np.broadcast_to(np.arange(MOE_BLOCKS + 1, dtype=np.float32), (P, MOE_BLOCKS + 1))
    L["before"] = np.triu(np.ones((P, P), np.float32), 1)
    cols = np.concatenate([a["x"][0], a["ctx"][0]]).T
    L["xy"] = cols.reshape(KD, P, NT).transpose(1, 0, 2)
    L["cond"] = np.stack([a["c"][0], a["c_ctx"]]).reshape(2, KD, P).transpose(2, 1, 0)
    L["w_mod"] = np.stack([slabs(w, 2) for w in a["w_mod"]])
    b = a["b_mod"].reshape(2, NMOD * KD, P).transpose(0, 2, 1)
    L["b_mod"] = np.repeat(b[..., None], 2, axis=3)
    g = a["norm_g"].reshape(2, 3 * KD, P).transpose(0, 2, 1)
    L["norm_g"] = np.repeat(g[..., None], 2, axis=3)
    for n in ("ffn1", "ffn2"):
        gu = a[n + "_w_gu"].reshape(2, KD, P, 2, KF, P)
        L[n + "_gu"] = np.ascontiguousarray(gu.transpose(0, 4, 2, 3, 1, 5)).reshape(2, KF, P, 2 * KD * P)
        L[n + "_d"] = np.stack([slabs(w, 1) for w in a[n + "_w_d"]])
    return L


def kernel(**inputs):
    import concourse.bacc as bacc
    from concourse.bass_utils import run_bass_kernel_spmd

    nc = bacc.Bacc("TRN2", target_bir_lowering=False, num_devices=1)
    arrays, io = {}, {}
    for name, a in layouts({k: np.asarray(v) for k, v in inputs.items()}).items():
        arrays[f"in_{name}"] = np.ascontiguousarray(a)
        io[name] = nc.dram_tensor(f"in_{name}", a.shape, F32, kind="ExternalInput").ap()
    for name in ("slots", "slots_out"):
        io[name] = nc.dram_tensor(name, (MOE_BLOCKS * P, D), F32, kind="Internal").ap()
    io["out"] = nc.dram_tensor("out", (P, KD, NX), F32, kind="ExternalOutput").ap()
    program(nc, io)
    r = run_bass_kernel_spmd(nc, [arrays], core_ids=[0])
    return r.results[0]["out"].transpose(2, 1, 0).reshape(1, NX, D)
```

```python
from contextlib import ExitStack

import numpy as np

import concourse.bass as bass
from concourse import mybir

F32 = mybir.dt.float32
F32R = mybir.dt.float32r
ALU = mybir.AluOpType
ACT = mybir.ActivationFunctionType
AX_X = mybir.AxisListType.X
ds = bass.ds

P = 128
D = 1024
KD = D // P
NX = 512
NY = 256
NT = NX + NY
FF = 2816
KF = FF // P
NMOD = 9
EPS = 1e-6
CMP_LEN, CMP_STRIDE, CMP_HIDDEN = 32, 16, 256
CMP_BLOCKS = NX // CMP_STRIDE - CMP_LEN // CMP_STRIDE + 1
NSA_WINDOW, SWA_WINDOW = 256, 128
EXPERTS, GROUPS = 32, 4
MOE_BLOCKS = EXPERTS + 2 * NX // P - 1
HEADS = 8
HD = 64
KT = NT // P
LAMBDA_INIT = 0.2
SLOTS = 3
SLOT = 2 * KD * P
FF_PARTS = ((6, 6, 6, 4), (12, 10))


class Count:

    def __init__(self, ctx, nc, name):
        self.sem = ctx.enter_context(nc.semaphore(name))
        self.at = 0


class Ring:

    def __init__(self, ctx, nc):
        self.buf = ctx.enter_context(nc.sbuf_tensor("weights", [P, SLOTS, SLOT], F32))
        self.landed = [ctx.enter_context(nc.semaphore(f"slab_landed{s}")) for s in range(SLOTS)]
        self.used = [ctx.enter_context(nc.semaphore(f"slab_used{s}")) for s in range(SLOTS)]
        self.n = [0] * SLOTS

    def view(self, s, *dims):
        size = int(np.prod(dims))
        names = "abcd"[:len(dims)]
        flat = self.buf[:, s, 0:size]
        if len(dims) == 1:
            return flat
        return flat.rearrange(f"p ({' '.join(names)}) -> p {' '.join(names)}",
                              **{a: n for a, n in zip(names, dims)})


def program(nc, io):
    with ExitStack() as ctx:
        build(nc, io, ctx)


def build(nc, io, ctx):
    def sb(name, shape, at=ctx, dtype=F32):
        return at.enter_context(nc.sbuf_tensor(name, shape, dtype))

    def count(name):
        return Count(ctx, nc, name)

    ring = Ring(ctx, nc)
    ps = ctx.enter_context(nc.psum_tensor("ps", [P, 8, 512], F32))

    xy = sb("xy", [P, KD, NT])
    ones = sb("ones", [P, P])
    eps = sb("eps", [P, 1])
    mods = [sb(f"mods{i}", [P, NMOD * KD, 2 - i]) for i in range(2)]
    mod_gain = [sb(f"mod_gain{i}", [P, 3, KD, 2 - i]) for i in range(2)]
    bmod = sb("bmod", [P, NMOD * KD, 2])
    normg = sb("normg", [P, 3 * KD, 2])
    mod_sum = sb("mod_sum", [P, 2, 3, 2])
    tmp = sb("tmp", [P, 2, NT])
    rstd = tmp[:, 1, :]

    bones = sb("bones", [P, P])
    ident = sb("ident", [P, P])
    rot = sb("rot", [P, 3, P])
    qkg = sb("qkg", [P, 2])
    lamt = sb("lamt", [P, 8])
    subg = sb("subg", [P, 2])
    stat = sb("stat", [P, 2, 8])
    gains2 = sb("gains2", [P, 3, KD, 1])
    dist = tmp[:].rearrange("p a n -> p (a n)")[:, 0:1152]
    dist_c = sb("dist_c", [P, 4, CMP_BLOCKS])
    slopes = sb("slopes", [P, 16])
    sinks = sb("sinks", [P, 8])
    gates = sb("gates", [P, HEADS, 3, 4])
    stat2 = sb("stat2", [P, 2, 4, 16])
    kc_sb = sb("kc", [P, CMP_BLOCKS])
    vc_sb = sb("vc", [CMP_BLOCKS, 2, HD])

    dest = ctx.enter_context(nc.sbuf_tensor("dest", [P, 2 * NX // P], mybir.dt.uint32))
    share = sb("share", [P, 2, NX // P])
    block_expert = ctx.enter_context(nc.sbuf_tensor("block_expert", [1, MOE_BLOCKS + 1], mybir.dt.int32))

    def wset(s):
        if s == 0:
            return ring.buf[:, :, 0:2 * KD * P]
        return big[:, 4 * D + (s - 1) * 6 * D:4 * D + s * 6 * D].rearrange("p (a n) -> p a n", a=3)

    def xin(s):
        return work[:, 6 * D + s * D:7 * D + s * D]

    hbuf = h = big = work = rope = mod_w = cond_row = None

    def stage_buffers(tag, which=("big", "work"), own=None):
        nonlocal hbuf, h, big, work, rope, mod_w, cond_row
        own = ExitStack() if own is None else own
        if "big" in which:
            big = sb("big" + tag, [P, 16 * D], own)
            rope = sb("rope" + tag, [P, 4, NX], own)
        if "work" not in which:
            return own
        hbuf = sb("hbuf" + tag, [P, KD * NT], own)
        h = hbuf[:].rearrange("p (k n) -> p k n", k=KD)
        work = sb("work" + tag, [P, 12 * NT], own)
        mod_w = [work[:, b * 3 * D:(b + 1) * 3 * D].rearrange("p (a k) -> p a k", a=3) for b in range(2)]
        cond_row = work[:, 6 * D:8 * D].rearrange("p (c k) -> p c k", c=2)
        return own

    loaded = count("inputs_loaded")
    tables = count("tables_landed")
    proj_done = [count(f"head_product{s}") for s in range(2)]
    raw_done = [count(f"head_copied{s}") for s in range(2)]
    hss_done = [count(f"head_square_sums{s}") for s in range(2)]
    hroot = [count(f"head_roots{s}") for s in range(2)]
    t1_done = [count(f"rope_cos_part{s}") for s in range(2)]
    head_done = [count(f"head_normalised{s}") for s in range(2)]
    staged = [count(f"head_staged{s}") for s in range(2)]
    score_done = [count(f"scores{s}") for s in range(2)]
    max_done = [count(f"score_max{s}") for s in range(2)]
    exp_done = [count(f"exponentials{s}") for s in range(2)]
    prob_done = [count(f"probabilities{s}") for s in range(2)]
    turn_done = [count(f"turned{s}") for s in range(2)]
    turn_ev = [count(f"turned_copied{s}") for s in range(2)]
    pv_done = [count(f"values_product{s}") for s in range(2)]
    o_done = [count(f"output_copied{s}") for s in range(2)]
    const_set = count("constants_set")
    silu_done = count("condition_silu")
    mod_landed = [count(f"mod_weights_landed{b}") for b in range(2)]
    mod_summed = count("mod_sums")
    mod_used = [count(f"mod_stored{b}") for b in range(2)]
    small_landed = count("mod_tables_landed")
    dve_chain = count("vector_step")
    sq_done = count("squares")
    ss_done = count("square_sums")
    root_done = count("roots")
    rstd_done = count("inverse_roots")
    scaled = count("scaled")
    shifted = count("shifted")
    silu_g = [count(f"gate_silu{s}") for s in range(2)]
    act_done = [count(f"hidden{s}") for s in range(2)]
    down_done = [count(f"down_product{s}") for s in range(2)]
    added = [count(f"residual_added{s}") for s in range(2)]
    out_done = count("out_stored")
    high_done = [count(f"weights_high_part{s}") for s in range(2)]
    slab_done = [count(f"slab_product{s}") for s in range(2)]
    hidden_high = [count(f"hidden_high_part{s}") for s in range(2)]
    hidden_low = [count(f"hidden_low_part{s}") for s in range(2)]
    in_high = count("input_high_part")
    in_low = count("input_low_part")
    room_act = count("hidden_room_found")
    zeroed = count("slots_zeroed")
    counted = count("assignments_counted")
    scattered = count("tokens_scattered")
    gathered = [count(f"results_gathered{i}") for i in range(NX // P)]
    x_landed = [count(f"block_rows_landed{s}") for s in range(3)]
    set_landed = [count(f"expert_weights_landed{s}") for s in range(3)]
    rows_turned = count("block_rows_turned")
    rows_by_act = count("block_rows_copied_by_scalar")
    rows_by_vec = count("block_rows_copied_by_vector")
    hidden_mm = count("expert_gate_and_up_products")
    gate_done = count("expert_gate_silu")
    hidden_done = count("expert_hidden")
    y_mm = count("expert_down_products")
    y_by_act = count("block_result_copied_by_scalar")
    y_by_vec = count("block_result_copied_by_vector")
    y_stored = [count(f"block_result_stored{s}") for s in range(3)]
    room = count("staging_room_found")

    def step(ins):
        ins.then_inc(dve_chain.sem, 1)
        dve_chain.at += 1

    def steps_done(eng):
        eng.wait_ge(dve_chain.sem, dve_chain.at)

    def prefetch(sync, first, used):
        for s, src in first:
            sync.wait_ge(ring.used[s], used[s])
            sync.dma_start(ring.buf[:, s, 0:src.shape[1]], src).then_inc(ring.landed[s], 16)

    def first_gu(name, i):
        return [(s, io[name + "_gu"][i, s]) for s in range(2)]

    def open_counts(eng, counts):
        for c in counts:
            eng.sem_inc(c.sem, 1)
            c.at = 1

    mod_product = ps[:, 6:8, :].rearrange("p b n -> p (b n)")

    def load_mod(sync, i, b, tile, n):
        sync.dma_start(mod_w[b][:, 0:n], io["w_mod"][i, ds(tile, n)].rearrange("a p k -> p a k"))\
            .then_inc(mod_landed[b].sem, 16)

    def sum_mod(vector, i, b, tile, n, landed, sums):
        conds = 2 - i
        vector.wait_ge(mod_landed[b].sem, landed)
        for j in range(n):
            for c in range(conds):
                last = c == conds - 1
                if not last:
                    vector.wait_ge(mod_summed.sem, sums - n * conds + j * conds)
                vector.tensor_tensor_reduce(mod_w[b][:, j, :] if last else mod_product, mod_w[b][:, j, :],
                                            cond_row[:, c, :], 1.0, 0.0, ALU.mult, ALU.add,
                                            mod_sum[:, b, j, c:c + 1]).then_inc(mod_summed.sem, 1)
        vector.wait_ge(mod_summed.sem, sums)
        at = ds(tile, n)
        vector.tensor_tensor(mods[i][:, at, :], mod_sum[:, b, 0:n, 0:conds], bmod[:, at, 0:conds], ALU.add)\
            .then_inc(mod_used[b].sem, 1)

    def gains_of_mods(vector, i, norms, gates):
        for b in range(2):
            vector.wait_ge(mod_used[b].sem, mod_used[b].at)
        for j in norms:
            a = (3 * j + 1) * KD
            step(vector.scalar_tensor_tensor(mod_gain[i][:, j], mods[i][:, a:a + KD, :], 1.0,
                                             normg[:, j * KD:(j + 1) * KD, 0:2 - i], ALU.add, ALU.mult))
        halve(vector, i, gates)

    def halve(vector, i, gates):
        for j in gates:
            g = mods[i][:, j * KD:(j + 1) * KD, :]
            step(vector.tensor_scalar(g, g, 0.5, None, ALU.mult))
        steps_done(vector)

    MOD_TURN = ((3, 2), (3, 3))
    MOD_BEFORE = [NMOD * KD - KF // 2 * sum(n) for n in MOD_TURN]

    def mod_groups(i):
        return [(g % 2, 3 * g, min(3, MOD_BEFORE[i] - 3 * g)) for g in range(-(-MOD_BEFORE[i] // 3))]

    def sum_first_mods(vector, i):
        for b, tile, n in mod_groups(i):
            mod_landed[b].at += 16
            mod_summed.at += n * (2 - i)
            sum_mod(vector, i, b, tile, n, mod_landed[b].at, mod_summed.at)
            mod_used[b].at += 1

    def start(nxt):
        with nc.Block() as block:
            @block.sync
            def _(sync):
                sync.dma_start(cond_row, io["cond"]).then_inc(loaded.sem, 16)
                groups = mod_groups(0)
                for g, (b, tile, n) in enumerate(groups):
                    if g >= 2:
                        sync.wait_ge(mod_used[b].sem, g // 2)
                    load_mod(sync, 0, b, tile, n)
                    if g == 1:
                        sync.dma_start(bmod[:], io["b_mod"][0]).then_inc(small_landed.sem, 16)
                        sync.dma_start(normg[:], io["norm_g"][0]).then_inc(small_landed.sem, 16)
                sync.dma_start(xy[:], io["xy"]).then_inc(loaded.sem, 16)
                prefetch(sync, nxt, ring.n)
                sync.wait_ge(loaded.sem, 32)

            @block.tensor
            def _(pe):
                open_counts(pe, pv_done + turn_done + proj_done + score_done + slab_done)

            @block.vector
            def _(vector):
                vector.memset(ones[:], 1.0).then_inc(const_set.sem, 1)
                vector.memset(eps[:], EPS).then_inc(const_set.sem, 1)
                open_counts(vector, [rows_by_act, rows_by_vec, y_by_act, y_by_vec] + y_stored)
                open_counts(vector, hidden_low + act_done + added + head_done + prob_done + o_done)
                vector.wait_ge(silu_done.sem, 1)
                vector.wait_ge(small_landed.sem, 32)
                sum_first_mods(vector, 0)
                gains_of_mods(vector, 0, (0,), ())

            @block.scalar
            def _(scalar):
                open_counts(scalar, raw_done + exp_done + turn_ev)
                scalar.wait_ge(loaded.sem, 16)
                scalar.activation(cond_row, cond_row, ACT.Silu).then_inc(silu_done.sem, 1)
        loaded.at = 32
        small_landed.at = 32
        silu_done.at = 1

    def norm(block, cols, gain, shift, loads=()):
        s0, q0, r0, i0, c0, f0 = (c.at for c in (sq_done, ss_done, root_done, rstd_done, scaled, shifted))
        sq = big[:, 0:KD * NT].rearrange("p (k n) -> p k n", k=KD)
        parts = [(0, NX, 0), (NX, NY, 1)][:1 if cols == NX else 2]
        @block.sync
        def _(sync):
            for dst, src, landed in loads:
                sync.dma_start(dst, src).then_inc(landed.sem, 16)

        @block.scalar
        def _(scalar):
            for k in range(KD):
                scalar.activation(sq[:, k, 0:cols], xy[:, k, 0:cols], ACT.Square).then_inc(sq_done.sem, 1)
            scalar.wait_ge(ss_done.sem, q0 + 1)
            for a, n, c in parts:
                scalar.activation(tmp[:, 0, a:a + n], ps[:, c, 0:n], ACT.Sqrt, bias=eps[:, 0:1],
                                  scale=1.0 / D).then_inc(root_done.sem, 1)
            if shift is not None:
                for k in range(KD):
                    for a, n, c in parts:
                        scalar.wait_ge(scaled.sem, c0 + k * len(parts) + c + 1)
                        scalar.activation(h[:, k, a:a + n], h[:, k, a:a + n], ACT.Identity,
                                          bias=shift[:, k, c:c + 1]).then_inc(shifted.sem, 1)
                scalar.wait_ge(shifted.sem, f0 + KD * len(parts))

        @block.tensor
        def _(pe):
            pe.wait_ge(const_set.sem, 2)
            for k in range(KD):
                pe.wait_ge(sq_done.sem, s0 + k + 1)
                for a, n, c in parts:
                    mm = pe.matmul(ps[:, c, 0:n], ones[:], sq[:, k, a:a + n],
                                   start=(k == 0), stop=(k == KD - 1))
            mm.then_inc(ss_done.sem, 1)

        @block.vector
        def _(vector):
            vector.wait_ge(root_done.sem, r0 + len(parts))
            vector.reciprocal(rstd[:, 0:cols], tmp[:, 0, 0:cols]).then_inc(rstd_done.sem, 1)
            vector.wait_ge(rstd_done.sem, i0 + 1)
            for k in range(KD):
                for a, n, c in parts:
                    vector.scalar_tensor_tensor(h[:, k, a:a + n], xy[:, k, a:a + n], gain[:, k, c:c + 1],
                                                rstd[:, a:a + n], ALU.mult, ALU.mult)\
                        .then_inc(scaled.sem, 1)
            vector.wait_ge(scaled.sem, c0 + KD * len(parts))
        sq_done.at += KD
        ss_done.at += 1
        root_done.at += len(parts)
        rstd_done.at += 1
        scaled.at += KD * len(parts)
        if shift is not None:
            shifted.at += KD * len(parts)

    def split_ahead(eng, phases, split, item, before=None):
        for j, ph in enumerate(phases):
            turns = ph[1]
            if before is not None:
                before(j)
            with eng.Fori(0, turns - 1) as t:
                split(ph, t, 1)
                item(ph, t, 0)
                split(ph, t + 1, 0)
                item(ph, t, 1)
            split(ph, turns - 1, 1)
            item(ph, turns - 1, 0)
            if j + 1 < len(phases):
                split(phases[j + 1], 0, 0)
            item(ph, turns - 1, 1)

    STREAMS = ((0, NX), (NX, NY))

    def feed_forward(name, i, cols, gain, shift, gate, nxt, mod=None, zero_slots=False):
        nonlocal mod_w, cond_row
        tag = f"_{name}_{i}"
        own = ExitStack()
        h_high, h_low = (sb(f"h_{p}{tag}", [P, KD, cols], own, F32R) for p in ("high", "low"))
        scratch = sb("scratch" + tag, [P, 7 * D], own)
        full = scratch[:, 0:KD * cols].rearrange("p (k n) -> p k n", k=KD)
        streams = STREAMS[:2 if cols > NX else 1]
        ns = len(streams)
        cuts = FF_PARTS[2 - ns]
        a_high, a_low = (sb(f"hidden_{p}{tag}", [P, cuts[0], cols], own, F32R) for p in ("high", "low"))
        w_high, w_low = (sb(f"weights_{p}{tag}", [P, 2, SLOT], own, F32R) for p in ("high", "low"))
        dturns = KD // 2
        phases = []
        n = first = 0
        for c, tiles in enumerate(cuts):
            phases.append(("gate_up", tiles // 2, n, first // 2, tiles, io[name + "_gu"], first, (0, SLOT)))
            n += tiles // 2
            phases.append(("down", dturns, n, c * dturns, tiles, io[name + "_d"], 0, (first * P, (first + tiles) * P)))
            n += dturns
            first += tiles
        slabs_of_slot = n
        n0 = list(ring.n)
        names = (high_done, slab_done, silu_g, act_done, hidden_high, hidden_low, added)
        b0, c0, s0, a0, e0, o0, r0 = ([c.at for c in cs] for cs in names)
        if mod is not None:
            conds, per = 2 - mod, sum(MOD_TURN[mod])
            at = [0, MOD_TURN[mod][0] * D, per * D, (per + conds) * D]
            mod_w = [scratch[:, at[b]:at[b + 1]].rearrange("p (a k) -> p a k", k=D) for b in range(2)]
            cond_row = scratch[:, at[2]:at[3]].rearrange("p (c k) -> p c k", k=D)
            first_tile = 0 if mod else MOD_BEFORE[0]
            w0 = [c.at for c in mod_used]
            l0 = [c.at for c in mod_landed]
            m0 = mod_summed.at
            t0, k0 = small_landed.at, silu_done.at
            mod_turns = KF // 2 + mod
        if zero_slots:
            fills = 6
            zeros = scratch[:, 0:MOE_BLOCKS * D // fills]
        norm_names = (sq_done, ss_done, root_done, rstd_done, scaled, in_high, in_low)
        q0, u0, y0, i0, z0, h0, j0 = (c.at for c in norm_names)

        def mod_turn(ph):
            return ph[3] + (mod if ph[2] > 0 else 0)

        def load_mod_turn(sync, b, u):
            load_mod(sync, mod, b, u * per + (first_tile + 3 * b), MOD_TURN[mod][b])

        def sum_mod_turn(vector, b, u):
            n, before = MOD_TURN[mod][b], 3 * b
            sum_mod(vector, mod, b, u * per + (first_tile + before), n, u * 16 + (l0[b] + 16),
                    u * (per * conds) + (m0 + (before + n) * conds))

        def gate_up(s, j, c):
            return ps[:, 3 * s + j, :] if c == 0 else ps[:, 3 * s + 2, j * NY:(j + 1) * NY]

        def down(s, c):
            return ps[:, 3 * s + 2, :] if ns == 1 else ps[:, 3 * s + c, 0:streams[c][1]]

        with nc.Block() as block:
            @block.sync
            def _(sync):
                if mod is not None:
                    sync.wait_ge(in_low.sem, j0 + KD * ns)
                    sync.dma_start(cond_row, io["cond"][:, 0:conds, :]).then_inc(small_landed.sem, 16)
                    sync.dma_start(bmod[:], io["b_mod"][mod]).then_inc(small_landed.sem, 16)
                    sync.dma_start(normg[:], io["norm_g"][mod]).then_inc(small_landed.sem, 16)
                for j, ph in enumerate(phases):
                    kind, turns, n1, turn0, tiles, w, slab0, (left, right) = ph
                    if mod is not None and (kind == "gate_up" or (mod and j == 1)):
                        u = mod_turn(ph) if kind == "gate_up" else phases[0][1]
                        for b in range(2):
                            sync.wait_ge(mod_used[b].sem, w0[b] + u)
                            load_mod_turn(sync, b, u)
                    with sync.Fori(0, turns - 1) as t:
                        for s in range(2):
                            sync.wait_ge(ring.used[s], t + (n0[s] + n1 + 1))
                            slab = w[i, ds(t * 2 + (slab0 + 2 + s), 1), :, left:right].rearrange("a p n -> (a p) n")
                            sync.dma_start(ring.buf[:, s, 0:right - left], slab).then_inc(ring.landed[s], 16)
                            if mod is not None and kind == "gate_up":
                                sync.wait_ge(mod_used[s].sem, t + (w0[s] + mod_turn(ph) + 1))
                                load_mod_turn(sync, s, t + (mod_turn(ph) + 1))
                    if j + 1 < len(phases):
                        w, slab0, (left, right) = phases[j + 1][5:8]
                        prefetch(sync, [(s, w[i, slab0 + s, :, left:right]) for s in range(2)],
                                 [n + n1 + turns for n in n0])
                prefetch(sync, nxt, [n + slabs_of_slot for n in n0])

            @block.gpsimd
            def _(gpsimd):
                if zero_slots:
                    gpsimd.wait_ge(in_low.sem, j0 + KD * ns)
                    gpsimd.memset(zeros, 0.0).then_inc(const_set.sem, 1)
                    gpsimd.wait_ge(const_set.sem, 3)
                    slots = io["slots"].rearrange("a n -> (a n)").rearrange("(j p n) -> j p n", j=fills, p=P)
                    for j in range(fills):
                        gpsimd.wait_ge(slab_done[0].sem, c0[0] + j + 1)
                        gpsimd.dma_start(slots[j], zeros).then_inc(zeroed.sem, 16)
                    gpsimd.wait_ge(zeroed.sem, 16 * fills)

            @block.tensor
            def _(pe):
                def three(out, w_at, x_at, n, ready=None):
                    for k in range(n):
                        if ready is not None:
                            ready(k)
                        wh, wl = w_at(w_high, k), w_at(w_low, k)
                        xh, xl = x_at(k)
                        pe.matmul(out, wh, xh, start=(k == 0), stop=False)
                        pe.matmul(out, wh, xl, start=False, stop=False)
                        mm = pe.matmul(out, wl, xh, start=False, stop=(k == n - 1))
                    return mm

                def slab(ph, t, s, first):
                    kind, turns, n1, turn0, tiles = ph[:5]

                    def input_ready(k):
                        pe.wait_ge(in_low.sem, j0 + (k + 1) * ns)

                    def hidden_ready(f):
                        if f in (0, tiles - 2, tiles - 1):
                            b = 1 if f == tiles - 1 else 0
                            pe.wait_ge(hidden_low[b].sem, o0[b] + n1 - turn0 - (1 if f == 0 else 0))
                        if f == 0:
                            pe.wait_ge(hidden_low[1].sem, o0[1] + n1 - turn0 - 1)

                    pe.wait_ge(ring.used[s], t + (n0[s] + n1 + 1))
                    if kind == "gate_up":
                        pe.wait_ge(act_done[s].sem, t * ns + (a0[s] + turn0 * ns))
                        for j in range(2):
                            for c, (a, n) in enumerate(streams):
                                mm = three(gate_up(s, j, c), lambda w, k: w[:, s, (j * KD + k) * P:(j * KD + k + 1) * P],
                                           lambda k: (h_high[:, k, a:a + n], h_low[:, k, a:a + n]), KD,
                                           input_ready if first and n1 == 0 and j == c == 0 else None)
                    else:
                        pe.wait_ge(added[s].sem, t * ns + (r0[s] + turn0 * ns))
                        for c, (a, n) in enumerate(streams):
                            mm = three(down(s, c), lambda w, f: w[:, s, f * P:(f + 1) * P],
                                       lambda f: (a_high[:, f, a:a + n], a_low[:, f, a:a + n]), tiles,
                                       hidden_ready if first and c == 0 else None)
                    mm.then_inc(slab_done[s].sem, 1)

                pe.wait_ge(const_set.sem, 2)
                for k in range(KD):
                    pe.wait_ge(sq_done.sem, q0 + k + 1)
                    for c, (a, n) in enumerate(streams):
                        mm = pe.matmul(ps[:, 6 + c, 0:n], ones[:], full[:, k, a:a + n], start=(k == 0), stop=(k == KD - 1))
                mm.then_inc(ss_done.sem, 1)
                for ph in phases:
                    kind, turns, n1, turn0 = ph[:4]
                    for s in range(2):
                        if ns > 1 and kind == "gate_up" and n1 > 0:
                            pe.wait_ge(added[s].sem, r0[s] + (n1 - turn0) * ns)
                        elif ns > 1 and kind == "down":
                            pe.wait_ge(act_done[s].sem, a0[s] + (n1 - turn0) * ns)
                    slab(ph, 0, 0, True)
                    slab(ph, 0, 1, False)
                    with pe.Fori(1, turns) as t:
                        for s in range(2):
                            slab(ph, t, s, False)

            @block.scalar
            def _(scalar):
                def split(ph, t, s):
                    n = ph[7][1] - ph[7][0]
                    scalar.wait_ge(ring.landed[s], t * 16 + 16 * (n0[s] + ph[2] + 1))
                    scalar.wait_ge(slab_done[s].sem, t + (c0[s] + ph[2]))
                    scalar.activation(w_high[:, s, 0:n], ring.buf[:, s, 0:n], ACT.Copy).then_inc(high_done[s].sem, 1)

                def item(ph, t, s):
                    kind, turn0 = ph[0], ph[3]
                    if kind == "gate_up":
                        scalar.wait_ge(slab_done[s].sem, t + (c0[s] + ph[2] + 1))
                        scalar.wait_ge(hidden_low[s].sem, t + (o0[s] + turn0))
                        for c, (a, n) in enumerate(streams):
                            scalar.activation(tmp[:, s, a:a + n], gate_up(s, 0, c), ACT.Silu).then_inc(silu_g[s].sem, 1)
                        scalar.wait_ge(act_done[s].sem, t * ns + (a0[s] + (turn0 + 1) * ns))
                        scalar.sem_inc(room_act.sem, 1)
                        scalar.activation(a_high[:, ds(t * 2 + s, 1), :].rearrange("p a n -> p (a n)"),
                                          tmp[:, s, 0:cols], ACT.Copy).then_inc(hidden_high[s].sem, 1)

                def before(j):
                    if j == 0 and mod is not None:
                        scalar.wait_ge(small_landed.sem, t0 + 48)
                        scalar.activation(cond_row, cond_row, ACT.Silu).then_inc(silu_done.sem, 1)

                for k in range(KD):
                    scalar.activation(full[:, k, :], xy[:, k, 0:cols], ACT.Square).then_inc(sq_done.sem, 1)
                split(phases[0], 0, 0)
                scalar.wait_ge(ss_done.sem, u0 + 1)
                for c, (a, n) in enumerate(streams):
                    scalar.activation(tmp[:, 0, a:a + n], ps[:, 6 + c, 0:n], ACT.Sqrt, bias=eps[:, 0:1],
                                      scale=1.0 / D).then_inc(root_done.sem, 1)
                for k in range(KD):
                    for c, (a, n) in enumerate(streams):
                        scalar.wait_ge(scaled.sem, z0 + k * ns + c + 1)
                        scalar.activation(h_high[:, k, a:a + n], full[:, k, a:a + n], ACT.Identity,
                                          bias=shift[:, k, c:c + 1]).then_inc(in_high.sem, 1)
                split_ahead(scalar, phases, split, item, before)

            @block.vector
            def _(vector):
                def split(ph, t, s):
                    n = ph[7][1] - ph[7][0]
                    vector.wait_ge(high_done[s].sem, t + (b0[s] + ph[2] + 1))
                    vector.tensor_tensor(w_low[:, s, 0:n], ring.buf[:, s, 0:n], w_high[:, s, 0:n].bitcast(F32),
                                         ALU.subtract).then_inc(ring.used[s], 1)

                def item(ph, t, s):
                    kind, turn0 = ph[0], ph[3]
                    if kind == "gate_up":
                        for c, (a, n) in enumerate(streams):
                            vector.wait_ge(silu_g[s].sem, t * ns + (s0[s] + turn0 * ns + c + 1))
                            vector.tensor_tensor(tmp[:, s, a:a + n], gate_up(s, 1, c), tmp[:, s, a:a + n], ALU.mult)\
                                .then_inc(act_done[s].sem, 1)
                        vector.wait_ge(hidden_high[s].sem, t + (e0[s] + turn0 + 1))
                        at = ds(t * 2 + s, 1)
                        vector.tensor_tensor(a_low[:, at, :].rearrange("p a n -> p (a n)"), tmp[:, s, 0:cols],
                                             a_high[:, at, :].rearrange("p a n -> p (a n)").bitcast(F32), ALU.subtract)\
                            .then_inc(hidden_low[s].sem, 1)
                        if mod is not None:
                            sum_mod_turn(vector, s, t + mod_turn(ph))
                    else:
                        vector.wait_ge(slab_done[s].sem, t + (c0[s] + ph[2] + 1))
                        for c, (a, n) in enumerate(streams):
                            x = xy[:, ds(t * 2 + s, 1), a:a + n].rearrange("p a n -> p (a n)")
                            g = gate[:, ds(t * 2 + s, 1), c:c + 1].rearrange("p a n -> p (a n)")
                            vector.scalar_tensor_tensor(x, down(s, c), g, x, ALU.mult, ALU.add)\
                                .then_inc(added[s].sem, 1)

                def before(j):
                    if j == 0 and mod is not None:
                        vector.wait_ge(silu_done.sem, k0 + 1)
                    if j == 1 and mod == 0:
                        for s in range(2):
                            vector.wait_ge(mod_used[s].sem, w0[s] + phases[0][1])
                        halve(vector, 0, (2,))
                    if j == 2 and mod == 1:
                        for s in range(2):
                            sum_mod_turn(vector, s, phases[0][1])

                split(phases[0], 0, 0)
                vector.wait_ge(root_done.sem, y0 + ns)
                vector.reciprocal(rstd[:, 0:cols], tmp[:, 0, 0:cols]).then_inc(rstd_done.sem, 1)
                vector.wait_ge(rstd_done.sem, i0 + 1)
                for k in range(KD + 1):
                    for c, (a, n) in enumerate(streams):
                        if k < KD:
                            vector.scalar_tensor_tensor(full[:, k, a:a + n], xy[:, k, a:a + n], gain[:, k, c:c + 1],
                                                        rstd[:, a:a + n], ALU.mult, ALU.mult).then_inc(scaled.sem, 1)
                    for c, (a, n) in enumerate(streams):
                        if k > 0:
                            done = (k - 1) * ns + c + 1
                            vector.wait_ge(scaled.sem, z0 + done)
                            vector.wait_ge(in_high.sem, h0 + done)
                            vector.scalar_tensor_tensor(h_low[:, k - 1, a:a + n], full[:, k - 1, a:a + n],
                                                        shift[:, k - 1, c:c + 1], h_high[:, k - 1, a:a + n].bitcast(F32),
                                                        ALU.add, ALU.subtract).then_inc(in_low.sem, 1)
                vector.wait_ge(in_low.sem, j0 + KD * ns)
                split_ahead(vector, phases, split, item, before)
                for s in range(2):
                    vector.wait_ge(added[s].sem, r0[s] + len(cuts) * dturns * ns)
                if mod is not None:
                    for s in range(2):
                        mod_landed[s].at += 16 * mod_turns
                        mod_used[s].at += mod_turns
                    mod_summed.at += mod_turns * per * conds
                    gains_of_mods(vector, mod, *(((1, 2), (8,)) if mod == 0 else ((0, 1, 2), (2, 8))))
        if mod is not None:
            small_landed.at += 48
            silu_done.at += 1
        for c, n in zip(norm_names, (KD, 1, ns, 1, KD * ns, KD * ns, KD * ns)):
            c.at += n
        for s in range(2):
            ring.n[s] += slabs_of_slot
            high_done[s].at += slabs_of_slot
            slab_done[s].at += slabs_of_slot
            added[s].at += len(cuts) * dturns * ns
            for cs, n in ((silu_g, ns), (act_done, ns), (hidden_high, 1), (hidden_low, 1)):
                cs[s].at += KF // 2 * n
        own.close()

    def store_output(block, dst, first):
        @block.sync
        def _(sync):
            for k in range(KD):
                sync.wait_ge(scaled.sem, first + k + 1)
                sync.dma_start(dst[:, k, :], h[:, k, 0:NX]).then_inc(out_done.sem, 16)
            sync.wait_ge(out_done.sem, 16 * KD)

    def own_rows(c):
        return bones[:, c * HD:c * HD + 1].to_broadcast([P, NX])

    def advance(counts, n):
        for c in counts:
            c.at += n

    def attention_tables(block):
        t0, e0 = tables.at, exp_done[0].at
        lamv = work[:, 0:4 * HD].rearrange("p (a n) -> p a n", a=4)
        @block.sync
        def _(sync):
            for dst, name in ((bones[:], "bones"), (ident[:], "ident"), (lamv, "lam"), (qkg[:], "qk_gain"),
                              (subg[:, 0:1], "sub_gain"), (rope[:, 0:2], "rope"), (rot[:, 0], "rot")):
                sync.dma_start(dst, io[name]).then_inc(tables.sem, 16)

        @block.vector
        def _(vector):
            vector.wait_ge(tables.sem, t0 + 16 * 7)
            for j in range(2):
                step(vector.tensor_scalar(rope[:, 2 + j, :], rope[:, 0, :], qkg[:, j:j + 1], None, ALU.mult))
                step(vector.tensor_scalar(rot[:, 1 + j, :], rot[:, 0, :], qkg[:, j:j + 1], None, ALU.mult))
                step(vector.tensor_tensor(lamv[:, 2 * j, :], lamv[:, 2 * j, :], lamv[:, 2 * j + 1, :], ALU.mult))
            step(vector.tensor_scalar(subg[:, 1:2], subg[:, 0:1], 1.0 - LAMBDA_INIT, None, ALU.mult))
            steps_done(vector)
            for j in range(2):
                step(vector.reduce_sum(lamt[:, j:j + 1], lamv[:, 2 * j, :], AX_X))
            lam_sum = dve_chain.at
            vector.wait_ge(exp_done[0].sem, e0 + 1)
            step(vector.tensor_tensor(lamt[:, 4:5], lamt[:, 3:4], lamt[:, 2:3], ALU.subtract))
            steps_done(vector)
            step(vector.tensor_scalar(lamt[:, 5:6], lamt[:, 4:5], -LAMBDA_INIT, None, ALU.add))
            steps_done(vector)
            lam_at.append(lam_sum)

        @block.scalar
        def _(scalar):
            scalar.wait_ge(dve_chain.sem, lam_at[0])
            scalar.activation(lamt[:, 2:4], lamt[:, 0:2], ACT.Exp).then_inc(exp_done[0].sem, 1)
        exp_done[0].at += 1
        tables.at += 16 * 7

    lam_at = []

    def head_inputs(block, which, dst, nxt):
        turns, slab0 = 2, 4 * which
        has_ctx = which == 1
        HSTEPS = 4 if has_ctx else 3
        n0 = list(ring.n)
        x0 = [c.at for c in hstep]
        p0, w0, q0, r0, t0, d0 = ([c.at for c in cs] for cs in (proj_done, raw_done, hss_done, hroot, t1_done, head_done))
        width = NT if has_ctx else NX
        raw = work[:, 4 * NT:8 * NT].rearrange("p (s j n) -> p s j n", s=2, j=2)
        sq = work[:, 0:4 * NT].rearrange("p (s j n) -> p s j n", s=2, j=2)
        root = work[:, 8 * NT:12 * NT].rearrange("p (s j n) -> p s j n", s=2, j=2)
        @block.sync
        def _(sync):
            with sync.Fori(0, turns - 1) as t:
                for s in range(2):
                    sync.wait_ge(ring.used[s], t + (n0[s] + 1))
                    sync.dma_start(ring.buf[:, s, 0:2 * KD * P],
                                   io["w_qk"][ds(t * 2 + (slab0 + 2 + s), 1)].rearrange("a p n -> (a p) n"))\
                        .then_inc(ring.landed[s], 16)
            prefetch(sync, nxt, [n + (turns if s < 2 else 0) for s, n in enumerate(n0)])

        @block.tensor
        def _(pe):
            with pe.Fori(0, turns) as t:
                for s in range(2):
                    w = ring.view(s, 2, KD, P)
                    pe.wait_ge(ring.landed[s], t * 16 + 16 * (n0[s] + 1))
                    if s == 1:
                        pe.wait_ge(raw_done[0].sem, t * 2 + (w0[0] + 2))
                    else:
                        pe.wait_ge(raw_done[1].sem, t * 2 + w0[1])
                    for j in range(2):
                        for k in range(KD):
                            mm = pe.matmul(ps[:, j, :], w[:, j, k, :], h[:, k, 0:NX], start=(k == 0), stop=(k == KD - 1))
                        if has_ctx:
                            for k in range(KD):
                                mm = pe.matmul(ps[:, 2, j * NY:(j + 1) * NY], w[:, j, k, :], h[:, k, NX:NT],
                                               start=(k == 0), stop=(k == KD - 1))
                    mm.then_inc(proj_done[s].sem, 1)
                    pe.wait_ge(proj_done[s].sem, t + (p0[s] + 1))
                    pe.sem_inc(ring.used[s], 1)
                    if s == 1:
                        pe.wait_ge(head_done[0].sem, t * 2 + (d0[0] + 2))
                    else:
                        pe.wait_ge(head_done[1].sem, t * 2 + d0[1])
                    for j in range(2):
                        pe.wait_ge(raw_done[s].sem, t * 2 + (w0[s] + j + 1))
                        pe.matmul(ps[:, 3 + j, :], rot[:, 1 + which, :], raw[:, s, j, 0:NX], start=True, stop=True)
                        mm = pe.matmul(ps[:, 5 + j, :], bones[:], sq[:, s, j, 0:NX], start=True, stop=True)
                        if has_ctx:
                            mm = pe.matmul(ps[:, 7, j * NY:(j + 1) * NY], bones[:], sq[:, s, j, NX:NT],
                                           start=True, stop=True)
                    mm.then_inc(hss_done[s].sem, 1)

        @block.scalar
        def _(scalar):
            with scalar.Fori(0, turns) as t:
                for s in range(2):
                    scalar.wait_ge(proj_done[s].sem, t + (p0[s] + 1))
                    scalar.wait_ge(head_done[s].sem, t * 2 + d0[s])
                    for j in range(2):
                        ctx_ps = ps[:, 2, j * NY:(j + 1) * NY]
                        scalar.activation(raw[:, s, j, 0:NX], ps[:, j, :], ACT.Copy)
                        if has_ctx:
                            scalar.activation(raw[:, s, j, NX:NT], ctx_ps, ACT.Copy)
                            scalar.activation(sq[:, s, j, NX:NT], ctx_ps, ACT.Square)
                        scalar.activation(sq[:, s, j, 0:NX], ps[:, j, :], ACT.Square).then_inc(raw_done[s].sem, 1)
                    scalar.wait_ge(hss_done[s].sem, t + (q0[s] + 1))
                    for j in range(2):
                        if has_ctx:
                            scalar.activation(root[:, s, j, NX:NT], ps[:, 7, j * NY:(j + 1) * NY], ACT.Sqrt,
                                              bias=eps[:, 0:1], scale=1.0 / HD)
                        scalar.activation(root[:, s, j, 0:NX], ps[:, 5 + j, :], ACT.Sqrt,
                                          bias=eps[:, 0:1], scale=1.0 / HD).then_inc(hroot[s].sem, 1)

        @block.gpsimd
        def _(gpsimd):
            with gpsimd.Fori(0, turns) as t:
                for s in range(2):
                    for j in range(2):
                        gpsimd.wait_ge(raw_done[s].sem, t * 2 + (w0[s] + j + 1))
                        gpsimd.wait_ge(hss_done[s].sem, t + (q0[s] + 1))
                        gpsimd.tensor_tensor(sq[:, s, j, 0:NX], raw[:, s, j, 0:NX], rope[:, 2 + which, :], ALU.mult)\
                            .then_inc(t1_done[s].sem, 1)

        @block.vector
        def _(vector):
            with vector.Fori(0, turns) as t:
                for s in range(2):
                    for j in range(2):
                        out = ds(t * 4 + (2 * s + j), 1)
                        r = root[:, s, j, 0:width]
                        vector.wait_ge(hroot[s].sem, t * 2 + (r0[s] + j + 1))
                        vector.reciprocal(r, r).then_inc(hstep[s].sem, 1)
                        vector.wait_ge(t1_done[s].sem, t * 2 + (t0[s] + j + 1))
                        vector.tensor_tensor(raw[:, s, j, 0:NX], ps[:, 3 + j, :], rope[:, 1, :], ALU.mult)\
                            .then_inc(hstep[s].sem, 1)
                        vector.wait_ge(hstep[s].sem, t * (2 * HSTEPS) + (x0[s] + HSTEPS * j + 2))
                        vector.tensor_tensor(raw[:, s, j, 0:NX], raw[:, s, j, 0:NX], sq[:, s, j, 0:NX], ALU.add)\
                            .then_inc(hstep[s].sem, 1)
                        if has_ctx:
                            vector.scalar_tensor_tensor(dst[:, out, NX:NT].rearrange("p a n -> p (a n)"),
                                                        raw[:, s, j, NX:NT], qkg[:, 1:2], r[:, NX:NT],
                                                        ALU.mult, ALU.mult).then_inc(hstep[s].sem, 1)
                        vector.wait_ge(hstep[s].sem, t * (2 * HSTEPS) + (x0[s] + HSTEPS * j + HSTEPS))
                        vector.tensor_tensor(dst[:, out, 0:NX].rearrange("p a n -> p (a n)"),
                                             raw[:, s, j, 0:NX], r[:, 0:NX], ALU.mult).then_inc(head_done[s].sem, 1)
            for s in range(2):
                vector.wait_ge(head_done[s].sem, d0[s] + 2 * turns)
        for s in range(2):
            ring.n[s] += turns
        for cs, n in ((proj_done, turns), (raw_done, 2 * turns), (hss_done, turns), (hroot, 2 * turns),
                      (t1_done, 2 * turns), (head_done, 2 * turns), (hstep, 2 * HSTEPS * turns)):
            advance(cs, n)

    hstep = [count(f"head_step{s}") for s in range(2)]

    def values(block, V, nxt):
        turns, C = 2, 2 * P
        n0 = list(ring.n)
        p0, w0 = ([c.at for c in cs] for cs in (proj_done, raw_done))
        @block.sync
        def _(sync):
            with sync.Fori(0, turns - 1) as t:
                for s in range(2):
                    sync.wait_ge(ring.used[s], t + (n0[s] + 1))
                    sync.dma_start(ring.buf[:, s, 0:KD * C],
                                   io["w_v"][ds(t * 2 + (2 + s), 1)].rearrange("a p n -> (a p) n"))\
                        .then_inc(ring.landed[s], 16)
            prefetch(sync, nxt, [n + (turns if s < 2 else 0) for s, n in enumerate(n0)])

        @block.tensor
        def _(pe):
            for s in range(2):
                pe.wait_ge(raw_done[s].sem, w0[s])
            with pe.Fori(0, turns) as t:
                for s in range(2):
                    w = ring.view(s, KD, C)
                    pe.wait_ge(ring.landed[s], t * 16 + 16 * (n0[s] + 1))
                    for m in range(KT):
                        if m >= 3:
                            pe.wait_ge(raw_done[s].sem, t * KT + (w0[s] + m - 2))
                        elif s == 1:
                            pe.wait_ge(raw_done[0].sem, t * KT + (w0[0] + m + 4))
                        else:
                            pe.wait_ge(raw_done[1].sem, t * KT + (w0[1] + m - 2))
                        for k in range(KD):
                            mm = pe.matmul(ps[:, m % 3, 0:C], h[:, k, m * P:(m + 1) * P], w[:, k, :],
                                           start=(k == 0), stop=(k == KD - 1))
                        mm.then_inc(proj_done[s].sem, 1)
                    pe.wait_ge(proj_done[s].sem, t * KT + (p0[s] + KT))
                    pe.sem_inc(ring.used[s], 1)

        @block.scalar
        def _(scalar):
            with scalar.Fori(0, turns) as t:
                for s in range(2):
                    for m in range(KT):
                        scalar.wait_ge(proj_done[s].sem, t * KT + (p0[s] + m + 1))
                        scalar.activation(V[:, m, ds(t * 2 * C + s * C, C)], ps[:, m % 3, 0:C], ACT.Copy)\
                            .then_inc(raw_done[s].sem, 1)
            for s in range(2):
                scalar.wait_ge(raw_done[s].sem, w0[s] + turns * KT)
        for s in range(2):
            ring.n[s] += turns
        advance(proj_done, KT * turns)
        advance(raw_done, KT * turns)

    def attention(Q, K, V, O):
        QT = NX // P
        turns = HEADS // 2
        VS = 6
        names = (staged, score_done, max_done, exp_done, prob_done, turn_done, turn_ev, pv_done, o_done, hstep)
        g0, s0, m0, e0, b0, u0, v0, p0, o0, h0 = ([c.at for c in cs] for cs in names)
        at = [0]

        def part(n):
            at[0] += n
            return work[:, at[0] - n:at[0]]

        qs = [hbuf[:, (HEADS + 2 * b) * NX:(HEADS + 2 * b + 2) * NX].rearrange("p (c n) -> p c n", c=2) for b in range(2)]
        ks = [part(NT) for _ in range(2)]
        vs = [part(NT).rearrange("p (m n) -> p m n", m=KT) for _ in range(2)]
        pr = [part(2 * NT).rearrange("p (c n) -> p c n", c=2) for _ in range(2)]
        aT = part(KT * NX).rearrange("p (m n) -> p m n", m=KT)
        sc = ps[:, 0:4, :].rearrange("p (c b) n -> p c (b n)", c=2)
        tp = ps[:, 4:6, :].rearrange("p b n -> p (b n)")

        with nc.Block() as block:
            @block.gpsimd
            def _(gpsimd):
                with gpsimd.Fori(0, turns) as t:
                    for b in range(2):
                        hd = ds(t * 2 + b, 1)
                        gpsimd.wait_ge(pv_done[b].sem, t + p0[b])
                        gpsimd.sem_inc(room.sem, 1)
                        for c in range(2):
                            gpsimd.tensor_tensor(qs[b][:, c, :], Q[:, hd, :].rearrange("p a n -> p (a n)"), own_rows(c),
                                                 ALU.mult).then_inc(staged[b].sem, 1)
                        gpsimd.tensor_copy(ks[b], K[:, hd, :].rearrange("p a n -> p (a n)")).then_inc(staged[b].sem, 1)
                        gpsimd.tensor_copy(vs[b], V[:, :, ds(t * 2 * P + b * P, P)]).then_inc(staged[b].sem, 1)

            @block.tensor
            def _(pe):
                def scores(t, b, q):
                    for c in range(2):
                        if q > 0:
                            pe.wait_ge(exp_done[b].sem, t * (2 * QT) + (e0[b] + 2 * q + c - 1))
                        elif b == 1:
                            pe.wait_ge(exp_done[0].sem, t * (2 * QT) + (e0[0] + 2 * QT + c - 1))
                        else:
                            pe.wait_ge(exp_done[1].sem, t * (2 * QT) + e0[1])
                        for a, n in ((0, NX), (NX, NY)):
                            mm = pe.matmul(sc[:, c, a:a + n], qs[b][:, c, q * P:(q + 1) * P], ks[b][:, a:a + n],
                                           start=True, stop=True)
                        mm.then_inc(score_done[b].sem, 1)

                def turn(t, b, q):
                    pe.wait_ge(prob_done[b].sem, t * QT + (b0[b] + q + 1))
                    if q > 0:
                        pe.wait_ge(turn_ev[b].sem, t * QT + (v0[b] + q))
                    elif b == 1:
                        pe.wait_ge(turn_ev[0].sem, t * QT + (v0[0] + QT))
                    else:
                        pe.wait_ge(turn_ev[1].sem, t * QT + v0[1])
                    for m in range(KT):
                        mm = pe.transpose(tp[:, m * P:(m + 1) * P], pr[q % 2][:, 0, m * P:(m + 1) * P], ident[:])
                    mm.then_inc(turn_done[b].sem, 1)

                def first_scores(t, b):
                    pe.wait_ge(staged[b].sem, t * 4 + (g0[b] + 4))
                    scores(t, b, 0)

                def head(t, b, after):
                    for q in range(QT):
                        if q + 1 < QT:
                            scores(t, b, q + 1)
                        elif after is not None:
                            first_scores(*after)
                        turn(t, b, q)
                    pe.wait_ge(turn_ev[b].sem, t * QT + (v0[b] + QT))
                    pe.wait_ge(o_done[b].sem, t + o0[b])
                    for m in range(KT):
                        mm = pe.matmul(ps[:, 6 + b, :], vs[b][:, m, :], aT[:, m, :], start=(m == 0), stop=(m == KT - 1))
                    mm.then_inc(pv_done[b].sem, 1)

                first_scores(0, 0)
                with pe.Fori(0, turns - 1) as t:
                    head(t, 0, (t, 1))
                    head(t, 1, (t + 1, 0))
                head(turns - 1, 0, (turns - 1, 1))
                head(turns - 1, 1, None)

            @block.scalar
            def _(scalar):
                with scalar.Fori(0, turns) as t:
                    for b in range(2):
                        for q in range(QT):
                            if q >= 2:
                                scalar.wait_ge(turn_done[b].sem, t * QT + (u0[b] + q - 1))
                            elif b == 1:
                                scalar.wait_ge(turn_done[0].sem, t * QT + (u0[0] + QT - 1 + q))
                            for c in range(2):
                                if q < 2 and b == 0 and c == 0:
                                    scalar.wait_ge(turn_done[1].sem, t * QT + u0[1])
                                scalar.wait_ge(max_done[b].sem, t * (2 * QT) + (m0[b] + 2 * q + c + 1))
                                scalar.activation(pr[q % 2][:, c, :], sc[:, c, 0:NT], ACT.Exp,
                                                  bias=stat[:, q % 2, 2 + c:3 + c], scale=HD ** -0.5,
                                                  accum_out=stat[:, q % 2, 4 + c:5 + c]).then_inc(exp_done[b].sem, 1)
                            if q > 0:
                                scalar.wait_ge(turn_done[b].sem, t * QT + (u0[b] + q))
                                if q == 1:
                                    if b == 1:
                                        scalar.wait_ge(pv_done[0].sem, t + (p0[0] + 1))
                                    else:
                                        scalar.wait_ge(pv_done[1].sem, t + p0[1])
                                scalar.activation(aT[:, :, (q - 1) * P:q * P],
                                                  tp[:, 0:NT].rearrange("p (m n) -> p m n", m=KT), ACT.Copy).then_inc(turn_ev[b].sem, 1)
                        scalar.wait_ge(turn_done[b].sem, t * QT + (u0[b] + QT))
                        scalar.activation(aT[:, :, (QT - 1) * P:QT * P], tp[:, 0:NT].rearrange("p (m n) -> p m n", m=KT),
                                          ACT.Copy).then_inc(turn_ev[b].sem, 1)

            @block.vector
            def _(vector):
                def softmax(t, b, q):
                    def sstep(ins, n):
                        ins.then_inc(hstep[b].sem, 1)
                        vector.wait_ge(hstep[b].sem, t * (VS * QT) + (h0[b] + VS * q + n))
                    st = stat[:, q % 2]
                    for c in range(2):
                        vector.wait_ge(score_done[b].sem, t * (2 * QT) + (s0[b] + 2 * q + c + 1))
                        sstep(vector.reduce_max(st[:, c:c + 1], sc[:, c, 0:NT], AX_X), c + 1)
                        vector.tensor_scalar(st[:, 2 + c:3 + c], st[:, c:c + 1], -HD ** -0.5, None, ALU.mult)\
                            .then_inc(max_done[b].sem, 1)
                    vector.wait_ge(exp_done[b].sem, t * (2 * QT) + (e0[b] + 2 * q + 1))
                    sstep(vector.reciprocal(st[:, 6:7], st[:, 4:5]), 3)
                    sstep(vector.tensor_scalar(pr[q % 2][:, 0, :], pr[q % 2][:, 0, :], st[:, 6:7], None, ALU.mult), 4)
                    vector.wait_ge(exp_done[b].sem, t * (2 * QT) + (e0[b] + 2 * q + 2))
                    sstep(vector.reciprocal(st[:, 7:8], st[:, 5:6]), 5)
                    sstep(vector.tensor_scalar(st[:, 7:8], st[:, 7:8], lamt[:, 5:6], None, ALU.mult), 6)
                    vector.scalar_tensor_tensor(pr[q % 2][:, 0, :], pr[q % 2][:, 1, :], st[:, 7:8],
                                                pr[q % 2][:, 0, :], ALU.mult, ALU.add).then_inc(prob_done[b].sem, 1)

                def output(t, b):
                    vector.wait_ge(pv_done[b].sem, t + (p0[b] + 1))
                    vector.tensor_copy(O[:, ds(t * 2 + b, 1), :].rearrange("p a n -> p (a n)"), ps[:, 6 + b, :])\
                        .then_inc(o_done[b].sem, 1)

                def head(t, b, before):
                    for q in range(QT):
                        softmax(t, b, q)
                        if q == 0 and before is not None:
                            output(*before)

                head(0, 0, None)
                head(0, 1, (0, 0))
                with vector.Fori(1, turns) as t:
                    head(t, 0, (t - 1, 1))
                    head(t, 1, (t, 0))
                output(turns - 1, 1)
                for b in range(2):
                    vector.wait_ge(o_done[b].sem, o0[b] + turns)
        for cs, n in zip(names, (4, 2 * QT, 2 * QT, 2 * QT, QT, QT, QT, 1, 1, VS * QT)):
            advance(cs, n * turns)

    def output_norm(block, O, gain):
        q0, r0, s0, h0, d0, p0 = (c.at for c in (sq_done, root_done, ss_done, rstd_done, scaled, pv_done[0]))
        set_at = dve_chain.at + 2
        sq = work[:, 0:HEADS * NX].rearrange("p (b n) -> p b n", b=HEADS)
        column = work[:, HEADS * NX:HEADS * NX + 2 * P]
        row = work[:, HEADS * NX + 2 * P:HEADS * (NX + P) + 2 * P].rearrange("p (j n) -> p j n", j=HEADS)
        @block.scalar
        def _(scalar):
            for j in range(HEADS):
                scalar.activation(sq[:, j, :], O[:, j, :], ACT.Square).then_inc(sq_done.sem, 1)
            scalar.wait_ge(ss_done.sem, s0 + 1)
            scalar.activation(tmp[:, 0, 0:NX], ps[:, 0, :], ACT.Sqrt, bias=eps[:, 0:1], scale=1.0 / P)\
                .then_inc(root_done.sem, 1)

        @block.tensor
        def _(pe):
            pe.wait_ge(dve_chain.sem, set_at)
            for j in range(HEADS):
                pe.wait_ge(sq_done.sem, q0 + j + 1)
                mm = pe.matmul(ps[:, 0, :], column[:, P - j:2 * P - j], sq[:, j, :],
                               start=(j == 0), stop=(j == HEADS - 1))
            mm.then_inc(ss_done.sem, 1)
            pe.wait_ge(dve_chain.sem, set_at + HEADS)
            pe.wait_ge(rstd_done.sem, h0 + 1)
            for j in range(HEADS):
                if j >= 6:
                    pe.wait_ge(scaled.sem, d0 + j - 5)
                pe.matmul(ps[:, 1 + j % 6, :], row[:, j, :], rstd[:, 0:NX],
                          start=True, stop=True).then_inc(pv_done[0].sem, 1)

        @block.vector
        def _(vector):
            vector.memset(column, 0.0).then_inc(dve_chain.sem, 1)
            vector.wait_ge(dve_chain.sem, set_at - 1)
            vector.memset(column[:, P:P + 1], 1.0).then_inc(dve_chain.sem, 1)
            for j in range(HEADS):
                vector.tensor_copy(row[:, j, :], ident[:, j:j + 1].to_broadcast([P, P])).then_inc(dve_chain.sem, 1)
            vector.wait_ge(root_done.sem, r0 + 1)
            vector.reciprocal(rstd[:, 0:NX], tmp[:, 0, 0:NX]).then_inc(rstd_done.sem, 1)
            for j in range(HEADS):
                vector.wait_ge(pv_done[0].sem, p0 + j + 1)
                vector.scalar_tensor_tensor(O[:, j, :], O[:, j, :], gain, ps[:, 1 + j % 6, :], ALU.mult, ALU.mult)\
                    .then_inc(scaled.sem, 1)
            vector.wait_ge(scaled.sem, d0 + HEADS)
        dve_chain.at += 2 + HEADS
        advance((sq_done, scaled, pv_done[0]), HEADS)
        advance((root_done, ss_done, rstd_done), 1)

    def project_residual(block, w, src, gate, nxt, ready):
        turns = 2
        n0 = list(ring.n)
        d0, r0 = ([c.at for c in cs] for cs in (down_done, added))
        @block.sync
        def _(sync):
            with sync.Fori(0, turns - 1) as t:
                for s in range(2):
                    sync.wait_ge(ring.used[s], t + (n0[s] + 1))
                    sync.dma_start(ring.buf[:, s, 0:2 * KD * P], w[ds(t * 2 + (2 + s), 1)].rearrange("a p n -> (a p) n"))\
                        .then_inc(ring.landed[s], 16)
            prefetch(sync, nxt, [n + (turns if s < 2 else 0) for s, n in enumerate(n0)])

        @block.tensor
        def _(pe):
            for c in ready:
                pe.wait_ge(c.sem, c.at)
            with pe.Fori(0, turns) as t:
                for s in range(2):
                    wv = ring.view(s, 2, KD, P)
                    pe.wait_ge(ring.landed[s], t * 16 + 16 * (n0[s] + 1))
                    pe.wait_ge(added[s].sem, t * 2 + r0[s])
                    for j in range(2):
                        for k in range(KD):
                            mm = pe.matmul(ps[:, 2 * s + j, :], wv[:, j, k, :], src[:, k, 0:NX],
                                           start=(k == 0), stop=(k == KD - 1))
                    mm.then_inc(down_done[s].sem, 1)
                    pe.wait_ge(down_done[s].sem, t + (d0[s] + 1))
                    pe.sem_inc(ring.used[s], 1)

        @block.vector
        def _(vector):
            with vector.Fori(0, turns) as t:
                for s in range(2):
                    vector.wait_ge(down_done[s].sem, t + (d0[s] + 1))
                    for j in range(2):
                        x = xy[:, ds(t * 4 + (2 * s + j), 1), 0:NX].rearrange("p a n -> p (a n)")
                        if gate is None:
                            vector.tensor_tensor(x, ps[:, 2 * s + j, :], x, ALU.add).then_inc(added[s].sem, 1)
                        else:
                            g = gate[:, ds(t * 4 + (2 * s + j), 1), 0:1].rearrange("p a n -> p (a n)")
                            vector.scalar_tensor_tensor(x, ps[:, 2 * s + j, :], g, x, ALU.mult, ALU.add)\
                                .then_inc(added[s].sem, 1)
            for s in range(2):
                vector.wait_ge(added[s].sem, r0[s] + 2 * turns)
        for s in range(2):
            ring.n[s] += turns
        advance(down_done, turns)
        advance(added, 2 * turns)

    def second_gains():
        t0 = tables.at
        with nc.Block() as block:
            @block.sync
            def _(sync):
                sync.dma_start(gains2[:], io["gains2"]).then_inc(tables.sem, 16)
                sync.wait_ge(tables.sem, t0 + 16)
        tables.at += 16

    def dft_tables():
        cd = big[:, 16 * NX:16 * NX + D].rearrange("p (k n) -> p k n", k=2)
        cn = big[:, 16 * NX + D:24 * NX + D].rearrange("p (c t n) -> p c t n", c=2, t=NX // P)
        return cd, cn

    def fourier(block, F):
        groups, TT = 4, NX // P
        C = 2 * (D // groups)
        Y = big[:, 0:TT * groups * C].rearrange("p (t g n) -> p t g n", t=TT, g=groups)
        cd, cn = dft_tables()
        t0, p0, w0 = tables.at, [c.at for c in proj_done], [c.at for c in raw_done]
        units = TT * groups
        @block.tensor
        def _(pe):
            pe.wait_ge(tables.sem, t0 + 32)
            for u in range(units):
                t, g = u // groups, u % groups
                if u >= 8:
                    pe.wait_ge(raw_done[u % 2].sem, w0[u % 2] + (u - 8) // 2 + 1)
                for k in range(2):
                    mm = pe.matmul(ps[:, u % 8, :], h[:, 2 * g + k, t * P:(t + 1) * P], cd[:, k, :],
                                   start=(k == 0), stop=(k == 1))
                mm.then_inc(proj_done[u % 2].sem, 1)
            for s in range(2):
                pe.wait_ge(raw_done[s].sem, w0[s] + units // 2)
            for m in range(KD):
                g, half = m // 2, (m % 2) * P
                for n in range(2 * TT):
                    c, t = n // TT, n % TT
                    a = c * (C // 2) + half
                    mm = pe.matmul(ps[:, m, :], Y[:, t, g, a:a + P], cn[:, c, t, :],
                                   start=(n == 0), stop=(n == 2 * TT - 1))
                mm.then_inc(proj_done[m % 2].sem, 1)

        def copies(eng, s, copy):
            for u in range(s, units, 2):
                eng.wait_ge(proj_done[s].sem, p0[s] + u // 2 + 1)
                copy(Y[:, u // groups, u % groups, :], ps[:, u % 8, :]).then_inc(raw_done[s].sem, 1)
            for m in range(s, KD, 2):
                eng.wait_ge(proj_done[s].sem, p0[s] + units // 2 + m // 2 + 1)
                copy(F[:, m, :], ps[:, m, :]).then_inc(raw_done[s].sem, 1)

        @block.scalar
        def _(scalar):
            copies(scalar, 0, scalar.copy)

        @block.vector
        def _(vector):
            copies(vector, 1, vector.tensor_copy)
        tables.at += 32
        advance(proj_done, (units + KD) // 2)
        advance(raw_done, (units + KD) // 2)

    value_weights = ring.buf[:].rearrange("p s n -> p (s n)")[:, 0:KD * 3 * P]

    def mixer_inputs(gain, F, G, full, split_h, split_w):
        phases = [("queries", 2, 0, F[:, 0:8], HD ** -0.5, ACT.Copy), ("keys", 2, 2, F[:, 8:16], 1.0, ACT.Copy),
                  ("gates", 4, 4, G, 1.0, ACT.Sigmoid)]
        turns = 8
        h_high, h_low = split_h
        w_high, w_low = split_w
        w = io["w_in"]
        n0 = list(ring.n)
        norm_names = (sq_done, ss_done, root_done, rstd_done, scaled, in_high, in_low)
        q0, u0, y0, i0, z0, h0, j0 = (c.at for c in norm_names)
        p0, b0, r0 = ([c.at for c in cs] for cs in (proj_done, high_done, raw_done))
        with nc.Block() as block:
            @block.sync
            def _(sync):
                with sync.Fori(0, turns - 1) as t:
                    for s in range(2):
                        sync.wait_ge(ring.used[s], t + (n0[s] + 1))
                        sync.dma_start(ring.buf[:, s, :], w[ds(t * 2 + (2 + s), 1)].rearrange("a p n -> (a p) n"))\
                            .then_inc(ring.landed[s], 16)
                for s in range(2):
                    sync.wait_ge(ring.used[s], n0[s] + turns)
                sync.dma_start(value_weights, io["w_v2"]).then_inc(tables.sem, 16)

            @block.tensor
            def _(pe):
                for k in range(KD):
                    pe.wait_ge(sq_done.sem, q0 + k + 1)
                    mm = pe.matmul(ps[:, 6, :], ones[:], full[:, k, :], start=(k == 0), stop=(k == KD - 1))
                mm.then_inc(ss_done.sem, 1)

                def slab(t, s, first):
                    pe.wait_ge(ring.used[s], t + (n0[s] + 1))
                    pe.wait_ge(raw_done[s].sem, t * 2 + r0[s])
                    for j in range(2):
                        for k in range(KD):
                            if first and j == 0:
                                pe.wait_ge(in_low.sem, j0 + k + 1)
                            at = slice((j * KD + k) * P, (j * KD + k + 1) * P)
                            out = ps[:, 2 * s + j, :]
                            pe.matmul(out, w_high[:, s, at], h_high[:, k, :], start=(k == 0), stop=False)
                            pe.matmul(out, w_high[:, s, at], h_low[:, k, :], start=False, stop=False)
                            mm = pe.matmul(out, w_low[:, s, at], h_high[:, k, :], start=False, stop=(k == KD - 1))
                        mm.then_inc(proj_done[s].sem, 1)

                slab(0, 0, True)
                slab(0, 1, False)
                with pe.Fori(1, turns) as t:
                    for s in range(2):
                        slab(t, s, False)

            @block.scalar
            def _(scalar):
                def split(ph, t, s):
                    scalar.wait_ge(ring.landed[s], t * 16 + 16 * (n0[s] + ph[2] + 1))
                    scalar.wait_ge(proj_done[s].sem, t * 2 + (p0[s] + 2 * ph[2]))
                    scalar.activation(w_high[:, s, :], ring.buf[:, s, :], ACT.Copy).then_inc(high_done[s].sem, 1)

                def item(ph, t, s):
                    _, _, n1, dst, scale, func = ph
                    for j in range(2):
                        scalar.wait_ge(proj_done[s].sem, t * 2 + (p0[s] + 2 * n1 + j + 1))
                        scalar.sem_inc(room_act.sem, 1)
                        scalar.activation(dst[:, ds(t * 4 + (2 * s + j), 1), :].rearrange("p a n -> p (a n)"),
                                          ps[:, 2 * s + j, :], func, scale=scale).then_inc(raw_done[s].sem, 1)

                for k in range(KD):
                    scalar.activation(full[:, k, :], xy[:, k, 0:NX], ACT.Square).then_inc(sq_done.sem, 1)
                split(phases[0], 0, 0)
                scalar.wait_ge(ss_done.sem, u0 + 1)
                scalar.activation(tmp[:, 0, 0:NX], ps[:, 6, :], ACT.Sqrt, bias=eps[:, 0:1], scale=1.0 / D)\
                    .then_inc(root_done.sem, 1)
                for k in range(KD):
                    scalar.wait_ge(scaled.sem, z0 + k + 1)
                    scalar.activation(h_high[:, k, :], full[:, k, :], ACT.Copy).then_inc(in_high.sem, 1)
                split_ahead(scalar, phases, split, item)
                for s in range(2):
                    scalar.wait_ge(raw_done[s].sem, r0[s] + 2 * turns)

            @block.vector
            def _(vector):
                def split(ph, t, s):
                    vector.wait_ge(high_done[s].sem, t + (b0[s] + ph[2] + 1))
                    vector.tensor_tensor(w_low[:, s, :], ring.buf[:, s, :], w_high[:, s, :].bitcast(F32),
                                         ALU.subtract).then_inc(ring.used[s], 1)

                split(phases[0], 0, 0)
                vector.wait_ge(root_done.sem, y0 + 1)
                vector.reciprocal(rstd[:, 0:NX], tmp[:, 0, 0:NX]).then_inc(rstd_done.sem, 1)
                vector.wait_ge(rstd_done.sem, i0 + 1)
                for k in range(KD + 1):
                    if k < KD:
                        vector.scalar_tensor_tensor(full[:, k, :], xy[:, k, 0:NX], gain[:, k, 0:1], rstd[:, 0:NX],
                                                    ALU.mult, ALU.mult).then_inc(scaled.sem, 1)
                    if k > 0:
                        vector.wait_ge(scaled.sem, z0 + k)
                        vector.wait_ge(in_high.sem, h0 + k)
                        vector.tensor_tensor(h_low[:, k - 1, :], full[:, k - 1, :], h_high[:, k - 1, :].bitcast(F32),
                                             ALU.subtract).then_inc(in_low.sem, 1)
                split_ahead(vector, phases, split, lambda ph, t, s: None)
        for c, n in zip(norm_names, (KD, 1, 1, 1, KD, KD, KD)):
            c.at += n
        for s in range(2):
            ring.n[s] += turns
            high_done[s].at += turns
        advance(proj_done, 2 * turns)
        advance(raw_done, 2 * turns)

    def values_and_gates(F, V2, split_h, split_w, nxt):
        TT = NX // P
        n = KD * 3 * P
        raw = value_weights
        high, low = (a.rearrange("p s n -> p (s n)")[:, 0:n] for a in split_w)
        v_high, v_low = (a.rearrange("p (k n) -> p k n", k=KD) for a in (high, low))
        h_high, h_low = split_h
        t0, p0, w0, u0, v0 = tables.at, proj_done[0].at, raw_done[0].at, turn_done[0].at, turn_ev[0].at
        b0, y0 = high_done[0].at, dve_chain.at
        with nc.Block() as block:
            @block.sync
            def _(sync):
                for dst, name in ((dist, "dist"), (dist_c[:], "dist_cmp"), (slopes[:], "slopes"), (sinks[:], "sinks")):
                    sync.dma_start(dst, io[name]).then_inc(tables.sem, 16)
                sync.wait_ge(dve_chain.sem, y0 + 1)
                prefetch(sync, nxt, ring.n)

            @block.tensor
            def _(pe):
                for m in range(TT):
                    mm = pe.transpose(ps[:, 4, m * P:(m + 1) * P], F[:, 15, m * P:(m + 1) * P], ident[:])
                mm.then_inc(turn_done[0].sem, 1)
                pe.wait_ge(dve_chain.sem, y0 + 1)
                for m in range(TT):
                    for k in range(KD):
                        out = ps[:, m, 0:3 * P]
                        tok = slice(m * P, (m + 1) * P)
                        pe.matmul(out, h_high[:, k, tok], v_high[:, k, :], start=(k == 0), stop=False)
                        pe.matmul(out, h_high[:, k, tok], v_low[:, k, :], start=False, stop=False)
                        mm = pe.matmul(out, h_low[:, k, tok], v_high[:, k, :], start=False, stop=(k == KD - 1))
                    mm.then_inc(proj_done[0].sem, 1)

            @block.vector
            def _(vector):
                vector.wait_ge(high_done[0].sem, b0 + 1)
                vector.tensor_tensor(low, raw, high.bitcast(F32), ALU.subtract).then_inc(dve_chain.sem, 1)

            @block.scalar
            def _(scalar):
                scalar.wait_ge(turn_done[0].sem, u0 + 1)
                scalar.activation(gates[:].rearrange("p h b t -> p t (h b)"),
                                  ps[:, 4, :].rearrange("p (t n) -> p t n", t=TT)[:, :, 0:3 * HEADS],
                                  ACT.Sigmoid).then_inc(turn_ev[0].sem, 1)
                scalar.wait_ge(tables.sem, t0 + 5 * 16)
                scalar.activation(high, raw, ACT.Copy).then_inc(high_done[0].sem, 1)
                for m in range(TT):
                    scalar.wait_ge(proj_done[0].sem, p0 + m + 1)
                    scalar.activation(V2[:, m, :], ps[:, m, 0:3 * P], ACT.Copy).then_inc(raw_done[0].sem, 1)
                scalar.wait_ge(raw_done[0].sem, w0 + TT)
                scalar.wait_ge(turn_ev[0].sem, v0 + 1)
        tables.at += 5 * 16
        proj_done[0].at += TT
        raw_done[0].at += TT
        turn_done[0].at += 1
        turn_ev[0].at += 1
        high_done[0].at += 1
        dve_chain.at += 1

    def compress(F, kcT, vc):
        LP, NB = CMP_LEN // 2, CMP_BLOCKS
        w1 = work[:, 0:2 * LP * CMP_HIDDEN].rearrange("p (v l n) -> p v l n", v=2, l=LP)
        o = [0]

        def part(n):
            o[0] += n
            return hbuf[:, o[0] - n:o[0]]

        blk = part(2 * LP * 2 * NB).rearrange("p (v l c) -> p v l c", v=2, l=LP)
        pos = part(2 * LP * NB).rearrange("p (v l c) -> p v l c", v=2, l=LP)
        w2 = part(2 * 2 * HD).rearrange("p (v k n) -> p v k n", v=2, k=2)
        hid = part(2 * CMP_HIDDEN).rearrange("p (v n) -> p v n", v=2)
        hidT = part(2 * 2 * 2 * NB).rearrange("p (v k n) -> p v k n", v=2, k=2)
        t0, k0, p0, w0, u0, v0 = (c.at for c in (tables, t1_done[0], proj_done[0], raw_done[0], turn_done[0], turn_ev[0]))
        with nc.Block() as block:
            @block.sync
            def _(sync):
                sync.dma_start(pos, io["cmp_pos"]).then_inc(tables.sem, 16)
                sync.dma_start(w2, io["cmp_w2"]).then_inc(tables.sem, 16)
                sync.dma_start(w1[:, 0], io["cmp_w1"][:, 0]).then_inc(tables.sem, 16)
                sync.dma_start(w1[:, 1], io["cmp_w1"][:, 1]).then_inc(loaded.sem, 16)

            @block.vector
            def _(vector):
                vector.wait_ge(tables.sem, t0 + 48)
                for v in range(2):
                    for g in range(2):
                        for a in range(2):
                            half = slice(a * HD, (a + 1) * HD)
                            for e in range(2):
                                src = F[half, 11 + 2 * v + g, e * CMP_STRIDE:e * CMP_STRIDE + NB * CMP_STRIDE]
                                src = src.rearrange("p (c l) -> p l c", l=CMP_STRIDE)[:, a::2, :]
                                lp = slice(e * LP // 2, (e + 1) * LP // 2)
                                vector.tensor_tensor(blk[half, v, lp, g * NB:(g + 1) * NB], src, pos[half, v, lp, :],
                                                     ALU.add).then_inc(t1_done[0].sem, 1)

            @block.tensor
            def _(pe):
                pe.wait_ge(tables.sem, t0 + 48)
                for v in range(2):
                    if v == 1:
                        pe.wait_ge(loaded.sem, loaded.at + 16)
                    pe.wait_ge(t1_done[0].sem, k0 + 8 * (v + 1))
                    for l in range(LP):
                        mm = pe.matmul(ps[0:2 * NB, v, 0:CMP_HIDDEN], blk[:, v, l, :], w1[:, v, l, :],
                                       start=(l == 0), stop=(l == LP - 1))
                    mm.then_inc(proj_done[0].sem, 1)
                for v in range(2):
                    pe.wait_ge(raw_done[0].sem, w0 + v + 1)
                    for k in range(2):
                        mm = pe.transpose(ps[:, 2 + v, k * 2 * NB:(k + 1) * 2 * NB], hid[0:2 * NB, v, k * P:(k + 1) * P],
                                          ident[0:2 * NB, 0:2 * NB])
                    mm.then_inc(turn_done[0].sem, 1)
                pe.wait_ge(turn_ev[0].sem, v0 + 2)
                for g in range(2):
                    for k in range(2):
                        mm = pe.matmul(ps[g * HD:(g + 1) * HD, 4, 0:NB], w2[:, 0, k, :], hidT[:, 0, k, g * NB:(g + 1) * NB],
                                       start=(k == 0), stop=(k == 1))
                for g in range(2):
                    for k in range(2):
                        mm = pe.matmul(ps[0:NB, 5 + g, 0:HD], hidT[:, 1, k, g * NB:(g + 1) * NB], w2[:, 1, k, :],
                                       start=(k == 0), stop=(k == 1))
                mm.then_inc(proj_done[0].sem, 1)

            @block.scalar
            def _(scalar):
                for v in range(2):
                    scalar.wait_ge(proj_done[0].sem, p0 + v + 1)
                    scalar.activation(hid[0:2 * NB, v, :], ps[0:2 * NB, v, 0:CMP_HIDDEN], ACT.Silu)\
                        .then_inc(raw_done[0].sem, 1)
                for v in range(2):
                    scalar.wait_ge(turn_done[0].sem, u0 + v + 1)
                    scalar.activation(hidT[:, v, :, :], ps[:, 2 + v, 0:4 * NB].rearrange("p (k n) -> p k n", k=2),
                                      ACT.Copy).then_inc(turn_ev[0].sem, 1)
                scalar.wait_ge(proj_done[0].sem, p0 + 3)
                scalar.activation(kcT, ps[:, 4, 0:NB], ACT.Copy).then_inc(raw_done[0].sem, 1)
                scalar.activation(vc, ps[0:NB, 5:7, 0:HD], ACT.Copy).then_inc(raw_done[0].sem, 1)
                scalar.wait_ge(raw_done[0].sem, w0 + 4)
        tables.at += 48
        t1_done[0].at += 16
        proj_done[0].at += 3
        raw_done[0].at += 4
        turn_done[0].at += 2
        turn_ev[0].at += 2

    def branches(block, F, V2, kcT, vc, Oa, Ob):
        TT = NX // P
        TURNS = 4
        back = {1: TT, 2: NSA_WINDOW // P, 3: SWA_WINDOW // P}

        def width(br, q):
            return CMP_BLOCKS if br == 0 else (min(q, back[br]) + 1) * P

        where, total = {}, 0
        for br in range(4):
            for q in range(TT):
                where[br, q] = total
                total += width(br, q)
        S = [work[:, b * total:(b + 1) * total] for b in range(2)]
        PT = [ring.buf[:, 2, 0:1280], work[:, 2 * total:2 * total + 1280]]
        turned = {1: 0, 2: 512, 3: 896, 0: 896 + 256}
        qt = hbuf[:, KD * NX:(KD + 4) * NX].rearrange("p (b k n) -> p b k n", b=2, k=2)
        w0 = [c.at for c in weighed]
        names = (staged, score_done, prob_done, max_done, exp_done, hstep, turn_done, turn_ev, pv_done, o_done)
        g0, s0, b0, m0, e0, h0, u0, v0, p0, o0 = ([c.at for c in cs] for cs in names)

        def tile(t, base):
            return F[:, ds(t + base, 1), :].rearrange("p a n -> p (a n)")

        def score_bank(br, q):
            n = width(br, q)
            if br == 0:
                return ps[:, 2, 384:384 + n]
            return ps[:, br - 1, 0:n]

        def keys(br, q):
            if br == 0:
                return kcT
            first = (q + 1) * P - width(br, q)
            return F[:, 7 + br, first:(q + 1) * P]

        @block.gpsimd
        def _(gpsimd):
            with gpsimd.Fori(0, TURNS) as t:
                for b in range(2):
                    gpsimd.wait_ge(score_done[b].sem, t * TT + s0[b])
                    gpsimd.sem_inc(room.sem, 1)
                    for k in range(2):
                        gpsimd.tensor_tensor(qt[:, b, k, :], tile(t, 4 * k), own_rows(b), ALU.mult)\
                            .then_inc(staged[b].sem, 1)

        @block.tensor
        def _(pe):
            def scores(t, b, q):
                if q > 0:
                    pe.wait_ge(prob_done[b].sem, t * TT + (b0[b] + q))
                elif b == 1:
                    pe.wait_ge(prob_done[0].sem, t * TT + (b0[0] + TT))
                else:
                    pe.wait_ge(prob_done[1].sem, t * TT + b0[1])
                for br in range(4):
                    mm = pe.matmul(score_bank(br, q), qt[:, b, br // 3, q * P:(q + 1) * P], keys(br, q),
                                   start=True, stop=True)
                mm.then_inc(score_done[b].sem, 1)

            def turn(t, b, q):
                if q > 0:
                    pe.wait_ge(turn_ev[b].sem, t * TT + (v0[b] + q))
                elif b == 1:
                    pe.wait_ge(turn_ev[0].sem, t * TT + (v0[0] + TT))
                else:
                    pe.wait_ge(turn_ev[1].sem, t * TT + v0[1])
                pe.wait_ge(weighed[b].sem, t * (4 * TT) + (w0[b] + 4 * (q + 1)))
                for br in range(4):
                    n = width(br, q)
                    bank = {1: 3, 2: 4, 3: 5, 0: 5}[br]
                    c = 256 if br == 0 else 0
                    for a in range(0, n, P):
                        w = min(P, n - a)
                        src = S[b][:, where[br, q] + a:where[br, q] + a + w]
                        mm = pe.transpose(ps[0:w, bank, c + a:c + a + P], src, ident[:])
                mm.then_inc(turn_done[b].sem, 1)

            def weigh(t, b, q):
                half = slice(b * HD, (b + 1) * HD)
                pe.wait_ge(turn_ev[b].sem, t * TT + (v0[b] + q + 1))
                if q == 0:
                    pe.wait_ge(o_done[b].sem, t + o0[b])
                cols = slice(q * P, (q + 1) * P)
                jobs = [(6, vc[:, b, :], PT[q % 2][0:CMP_BLOCKS, turned[0]:turned[0] + P])]
                for br in (1, 2, 3):
                    n = width(br, q) // P
                    for a in range(n):
                        jobs.append((7 if br == 3 else 6,
                                     V2[:, q + 1 - n + a, (br - 1) * P + b * HD:(br - 1) * P + (b + 1) * HD],
                                     PT[q % 2][:, turned[br] + a * P:turned[br] + (a + 1) * P]))
                for bank in (6, 7):
                    own = [j for j in jobs if j[0] == bank]
                    for n, (_, w, p) in enumerate(own):
                        mm = pe.matmul(ps[half, bank, cols], w, p, start=(n == 0), stop=(n == len(own) - 1))
                mm.then_inc(pv_done[b].sem, 1)

            def front(t, b):
                pe.wait_ge(staged[b].sem, t * 2 + (g0[b] + 2))
                for q in range(TT):
                    scores(t, b, q)

            def rear(t, b, ahead=None):
                if ahead is not None:
                    pe.wait_ge(staged[b].sem, ahead * 2 + (g0[b] + 2))
                for q in range(TT):
                    if ahead is not None:
                        scores(ahead, b, q)
                    if q == 0:
                        turn(t, b, 0)
                    if q + 1 < TT:
                        turn(t, b, q + 1)
                    weigh(t, b, q)

            front(0, 0)
            front(0, 1)
            with pe.Fori(0, TURNS - 1) as t:
                for b in range(2):
                    rear(t, b, t + 1)
            rear(TURNS - 1, 0)
            rear(TURNS - 1, 1)

        @block.vector
        def _(vector):
            FRONT = 8 * TT + 2

            def counted(t, b, at):
                k = [at]

                def sstep(ins):
                    ins.then_inc(hstep[b].sem, 1)
                    k[0] += 1

                def sdone():
                    vector.wait_ge(hstep[b].sem, t * BSTEPS + (h0[b] + k[0]))
                return k, sstep, sdone

            def front_tile(t, b, q, steps, again):
                _, sstep, sdone = steps
                st = stat2[:, b]
                head = t + 4 * b
                if again:
                    vector.wait_ge(turn_done[b].sem, t * TT + (u0[b] - TT + q + 1))
                vector.wait_ge(score_done[b].sem, t * TT + (s0[b] + q + 1))
                for br in range(4):
                    n = width(br, q)
                    slope = slopes[:, ds(head + (8 if br == 3 else 0), 1)]
                    if br == 0:
                        d = dist_c[:, q, :]
                    else:
                        end = {1: 512, 2: 896, 3: 1152}[br]
                        d = dist[:, end - n:end]
                    sstep(vector.scalar_tensor_tensor(S[b][:, where[br, q]:where[br, q] + n], d, slope,
                                                      score_bank(br, q), ALU.mult, ALU.add))
                sdone()
                vector.sem_inc(prob_done[b].sem, 1)
                for br in range(4):
                    n = width(br, q)
                    sstep(vector.reduce_max(st[:, 0, br * TT + q:br * TT + q + 1],
                                            S[b][:, where[br, q]:where[br, q] + n], AX_X))

            def front_end(t, b, steps):
                k, sstep, sdone = steps
                st = stat2[:, b]
                sdone()
                sstep(vector.tensor_scalar(st[:, 0, 12:16], st[:, 0, 12:16], sinks[:, ds(t + 4 * b, 1)], None, ALU.max))
                sdone()
                sstep(vector.tensor_scalar(st[:, 1, :], st[:, 0, :], -1e20, -1.0, ALU.max, ALU.mult))
                sdone()
                vector.sem_inc(max_done[b].sem, 1)
                assert k[0] == FRONT

            def front(t, b):
                steps = counted(t, b, 0)
                for q in range(TT):
                    front_tile(t, b, q, steps, False)
                front_end(t, b, steps)

            def rear(t, b, ahead=None):
                head = t + 4 * b
                st = stat2[:, b]
                k, sstep, sdone = counted(t, b, FRONT)
                vector.wait_ge(exp_done[b].sem, t + (e0[b] + 1))
                sstep(vector.tensor_tensor(st[:, 2, 12:16], st[:, 2, 12:16], st[:, 3, 0:4], ALU.add))
                sdone()
                sstep(vector.tensor_scalar(st[:, 2, :], st[:, 2, :], 1e-30, None, ALU.max))
                sdone()
                sstep(vector.reciprocal(st[:, 2, :], st[:, 2, :]))
                sdone()
                sstep(vector.tensor_tensor(st[:, 2, 0:12], st[:, 2, 0:12],
                                           gates[:, ds(head, 1), :, :].rearrange("p a b t -> p (a b t)"), ALU.mult))
                sdone()
                assert k[0] == BSTEPS
                steps = None if ahead is None else counted(ahead, b, 0)
                for q in range(TT + 1):
                    if q < TT:
                        for br in range(4):
                            c = S[b][:, where[br, q]:where[br, q] + width(br, q)]
                            vector.tensor_scalar(c, c, st[:, 2, br * TT + q:br * TT + q + 1], None, ALU.mult)\
                                .then_inc(weighed[b].sem, 1)
                    if steps is not None and q > 0:
                        front_tile(ahead, b, q - 1, steps, True)
                if steps is not None:
                    front_end(ahead, b, steps)

            front(0, 0)
            front(0, 1)
            with vector.Fori(0, TURNS - 1) as t:
                for b in range(2):
                    rear(t, b, t + 1)
            rear(TURNS - 1, 0)
            rear(TURNS - 1, 1)

        @block.scalar
        def _(scalar):
            def exponentials(t, b, q):
                st = stat2[:, b]
                if q == 0:
                    scalar.wait_ge(max_done[b].sem, t + (m0[b] + 1))
                for br in range(4):
                    i = br * TT + q
                    c = S[b][:, where[br, q]:where[br, q] + width(br, q)]
                    scalar.activation(c, c, ACT.Exp, bias=st[:, 1, i:i + 1], accum_out=st[:, 2, i:i + 1])\
                        .then_inc(exp_part.sem, 1)
                if q == TT - 1:
                    scalar.activation(st[:, 3, 0:4], st[:, 1, 12:16], ACT.Exp, bias=sinks[:, ds(t + 4 * b, 1)])\
                        .then_inc(exp_part.sem, 1)
                    scalar.wait_ge(exp_part.sem, t * 34 + (x0 + 17 * (b + 1)))
                    scalar.sem_inc(exp_done[b].sem, 1)

            def rear(t, b, after):
                for q in range(TT):
                    scalar.wait_ge(turn_done[b].sem, t * TT + (u0[b] + q + 1))
                    if q >= 2:
                        scalar.wait_ge(pv_done[b].sem, t * TT + (p0[b] + q - 1))
                    elif b == 1:
                        scalar.wait_ge(pv_done[0].sem, t * TT + (p0[0] + TT - 1 + q))
                    else:
                        scalar.wait_ge(pv_done[1].sem, t * TT + p0[1])
                    for n, (bank, a) in enumerate(((3, 0), (4, 512), (5, 896))):
                        wide = width(n + 1, q)
                        scalar.activation(PT[q % 2][:, a:a + wide], ps[:, bank, 0:wide], ACT.Copy)\
                            .then_inc(ev_part.sem, 1)
                    scalar.activation(PT[q % 2][0:CMP_BLOCKS, turned[0]:turned[0] + P],
                                      ps[0:CMP_BLOCKS, 5, 256:256 + P], ACT.Copy).then_inc(ev_part.sem, 1)
                    scalar.wait_ge(ev_part.sem, t * (8 * TT) + (y0 + 4 * TT * b + 4 * (q + 1)))
                    scalar.sem_inc(turn_ev[b].sem, 1)
                    if after is not None:
                        exponentials(*after, q)
                half = slice(b * HD, (b + 1) * HD)
                scalar.wait_ge(pv_done[b].sem, t * TT + (p0[b] + TT))
                scalar.activation(Oa[half, ds(t, 1), :].rearrange("p a n -> p (a n)"), ps[half, 6, :], ACT.Copy)\
                    .then_inc(o_part.sem, 1)
                scalar.activation(Ob[half, ds(t, 1), :].rearrange("p a n -> p (a n)"), ps[half, 7, :], ACT.Copy)\
                    .then_inc(o_part.sem, 1)
                scalar.wait_ge(o_part.sem, t * 4 + (z0 + 2 * (b + 1)))
                scalar.sem_inc(o_done[b].sem, 1)

            for q in range(TT):
                exponentials(0, 0, q)
            with scalar.Fori(0, TURNS - 1) as t:
                rear(t, 0, (t, 1))
                rear(t, 1, (t + 1, 0))
            rear(TURNS - 1, 0, (TURNS - 1, 1))
            rear(TURNS - 1, 1, None)
        advance(staged, 2 * TURNS)
        for cs, n in zip(names[1:], (TT, TT, 1, 1, BSTEPS, TT, TT, TT, 1)):
            advance(cs, n * TURNS)
        advance(weighed, 4 * TT * TURNS)

    BSTEPS = 8 * 4 + 2 + 4
    weighed = [count(f"probabilities_weighed{b}") for b in range(2)]
    exp_part, ev_part, o_part = (count(n) for n in ("exp_part", "turned_part", "output_part"))
    x0 = y0 = z0 = 0

    def merge(block, Oab, G, U, nxt, ready):
        turns = 2
        w = io["w_ab"]
        n0 = list(ring.n)
        d0, r0 = ([c.at for c in cs] for cs in (down_done, added))
        k0 = dve_chain.at
        @block.sync
        def _(sync):
            with sync.Fori(0, turns - 1) as t:
                for s in range(2):
                    sync.wait_ge(ring.used[s], t + (n0[s] + 1))
                    sync.dma_start(ring.buf[:, s, 0:2 * KD * P], w[ds(t * 2 + (2 + s), 1)].rearrange("a p n -> (a p) n"))\
                        .then_inc(ring.landed[s], 16)
            prefetch(sync, nxt, [n + (turns if s < 2 else 0) for s, n in enumerate(n0)])

        @block.tensor
        def _(pe):
            for c in ready:
                pe.wait_ge(c.sem, c.at)
            with pe.Fori(0, turns) as t:
                for s in range(2):
                    wv = ring.view(s, 2, KD, P)
                    pe.wait_ge(ring.landed[s], t * 16 + 16 * (n0[s] + 1))
                    pe.wait_ge(added[s].sem, t * 2 + r0[s])
                    for j in range(2):
                        for k in range(KD):
                            mm = pe.matmul(ps[:, 4 * s + 2 * j + k // 4, :], wv[:, j, k, :], Oab[:, k, :],
                                           start=(k % 4 == 0), stop=(k % 4 == 3))
                    mm.then_inc(down_done[s].sem, 1)
                    pe.wait_ge(down_done[s].sem, t + (d0[s] + 1))
                    pe.sem_inc(ring.used[s], 1)

        @block.vector
        def _(vector):
            with vector.Fori(0, turns) as t:
                for s in range(2):
                    vector.wait_ge(down_done[s].sem, t + (d0[s] + 1))
                    for j in range(2):
                        m = t * 4 + (2 * s + j)

                        def at(buf, i):
                            return buf[:, ds(i, 1), :].rearrange("p a n -> p (a n)")
                        k = 4 * s + 2 * j
                        vector.tensor_tensor(at(U, m), ps[:, k, :], at(G, m), ALU.mult).then_inc(dve_chain.sem, 1)
                        vector.tensor_tensor(tmp[:, 0, 0:NX], ps[:, k + 1, :], at(G, m + 8), ALU.mult)\
                            .then_inc(dve_chain.sem, 1)
                        vector.wait_ge(dve_chain.sem, t * 12 + (k0 + 6 * s + 3 * j + 2))
                        vector.tensor_tensor(at(U, m), at(U, m), tmp[:, 0, 0:NX], ALU.add).then_inc(dve_chain.sem, 1)
                        vector.wait_ge(dve_chain.sem, t * 12 + (k0 + 6 * s + 3 * j + 3))
                        vector.sem_inc(added[s].sem, 1)
        for s in range(2):
            ring.n[s] += turns
        dve_chain.at += 12 * turns
        advance(down_done, turns)
        advance(added, 2 * turns)

    def router_tables():
        o, tabs = 0, []
        for name in ("w_route", "b_route", "rev", "expert_base", "block_numbers", "before"):
            n = int(np.prod(io[name].shape[1:]))
            dst = work[:, o:o + n]
            tabs.append((dst.rearrange("p (k n) -> p k n", k=KD) if name == "w_route" else dst, io[name], tables))
            o += n
        return tabs

    def route():
        TT = NX // P
        NE, NG, PER = EXPERTS, GROUPS, EXPERTS // GROUPS

        def part(n):
            o[0] += n
            return work[:, o[0] - n:o[0]]

        wr, rb, rev, base, slot_no, before = (dst for dst, _, _ in router_tables())
        o = [sum(int(np.prod(dst.shape[1:])) for dst, _, _ in router_tables())]
        hot = part(TT * NE).rearrange("p (t n) -> p t n", t=TT)
        row = part(TT * NE).rearrange("p (t n) -> p t n", t=TT)
        shift = part(NE)
        extra = part(P)
        past = part(8)
        expert = part(MOE_BLOCKS + 1)
        rowf = part(2 * TT).rearrange("p (r t) -> p r t", r=2)
        hT = big[:, 0:TT * D].rearrange("p (t d) -> p t d", t=TT)
        nearer = ps[:, 1, 0:TT * NE].rearrange("p (t n) -> p t n", t=TT)
        L = part(TT * (NG + NE)).rearrange("p (t n) -> p t n", t=TT)
        eq = part(TT * NE).rearrange("p (t n) -> p t n", t=TT)
        em = part(TT * NE).rearrange("p (t n) -> p t n", t=TT)
        oh1 = part(TT * NE).rearrange("p (t n) -> p t n", t=TT)
        oh2 = part(TT * NE).rearrange("p (t n) -> p t n", t=TT)
        gs = part(TT * 16).rearrange("p (t n) -> p t n", t=TT)
        v = part(TT * 16).rearrange("p (t n) -> p t n", t=TT)
        t0, p0, e0, u0, v0 = (c.at for c in (tables, proj_done[0], exp_done[0], turn_done[0], turn_ev[0]))
        c0 = counted.at
        mark = []

        def turned(i):
            return ps[:, 2 + 2 * (i % 3):4 + 2 * (i % 3), :].rearrange("p b n -> p (b n)")

        with nc.Block() as block:
            @block.sync
            def _(sync):
                sync.dma_start(wset(1), io["w_exp"][1].rearrange("p (a n) -> p a n", a=3)).then_inc(set_landed[1].sem, 16)
                sync.wait_ge(scattered.sem, 32 * TT)
                for s in range(3):
                    sync.dma_start(xin(s), io["slots"][s * P:(s + 1) * P, :]).then_inc(x_landed[s].sem, 16)

            @block.vector
            def _(vector):
                vector.wait_ge(tables.sem, t0 + 96)
                tiles = range(TT)

                def each(f):
                    for i in tiles:
                        step(f(i))
                    steps_done(vector)

                def first_of_max(dst, src, m, n, t2):
                    each(lambda i: vector.scalar_tensor_tensor(eq[:, i, 0:n], src(i), m(i), rev[:, NE - n:NE],
                                                               ALU.is_ge, ALU.mult))
                    each(lambda i: vector.reduce_max(t2(i), eq[:, i, 0:n], AX_X))
                    each(lambda i: vector.tensor_scalar(dst(i), eq[:, i, 0:n], t2(i), None, ALU.is_ge))

                vector.wait_ge(proj_done[0].sem, p0 + TT)
                for i in tiles:
                    step(vector.tensor_tensor(L[:, i, :], ps[:, 0, i * (NG + NE):(i + 1) * (NG + NE)], rb, ALU.add))
                steps_done(vector)
                each(lambda i: vector.reduce_max(v[:, i, 0:1], L[:, i, 0:NG], AX_X))
                each(lambda i: vector.tensor_scalar(v[:, i, 1:2], v[:, i, 0:1], -1.0, None, ALU.mult))
                mark.append(dve_chain.at)
                first_of_max(lambda i: gs[:, i, 0:NG], lambda i: L[:, i, 0:NG], lambda i: v[:, i, 0:1], NG,
                             lambda i: v[:, i, 2:3])
                each(lambda i: vector.tensor_scalar(gs[:, i, NG:2 * NG], gs[:, i, 0:NG], -1.0, 1e30, ALU.add, ALU.mult))
                for g in range(NG):
                    a = slice(g * PER, (g + 1) * PER)
                    each(lambda i: vector.tensor_scalar(em[:, i, a], L[:, i, NG + g * PER:NG + (g + 1) * PER],
                                                        gs[:, i, NG + g:NG + g + 1], None, ALU.add))
                each(lambda i: vector.reduce_max(v[:, i, 3:4], em[:, i, :], AX_X))
                first_of_max(lambda i: oh1[:, i, :], lambda i: em[:, i, :], lambda i: v[:, i, 3:4], NE,
                             lambda i: v[:, i, 4:5])
                each(lambda i: vector.scalar_tensor_tensor(em[:, i, :], oh1[:, i, :], -1e30, em[:, i, :],
                                                           ALU.mult, ALU.add))
                each(lambda i: vector.reduce_max(v[:, i, 5:6], em[:, i, :], AX_X))
                first_of_max(lambda i: oh2[:, i, :], lambda i: em[:, i, :], lambda i: v[:, i, 5:6], NE,
                             lambda i: v[:, i, 6:7])
                step(vector.tensor_tensor(hot, oh1, oh2, ALU.add))
                mark.append(dve_chain.at)
                each(lambda i: vector.tensor_tensor(v[:, i, 7:8], v[:, i, 5:6], v[:, i, 3:4], ALU.subtract))
                mark.append(dve_chain.at)
                vector.wait_ge(counted.sem, c0 + 1)
                step(vector.tensor_scalar(extra[0:NE], ps[0:NE, 1, P:2 * P], P + 0.5, None, ALU.is_ge))
                steps_done(vector)
                for j in range(2, TT):
                    step(vector.scalar_tensor_tensor(extra[0:NE], ps[0:NE, 1, P:2 * P], j * P + 0.5, extra[0:NE],
                                                     ALU.is_ge, ALU.add))
                    steps_done(vector)
                mark.append(dve_chain.at)
                vector.wait_ge(counted.sem, c0 + 2)
                step(vector.tensor_tensor(past[0:NE], slot_no[0:NE, 0:8], ps[0:NE, 1, 2 * P:2 * P + 8], ALU.is_ge))
                mark.append(dve_chain.at)
                step(vector.tensor_scalar(shift, ps[:, 1, 3 * P:3 * P + NE], float(P), float((NE - 1) * P),
                                          ALU.mult, ALU.add))
                steps_done(vector)
                step(vector.tensor_tensor(shift, shift, base, ALU.subtract))
                steps_done(vector)
                each(lambda i: vector.scalar_tensor_tensor(row[:, i, :], nearer[:, i, :], P - 0.5, shift,
                                                           ALU.is_ge, ALU.mult))
                each(lambda i: vector.tensor_tensor(row[:, i, :], row[:, i, :], nearer[:, i, :], ALU.add))
                each(lambda i: vector.tensor_tensor(row[:, i, :], row[:, i, :], base, ALU.add))
                for r, oh in enumerate((oh1, oh2)):
                    step(vector.tensor_tensor(eq, oh, row, ALU.mult))
                    steps_done(vector)
                    step(vector.reduce_sum(rowf[:, r, :], eq, AX_X))
                    steps_done(vector)
                step(vector.tensor_copy(dest[:], rowf.rearrange("p r t -> p (r t)")))
                mark.append(dve_chain.at)
                vector.wait_ge(counted.sem, c0 + 3)
                step(vector.tensor_scalar(expert[0:1, 0:NE], slot_no[0:1, 0:NE], 0.0, None, ALU.add))
                step(vector.tensor_scalar(expert[0:1, NE:NE + 8], ps[0:1, 0, 0:8], float(NE - 1),
                                          None, ALU.min))
                steps_done(vector)
                step(vector.tensor_copy(block_expert[:], expert[0:1, :]))
                vector.wait_ge(exp_done[0].sem, e0 + 2 * TT)
                each(lambda i: vector.tensor_scalar(v[:, i, 10:11], v[:, i, 8:9], 1.0, v[:, i, 9:10], ALU.add, ALU.mult))
                each(lambda i: vector.reciprocal(share[:, 0, i:i + 1], v[:, i, 10:11]))
                each(lambda i: vector.tensor_tensor(share[:, 1, i:i + 1], share[:, 0, i:i + 1], v[:, i, 8:9], ALU.mult))

            @block.scalar
            def _(scalar):
                for i in range(TT):
                    scalar.wait_ge(turn_done[0].sem, u0 + i + 1)
                    scalar.activation(hT[:, i, :], turned(i), ACT.Copy).then_inc(turn_ev[0].sem, 1)
                scalar.wait_ge(dve_chain.sem, mark[0])
                for i in range(TT):
                    scalar.activation(gs[:, i, 8:8 + NG], L[:, i, 0:NG], ACT.Exp, bias=v[:, i, 1:2],
                                      accum_out=v[:, i, 9:10]).then_inc(exp_done[0].sem, 1)
                scalar.wait_ge(dve_chain.sem, mark[2])
                for i in range(TT):
                    scalar.activation(v[:, i, 8:9], v[:, i, 7:8], ACT.Exp).then_inc(exp_done[0].sem, 1)
            @block.tensor
            def _(pe):
                pe.wait_ge(tables.sem, t0 + 96)
                for i in range(TT):
                    for k in range(KD):
                        mm = pe.matmul(ps[:, 0, i * (NG + NE):(i + 1) * (NG + NE)], h[:, k, i * P:(i + 1) * P], wr[:, k, :],
                                       start=(k == 0), stop=(k == KD - 1))
                    mm.then_inc(proj_done[0].sem, 1)
                for i in range(TT):
                    if i == 3:
                        pe.wait_ge(turn_ev[0].sem, v0 + 1)
                    for k in range(KD):
                        mm = pe.transpose(turned(i)[:, k * P:(k + 1) * P], h[:, k, i * P:(i + 1) * P], ident[:])
                    mm.then_inc(turn_done[0].sem, 1)
                pe.wait_ge(dve_chain.sem, mark[1])
                for i in range(TT):
                    for j in range(i + 1):
                        pe.matmul(nearer[:, i, :], before if j == i else ones[:], hot[:, j, :],
                                  start=(j == 0), stop=(j == i))
                for i in range(TT):
                    mm = pe.matmul(ps[0:NE, 1, P:2 * P], hot[:, i, :], ones[:], start=(i == 0), stop=(i == TT - 1))
                mm.then_inc(counted.sem, 1)
                pe.wait_ge(dve_chain.sem, mark[3])
                pe.matmul(ps[0:NE, 1, 2 * P:3 * P], before[0:NE, 0:NE], extra[0:NE], start=True, stop=False)
                pe.matmul(ps[0:NE, 1, 2 * P:3 * P], ident[0:NE, 0:NE], extra[0:NE], start=False, stop=True)
                pe.matmul(ps[:, 1, 3 * P:3 * P + NE], extra[0:NE], before[0:NE, 0:NE], start=True, stop=True)\
                    .then_inc(counted.sem, 1)
                pe.wait_ge(dve_chain.sem, mark[4])
                pe.matmul(ps[:, 0, 0:8], ones[0:NE, :], past[0:NE], start=True, stop=True)\
                    .then_inc(counted.sem, 1)

            @block.gpsimd
            def _(gpsimd):
                gpsimd.wait_ge(turn_ev[0].sem, v0 + TT)
                gpsimd.wait_ge(dve_chain.sem, mark[5])
                for r in range(2):
                    for i in range(TT):
                        c = r * TT + i
                        gpsimd.indirect_dma_start(io["slots"], bass.IndirectOffsetOnAxis(dest[:, c:c + 1], 0),
                                                  hT[:, i, :], None).then_inc(scattered.sem, 16)
        tables.at += 96
        proj_done[0].at += TT
        exp_done[0].at += 2 * TT
        turn_done[0].at += TT
        turn_ev[0].at += TT
        counted.at += 3

    def experts():
        LAST = MOE_BLOCKS // 3 - 1
        gT = work[:, 0:D].rearrange("p (k n) -> p k n", k=KD)
        gate = [work[:, D + s * 2 * P:D + (s + 1) * 2 * P] for s in range(3)]
        act = [work[:, D + (3 + s) * 2 * P:D + (4 + s) * 2 * P].rearrange("p (f n) -> p f n", f=2) for s in range(3)]
        y = [work[:, 3 * D + s * D:4 * D + s * D] for s in range(3)]
        rows_ps = ps[:, 0:2, :].rearrange("p b n -> p (b n)")
        y_ps = ps[:, 5:7, :].rearrange("p b n -> p (b n)")
        HF = D // 2

        def in_order(eng, turn, gate_up, down):
            turn(0, 0)
            gate_up(0, 0)
            turn(0, 1)
            with eng.Fori(0, LAST) as t:
                for s in range(3):
                    gate_up(t + (s + 1) // 3, (s + 1) % 3)
                    turn(t + (s + 2) // 3, (s + 2) % 3)
                    down(t, s)
            gate_up(LAST, 1)
            turn(LAST, 2)
            down(LAST, 0)
            gate_up(LAST, 2)
            down(LAST, 1)
            down(LAST, 2)

        with nc.Block() as block:
            @block.sync
            def _(sync):
                def store(t, s):
                    for c in (y_by_act, y_by_vec):
                        sync.wait_ge(c.sem, t * 3 + (s + 2))
                    sync.dma_start(io["slots_out"][ds(t * (3 * P) + s * P, P), :], y[s]).then_inc(y_stored[s].sem, 16)

                with sync.Fori(0, LAST) as t:
                    for s in range(3):
                        sync.wait_ge(rows_turned.sem, t * 3 + (s + 1))
                        sync.dma_start(xin(s), io["slots"][ds(t * (3 * P) + (3 + s) * P, P), :]).then_inc(x_landed[s].sem, 16)
                        store(t, s)
                        e = sync.value_load(block_expert[0:1, ds(t * 3 + (3 + s), 1)], min_val=0, max_val=EXPERTS - 1)
                        sync.dma_start(wset(s), io["w_exp"][ds(e, 1)].rearrange("a p (c n) -> (a p) c n", c=3))\
                            .then_inc(set_landed[s].sem, 16)
                for s in range(3):
                    store(LAST, s)
                for s in range(3):
                    sync.wait_ge(y_stored[s].sem, 16 * (LAST + 1) + 1)

            @block.tensor
            def _(pe):
                def turn(t, s):
                    pe.wait_ge(x_landed[s].sem, t * 16 + 16)
                    for c in (rows_by_act, rows_by_vec):
                        pe.wait_ge(c.sem, t * 3 + (s + 1))
                    for k in range(KD):
                        mm = pe.transpose(rows_ps[:, k * P:(k + 1) * P], xin(s)[:, k * P:(k + 1) * P], ident[:])
                    mm.then_inc(rows_turned.sem, 1)

                def gate_up(t, s):
                    w = wset(s)[:, 0:2].rearrange("p f (j k n) -> p f j k n", j=2, k=KD)
                    pe.wait_ge(set_landed[s].sem, t * 16 + 16)
                    for c in (rows_by_act, rows_by_vec):
                        pe.wait_ge(c.sem, t * 3 + (s + 2))
                    for j in range(2):
                        for f in range(2):
                            for k in range(KD):
                                mm = pe.matmul(ps[:, 2 + s, (2 * j + f) * P:(2 * j + f + 1) * P], w[:, f, j, k, :],
                                               gT[:, k, :], start=(k == 0), stop=(k == KD - 1))
                    mm.then_inc(hidden_mm.sem, 1)

                def down(t, s):
                    w = wset(s)[:, 2].rearrange("p (f n) -> p f n", f=2)
                    pe.wait_ge(hidden_done.sem, t * 3 + (s + 1))
                    for c in (y_by_act, y_by_vec):
                        pe.wait_ge(c.sem, t * 3 + (s + 1))
                    for a in range(2):
                        for f in range(2):
                            mm = pe.matmul(y_ps[:, a * HF:(a + 1) * HF], act[s][:, f, :], w[:, f, a * HF:(a + 1) * HF],
                                           start=(f == 0), stop=(f == 1))
                        mm.then_inc(y_mm.sem, 1)

                in_order(pe, turn, gate_up, down)

            @block.scalar
            def _(scalar):
                def turn(t, s):
                    scalar.wait_ge(rows_turned.sem, t * 3 + (s + 1))
                    scalar.activation(gT[:, 0:KD // 2, :].rearrange("p k n -> p (k n)"), rows_ps[:, 0:HF], ACT.Copy)\
                        .then_inc(rows_by_act.sem, 1)

                def gate_up(t, s):
                    scalar.wait_ge(hidden_mm.sem, t * 3 + (s + 1))
                    scalar.activation(gate[s], ps[:, 2 + s, 0:2 * P], ACT.Silu).then_inc(gate_done.sem, 1)

                def down(t, s):
                    scalar.wait_ge(y_mm.sem, t * 6 + (2 * s + 1))
                    scalar.wait_ge(y_stored[s].sem, t * 16 + 1)
                    scalar.activation(y[s][:, 0:HF], y_ps[:, 0:HF], ACT.Copy).then_inc(y_by_act.sem, 1)

                in_order(scalar, turn, gate_up, down)

            @block.vector
            def _(vector):
                def turn(t, s):
                    vector.wait_ge(rows_turned.sem, t * 3 + (s + 1))
                    vector.tensor_copy(gT[:, KD // 2:KD, :].rearrange("p k n -> p (k n)"), rows_ps[:, HF:D])\
                        .then_inc(rows_by_vec.sem, 1)

                def gate_up(t, s):
                    vector.wait_ge(gate_done.sem, t * 3 + (s + 1))
                    vector.tensor_tensor(act[s].rearrange("p f n -> p (f n)"), gate[s], ps[:, 2 + s, 2 * P:4 * P],
                                         ALU.mult).then_inc(hidden_done.sem, 1)

                def down(t, s):
                    vector.wait_ge(y_mm.sem, t * 6 + (2 * s + 2))
                    vector.wait_ge(y_stored[s].sem, t * 16 + 1)
                    vector.tensor_copy(y[s][:, HF:D], y_ps[:, HF:D]).then_inc(y_by_vec.sem, 1)

                in_order(vector, turn, gate_up, down)

    def combine():
        TT = NX // P
        Y = big[:, 0:2 * TT * D].rearrange("p (r t d) -> p r t d", r=2, t=TT)
        m0, u0, a0 = dve_chain.at, turn_done[0].at, added[0].at

        def turned(i):
            return ps[:, 2 * (i % 2):2 + 2 * (i % 2), :].rearrange("p b n -> p (b n)")

        with nc.Block() as block:
            @block.gpsimd
            def _(gpsimd):
                for i in range(TT):
                    for r in range(2):
                        c = r * TT + i
                        gpsimd.indirect_dma_start(Y[:, r, i, :], None, io["slots_out"],
                                                  bass.IndirectOffsetOnAxis(dest[:, c:c + 1], 0)).then_inc(gathered[i].sem, 16)

            @block.tensor
            def _(pe):
                for i in range(TT):
                    pe.wait_ge(dve_chain.sem, m0 + 2 * i + 2)
                    if i >= 2:
                        pe.wait_ge(added[0].sem, a0 + i - 1)
                    for k in range(KD):
                        mm = pe.transpose(turned(i)[:, k * P:(k + 1) * P], Y[:, 0, i, k * P:(k + 1) * P], ident[:])
                    mm.then_inc(turn_done[0].sem, 1)

            @block.vector
            def _(vector):
                def weigh(i):
                    vector.wait_ge(gathered[i].sem, 32)
                    step(vector.tensor_scalar(Y[:, 0, i, :], Y[:, 0, i, :], share[:, 0, i:i + 1], None, ALU.mult))
                    steps_done(vector)
                    step(vector.scalar_tensor_tensor(Y[:, 0, i, :], Y[:, 1, i, :], share[:, 1, i:i + 1], Y[:, 0, i, :],
                                                     ALU.mult, ALU.add))

                def add(i):
                    vector.wait_ge(turn_done[0].sem, u0 + i + 1)
                    cols = xy[:, :, i * P:(i + 1) * P]
                    vector.tensor_tensor(cols, turned(i).rearrange("p (k n) -> p k n", k=KD), cols, ALU.add)\
                        .then_inc(added[0].sem, 1)

                for i in range(TT):
                    weigh(i)
                    if i > 0:
                        add(i - 1)
                add(TT - 1)
        turn_done[0].at += TT
        added[0].at += TT

    def two(w, a=0):
        return [(s, w[a + s]) for s in range(2)]

    def chunk(i, j):
        return mods[i][:, j * KD:(j + 1) * KD, :]

    own = stage_buffers("")
    start(first_gu("ffn1", 0))
    own.close()
    feed_forward("ffn1", 0, NT, mod_gain[0][:, 0], chunk(0, 0), chunk(0, 2), two(io["w_qk"]), mod=0)
    own = stage_buffers("_0")
    with nc.Block() as block:
        norm(block, NT, mod_gain[0][:, 1], chunk(0, 3))
        attention_tables(block)
    Qh = big[:, 0:HEADS * NX].rearrange("p (a n) -> p a n", a=HEADS)
    Kh = big[:, HEADS * NX:HEADS * (NX + NT)].rearrange("p (a n) -> p a n", a=HEADS)
    Vh = big[:, HEADS * (NX + NT):HEADS * (NX + NT) + KT * D].rearrange("p (m n) -> p m n", m=KT)
    Oh = hbuf[:, 0:HEADS * NX].rearrange("p (a n) -> p a n", a=HEADS)
    with nc.Block() as block:
        head_inputs(block, 0, Qh, two(io["w_qk"], 4))
        head_inputs(block, 1, Kh, two(io["w_v"]))
        values(block, Vh, two(io["w_o"]))
    attention(Qh, Kh, Vh, Oh)
    with nc.Block() as block:
        output_norm(block, Oh, subg[:, 1:2])
        project_residual(block, io["w_o"], Oh, chunk(0, 5), first_gu("ffn2", 0), [scaled])
    own.close()
    feed_forward("ffn2", 0, NX, mod_gain[0][:, 2], chunk(0, 6), chunk(0, 8), first_gu("ffn1", 1), mod=1)
    feed_forward("ffn1", 1, NX, mod_gain[1][:, 0], chunk(1, 0), chunk(1, 2), two(io["w_f"]), zero_slots=True)
    own = stage_buffers("_1")
    with nc.Block() as block:
        norm(block, NX, mod_gain[1][:, 1], chunk(1, 3),
             [(dst, io[name], tables) for dst, name in zip(dft_tables(), ("dft_feature", "dft_token"))])
    F = work[:, 0:KD * NX].rearrange("p (k n) -> p k n", k=KD)
    with nc.Block() as block:
        fourier(block, F)
        project_residual(block, io["w_f"], F, chunk(1, 5), first_gu("ffn2", 1), raw_done)
    own.close()
    feed_forward("ffn2", 1, NX, mod_gain[1][:, 2], chunk(1, 6), chunk(1, 8), two(io["w_in"]))
    own = stage_buffers("_2", ("big",))
    second_gains()
    F = big[:, 0:16 * NX].rearrange("p (k n) -> p k n", k=16)
    G = big[:, 16 * NX:32 * NX].rearrange("p (k n) -> p k n", k=16)
    V2 = rope[:].rearrange("p a n -> p (a n)")[:, 0:12 * P].rearrange("p (t n) -> p t n", t=4)
    split = ExitStack()
    split_h = [sb(f"mixer_h_{p}", [P, KD, NX], split, F32R)[:] for p in ("high", "low")]
    split_w = [sb(f"mixer_w_{p}", [P, 2, SLOT], split, F32R)[:] for p in ("high", "low")]
    mixer_inputs(gains2[:, 0], F, G, G[:, 0:KD], split_h, split_w)
    values_and_gates(F, V2, split_h, split_w, two(io["w_ab"]))
    split.close()
    stage_buffers("_2", ("work",), own)
    compress(F, kc_sb[:], vc_sb[:])
    Oab = hbuf[:, 0:KD * NX].rearrange("p (k n) -> p k n", k=KD)
    U = big[:, 0:KD * NX].rearrange("p (k n) -> p k n", k=KD)
    with nc.Block() as block:
        branches(block, F, V2, kc_sb[:], vc_sb[:], Oab[:, 0:4], Oab[:, 4:8])
        merge(block, Oab, G, U, two(io["w_o2"]), o_done + turn_ev)
        project_residual(block, io["w_o2"], U, None, [], added)
    with nc.Block() as block:
        norm(block, NX, gains2[:, 1], None, router_tables() + [
            (wset(s), io["w_exp"][s].rearrange("p (a n) -> p a n", a=3), set_landed[s]) for s in (0, 2)])
    route()
    experts()
    combine()
    first = scaled.at
    with nc.Block() as block:
        norm(block, NX, gains2[:, 2], None)
        store_output(block, io["out"], first)
    own.close()


def slabs(w, per):
    k, m = w.shape
    w = w.reshape(k // P, P, m // P // per, per, P)
    return np.ascontiguousarray(w.transpose(2, 1, 3, 0, 4)).reshape(m // P // per, P, per * k)


def columns(v):
    v = v.reshape(v.shape[:-1] + (-1, P))
    return np.ascontiguousarray(np.moveaxis(v, -1, 0))


def layouts(a):
    L = {}
    n = np.arange(P)
    L["bones"] = (n[:, None] // HD == n[None, :] // HD).astype(np.float32)
    L["ident"] = np.eye(P, dtype=np.float32)
    L["lam"] = np.broadcast_to(np.stack([a["attn_lam_" + i][0] for i in ("q1", "k1", "q2", "k2")]), (P, 4, HD))
    L["qk_gain"] = np.stack([np.tile(a["attn_" + i + "_g"][0], 2) for i in "qk"], axis=1)
    L["sub_gain"] = a["attn_sub_g"][0][:, None]
    pairs = HD // 4
    inv_freq = np.float32(10000.0) ** (-(np.arange(pairs, dtype=np.float32) / pairs))
    tok = np.arange(NX)
    place = np.stack([tok // 64, tok % 64]).astype(np.float32)
    angle = (place[(n % HD) // 32] * inv_freq[n % pairs][:, None]).astype(np.float32)
    L["rope"] = np.stack([np.cos(angle), np.sin(angle)], axis=1).astype(np.float32)
    r = np.zeros((P, P), np.float32)
    for p in range(P):
        if (p // pairs) % 2:
            r[p, p - pairs] = -1.0
        else:
            r[p, p + pairs] = 1.0
    L["rot"] = r
    qkv = a["attn_w_qkv"][0]
    L["w_qk"] = slabs(qkv[:, 0:2 * D], 2)
    L["w_v"] = np.ascontiguousarray(qkv[:, 2 * D:].reshape(KD, P, 4, 2 * P).transpose(2, 1, 0, 3)).reshape(4, P, -1)
    L["w_o"] = slabs(a["attn_w_o"][0], 2)
    L["w_f"] = slabs(a["fourier_w"][0], 2)
    W = D // 4
    f, t = np.arange(W), np.arange(NX)
    af, at = 2 * np.pi * (np.outer(f, f) % W) / W, 2 * np.pi * (np.outer(t, t) % NX) / NX
    L["dft_feature"] = (np.concatenate([np.cos(af), np.sin(af)], 1) / np.sqrt(W)).astype(np.float32)\
        .reshape(2, P, 2 * W).transpose(1, 0, 2)
    L["dft_token"] = (np.stack([np.cos(at), -np.sin(at)]) / np.sqrt(NX)).astype(np.float32)\
        .reshape(2, NX // P, P, NX).transpose(2, 0, 1, 3)
    L["gains2"] = np.stack([columns(a[k].reshape(D)) for k in ("norm_mix_g_2", "norm_ffn_g_2", "norm_final_g_2")],
                           axis=1)[..., None]
    w = a["w_in_2"][0]
    edges = np.cumsum([0, 512, 128, 128, 128, 128, 128, 128, 24, 512, 128, 128, 2048])
    qa, kcmp, vcmp, kslc, vslc, kwin, vwin, gn, qb, kb, vb, gm = (w[:, x:y] for x, y in zip(edges[:-1], edges[1:]))

    def paired(m):
        return m.reshape(-1, 2, 4, HD).transpose(0, 2, 1, 3).reshape(-1, 8 * HD)

    def doubled(m):
        return np.repeat(m.reshape(-1, 2, 1, HD), 2, axis=2).reshape(-1, 4 * HD)

    pad = np.zeros((D, P - gn.shape[1]), np.float32)
    L["w_in"] = slabs(np.concatenate([paired(qa), paired(qb), kslc, kwin, kb, doubled(kcmp), doubled(vcmp), gn, pad, gm],
                                     axis=1), 2)
    L["w_v2"] = np.concatenate([vslc, vwin, vb], axis=1).reshape(KD, P, 3 * P).transpose(1, 0, 2)
    L["w_ab"] = slabs(np.concatenate([paired(a[k][0].T).T for k in ("w_a_2", "w_b_2")], axis=0), 2)
    L["w_o2"] = slabs(a["w_o_2"][0], 2)
    LP = CMP_LEN // 2
    L["cmp_w1"] = np.stack([a[f"cmp_w1_{v}_2"][0].reshape(LP, P, CMP_HIDDEN).transpose(1, 0, 2) for v in "kv"], axis=1)
    L["cmp_w2"] = np.stack([a[f"cmp_w2_{v}_2"][0].reshape(2, P, HD).transpose(1, 0, 2) for v in "kv"], axis=1)
    pos = np.stack([a[f"cmp_pos_{v}_2"][0].reshape(LP, P).T for v in "kv"], axis=1)
    L["cmp_pos"] = np.repeat(pos[..., None], CMP_BLOCKS, axis=3)
    p = np.arange(P)[:, None]

    def distances(before, window):
        d = before + p - np.arange(before + P)[None, :]
        return np.where((d >= 0) & (d < window), d, 1e35)

    L["dist"] = np.concatenate([distances(NX - P, NX), distances(NSA_WINDOW, NSA_WINDOW),
                                distances(SWA_WINDOW, SWA_WINDOW)], axis=1).astype(np.float32)
    end = np.arange(CMP_BLOCKS) * CMP_STRIDE + CMP_LEN - 1
    dc = (np.arange(4)[None, :, None] * P + p[:, :, None]) - end
    L["dist_cmp"] = np.where(dc >= 0, dc, 1e35).astype(np.float32)
    slope = 2.0 ** (-8.0 * np.arange(1, 17) / 16)
    L["slopes"] = np.broadcast_to(-np.concatenate([slope[8:], slope[:8]]).astype(np.float32), (P, 16))
    L["sinks"] = np.broadcast_to(a["sinks_2"][0], (P, 8))
    L["w_route"] = np.concatenate([a["w_group_2"][0], a["w_expert_2"][0]], axis=1).reshape(KD, P, -1).transpose(1, 0, 2)
    L["b_route"] = np.broadcast_to(np.concatenate([a["b_group_2"][0], a["b_expert_2"][0]]), (P, GROUPS + EXPERTS))
    L["rev"] = np.broadcast_to(np.arange(EXPERTS, 0, -1, dtype=np.float32), (P, EXPERTS))
    FE = 2
    gu = np.stack([a["w_gate_e_2"][0], a["w_up_e_2"][0]], axis=1)
    gu = gu.reshape(EXPERTS, 2, KD, P, FE, P).transpose(0, 4, 3, 1, 2, 5).reshape(EXPERTS, FE, P, 2 * KD * P)
    dn = a["w_down_e_2"][0].reshape(EXPERTS, FE, P, D).transpose(0, 2, 1, 3).reshape(EXPERTS, 1, P, FE * D)
    L["w_exp"] = np.concatenate([gu, dn], axis=1).transpose(0, 2, 1, 3).reshape(EXPERTS, P, 3 * 2 * KD * P)
    L["expert_base"] = np.broadcast_to(P * np.arange(EXPERTS, dtype=np.float32), (P, EXPERTS))
    L["block_numbers"] = np.broadcast_to(np.arange(MOE_BLOCKS + 1, dtype=np.float32), (P, MOE_BLOCKS + 1))
    L["before"] = np.triu(np.ones((P, P), np.float32), 1)
    cols = np.concatenate([a["x"][0], a["ctx"][0]]).T
    L["xy"] = cols.reshape(KD, P, NT).transpose(1, 0, 2)
    L["cond"] = np.broadcast_to(np.stack([a["c"][0], a["c_ctx"]]), (P, 2, D))
    L["w_mod"] = a["w_mod"].transpose(0, 2, 1).reshape(2, NMOD * KD, P, D)
    b = a["b_mod"].reshape(2, NMOD * KD, P).transpose(0, 2, 1)
    L["b_mod"] = np.repeat(b[..., None], 2, axis=3)
    g = a["norm_g"].reshape(2, 3 * KD, P).transpose(0, 2, 1)
    L["norm_g"] = np.repeat(g[..., None], 2, axis=3)
    for n in ("ffn1", "ffn2"):
        gu = a[n + "_w_gu"].reshape(2, KD, P, 2, KF, P)
        L[n + "_gu"] = np.ascontiguousarray(gu.transpose(0, 4, 2, 3, 1, 5)).reshape(2, KF, P, 2 * KD * P)
        L[n + "_d"] = np.stack([slabs(w, 1) for w in a[n + "_w_d"]])
    return L


def kernel(**inputs):
    import concourse.bacc as bacc
    from concourse.bass_utils import run_bass_kernel_spmd

    nc = bacc.Bacc("TRN2", target_bir_lowering=False, num_devices=1)
    arrays, io = {}, {}
    for name, a in layouts({k: np.asarray(v) for k, v in inputs.items()}).items():
        arrays[f"in_{name}"] = np.ascontiguousarray(a)
        io[name] = nc.dram_tensor(f"in_{name}", a.shape, F32, kind="ExternalInput").ap()
    for name in ("slots", "slots_out"):
        io[name] = nc.dram_tensor(name, (MOE_BLOCKS * P, D), F32, kind="Internal").ap()
    io["out"] = nc.dram_tensor("out", (P, KD, NX), F32, kind="ExternalOutput").ap()
    program(nc, io)
    r = run_bass_kernel_spmd(nc, [arrays], core_ids=[0])
    return r.results[0]["out"].transpose(2, 1, 0).reshape(1, NX, D)
```
